# Optimizing a Trainium2 kernel written in Bass

```python
import math
import jax, jax.numpy as jnp
from jax import lax
import numpy as np
import jax
import jax.numpy as jnp

D_MODEL = 1024
BATCH = 1
SEQ = 512
DEPTH = 1

PLE_DIM = 256
RMS_EPS = 1e-6

RWKV_HEADS = 8
RWKV_HEAD_DIM = 64
RWKV_WIDTH = RWKV_HEADS * RWKV_HEAD_DIM
DECAY_LORA = 64
AAA_LORA = 64
GATE_LORA = 128
GN_EPS = 64e-5
RWKV_COLS = 3 * RWKV_WIDTH + DECAY_LORA + AAA_LORA + GATE_LORA

DIFF_HEADS = 4
DIFF_HEAD_DIM = 64
DIFF_QK_WIDTH = DIFF_HEADS * 2 * DIFF_HEAD_DIM
DIFF_V_DIM = 2 * DIFF_HEAD_DIM
DIFF_V_WIDTH = DIFF_HEADS * DIFF_V_DIM
DIFF_COLS = 2 * DIFF_QK_WIDTH + DIFF_V_WIDTH
ROPE_THETA = 10000.0
Q_BLOCK = 128

GATE_COLS = 2 * D_MODEL
IN_COLS = RWKV_COLS + DIFF_COLS + GATE_COLS

N_GROUPS = 4
EXPERTS_PER_GROUP = 8
N_EXPERTS = N_GROUPS * EXPERTS_PER_GROUP
TOP_K = 2
EXPERT_FF = 512
ROW_BLOCK = 128


def rms_norm(x, gain, eps=RMS_EPS):
    xf = x.astype(jnp.float32)
    y = xf * lax.rsqrt(jnp.mean(xf * xf, axis=-1, keepdims=True) + eps)
    return (y * gain.astype(jnp.float32)).astype(x.dtype)

def rope_tables(seq, dim):
    inv = ROPE_THETA ** (-jnp.arange(0, dim, 2, dtype=jnp.float32) / dim)
    ang = jnp.arange(seq, dtype=jnp.float32)[:, None] * inv[None, :]
    ang = jnp.concatenate([ang, ang], axis=-1)
    return jnp.cos(ang), jnp.sin(ang)

def apply_rope(x, cos, sin):
    c = cos[:, None, None, :]
    s = sin[:, None, None, :]
    x1, x2 = jnp.split(x, 2, axis=-1)
    rot = jnp.concatenate([-x2, x1], axis=-1)
    return (x.astype(jnp.float32) * c + rot.astype(jnp.float32) * s).astype(x.dtype)

def wkv7_scan(r, decay, k, kk, a, v):
    b, s, h, n = r.shape

    def step(state, inp):
        r_t, w_t, k_t, kk_t, a_t, v_t = inp
        sa = jnp.einsum('bhvk,bhk->bhv', state, -kk_t)
        state = (state * w_t[:, :, None, :]
                 + sa[..., None] * (kk_t * a_t)[:, :, None, :]
                 + v_t[..., None] * k_t[:, :, None, :])
        return state, jnp.einsum('bhvk,bhk->bhv', state, r_t)

    s0 = jnp.zeros((b, h, n, n), jnp.float32)
    xs = (jnp.swapaxes(r, 0, 1), jnp.swapaxes(decay, 0, 1), jnp.swapaxes(k, 0, 1),
          jnp.swapaxes(kk, 0, 1), jnp.swapaxes(a, 0, 1), jnp.swapaxes(v, 0, 1))
    _, y = lax.scan(step, s0, xs)
    return jnp.swapaxes(y, 0, 1)

def rwkv7_branch(pr, mu, w0, w2, a0, a2, g2, k_k, k_a, r_k, ln_w, ln_b):
    b, s, _ = pr.shape
    f32 = jnp.float32
    prev = jnp.pad(pr[:, :-1], ((0, 0), (1, 0), (0, 0)))
    xs = pr + (prev - pr) * mu
    c0 = RWKV_WIDTH
    r, k, v, xw, xa, xg = jnp.split(
        xs, [c0, 2 * c0, 3 * c0, 3 * c0 + DECAY_LORA, 3 * c0 + DECAY_LORA + AAA_LORA], axis=-1)
    w_log = -jax.nn.softplus(-(w0 + jnp.tanh(xw) @ w2).astype(f32)) - 0.5
    decay = jnp.exp(-jnp.exp(w_log))
    a = jax.nn.sigmoid((a0 + xa @ a2).astype(f32))
    g = jax.nn.sigmoid(xg) @ g2

    def heads(t):
        return t.reshape(b, s, RWKV_HEADS, RWKV_HEAD_DIM).astype(f32)

    kk = heads(k * k_k)
    kk = kk / jnp.maximum(jnp.sqrt(jnp.sum(kk * kk, axis=-1, keepdims=True)), 1e-12)
    k_mod = k.astype(f32) * (1.0 + (a - 1.0) * k_a.astype(f32))
    r_h, k_h, v_h = heads(r), heads(k_mod), heads(v)
    y = wkv7_scan(r_h, heads(decay), k_h, kk, heads(a), v_h)
    mean = jnp.mean(y, axis=-1, keepdims=True)
    var = jnp.mean(jnp.square(y - mean), axis=-1, keepdims=True)
    y = ((y - mean) * lax.rsqrt(var + GN_EPS)).reshape(b, s, RWKV_WIDTH)
    y = y * ln_w.astype(f32) + ln_b.astype(f32)
    bonus = jnp.sum(r_h * k_h * r_k.astype(f32), axis=-1, keepdims=True) * v_h
    out = (y + bonus.reshape(b, s, RWKV_WIDTH)) * g.astype(f32)
    return out.astype(pr.dtype)

def diff_attention_branch(pd, q_gain, k_gain, lq1, lk1, lq2, lk2, subln_w, lam_init, cos, sin):
    b, s, _ = pd.shape
    f32 = jnp.float32
    q, k, v = jnp.split(pd, [DIFF_QK_WIDTH, 2 * DIFF_QK_WIDTH], axis=-1)
    q = apply_rope(rms_norm(q.reshape(b, s, DIFF_HEADS, 2, DIFF_HEAD_DIM), q_gain), cos, sin)
    k = apply_rope(rms_norm(k.reshape(b, s, DIFF_HEADS, 2, DIFF_HEAD_DIM), k_gain), cos, sin)
    q = q.transpose(0, 2, 3, 1, 4)
    k = k.transpose(0, 2, 3, 1, 4)
    v = v.reshape(b, s, DIFF_HEADS, DIFF_V_DIM).transpose(0, 2, 1, 3)
    lam = (jnp.exp(jnp.sum(lq1.astype(f32) * lk1.astype(f32)))
           - jnp.exp(jnp.sum(lq2.astype(f32) * lk2.astype(f32))) + lam_init)
    scale = DIFF_HEAD_DIM ** -0.5
    neg = jnp.finfo(f32).min
    blocks = []
    for i in range(s // Q_BLOCK):
        q0 = i * Q_BLOCK
        end = q0 + Q_BLOCK
        sc = jnp.einsum('bhcqd,bhckd->bhcqk', q[:, :, :, q0:end], k[:, :, :, :end]).astype(f32) * scale
        causal = jnp.arange(end)[None, :] <= (q0 + jnp.arange(Q_BLOCK))[:, None]
        prob = jax.nn.softmax(jnp.where(causal, sc, neg), axis=-1)
        attn = prob[:, :, 0] - lam * prob[:, :, 1]
        blocks.append(jnp.einsum('bhqk,bhkv->bhqv', attn.astype(v.dtype), v[:, :, :end]))
    o = jnp.concatenate(blocks, axis=2)
    o = rms_norm(o, subln_w) * (1.0 - lam_init)
    return o.transpose(0, 2, 1, 3).reshape(b, s, DIFF_V_WIDTH)

def hierarchical_moe(h, w_group, b_group, w_er, b_er, w_gate, w_up, w_down):
    b, s, d = h.shape
    t = b * s
    f32 = jnp.float32
    hf = h.reshape(t, d)
    g_prob = jax.nn.softmax((hf @ w_group).astype(f32) + b_group.astype(f32), axis=-1)
    g_top, g_idx = lax.top_k(g_prob, 1)
    e_logits = ((hf @ w_er).astype(f32) + b_er.astype(f32)).reshape(t, N_GROUPS, EXPERTS_PER_GROUP)
    sel = jnp.broadcast_to(g_idx[:, :, None], (t, 1, EXPERTS_PER_GROUP))
    e_logits = jnp.take_along_axis(e_logits, sel, axis=1)[:, 0]
    e_top, e_idx = lax.top_k(e_logits, TOP_K)
    weights = g_top * jax.nn.softmax(e_top, axis=-1)
    expert_id = g_idx * EXPERTS_PER_GROUP + e_idx

    n_assign = t * TOP_K
    eid = expert_id.reshape(n_assign).astype(jnp.int32)
    tid = jnp.repeat(jnp.arange(t, dtype=jnp.int32), TOP_K)
    wt = weights.reshape(n_assign)
    order = jnp.argsort(eid)
    se = eid[order]
    counts = jnp.bincount(eid, length=N_EXPERTS).astype(jnp.int32)
    starts = jnp.cumsum(counts) - counts
    pcounts = ((counts + ROW_BLOCK - 1) // ROW_BLOCK) * ROW_BLOCK
    pends = jnp.cumsum(pcounts)
    pstarts = pends - pcounts
    dest = pstarts[se] + (jnp.arange(n_assign, dtype=jnp.int32) - starts[se])
    rows = n_assign + N_EXPERTS * ROW_BLOCK
    n_blocks = rows // ROW_BLOCK
    buf_tok = jnp.full((rows,), t, jnp.int32).at[dest].set(tid[order])
    buf_w = jnp.zeros((rows,), wt.dtype).at[dest].set(wt[order])
    blk_e = jnp.minimum(jnp.searchsorted(pends, jnp.arange(n_blocks, dtype=jnp.int32) * ROW_BLOCK,
                                         side='right'), N_EXPERTS - 1)
    hpad = jnp.concatenate([hf, jnp.zeros((1, d), hf.dtype)], axis=0)
    xs = hpad[buf_tok].reshape(n_blocks, ROW_BLOCK, d)

    def expert_block(args):
        xb, e = args
        return (jax.nn.silu(xb @ w_gate[e]) * (xb @ w_up[e])) @ w_down[e]

    yb = lax.map(expert_block, (xs, blk_e)).reshape(rows, d)
    yb = yb * buf_w[:, None].astype(yb.dtype)
    out = jax.ops.segment_sum(yb, buf_tok, num_segments=t + 1)[:t]
    return out.reshape(b, s, d)

def first_inputs(seed: int = 0) -> dict:
    key = jax.random.key(seed)
    ks = iter(jax.random.split(key, 40))
    L = DEPTH
    f32 = jnp.float32

    def nrm(shape, scale):
        return scale * jax.random.normal(next(ks), shape, f32)

    def gain(shape, base=1.0):
        return base + 0.1 * jax.random.normal(next(ks), shape, f32)

    return {
        'x': nrm((BATCH, SEQ, D_MODEL), 1.0),
        'p': nrm((L, BATCH, SEQ, PLE_DIM), 1.0),
        'norm_mix': gain((L, D_MODEL)),
        'w_in': nrm((L, D_MODEL, IN_COLS), D_MODEL ** -0.5),
        'rwkv_mu': jax.random.uniform(next(ks), (L, RWKV_COLS), f32),
        'rwkv_w0': jax.random.uniform(next(ks), (L, RWKV_WIDTH), f32, -6.0, 0.0),
        'rwkv_w2': nrm((L, DECAY_LORA, RWKV_WIDTH), DECAY_LORA ** -0.5),
        'rwkv_a0': nrm((L, RWKV_WIDTH), 0.5),
        'rwkv_a2': nrm((L, AAA_LORA, RWKV_WIDTH), AAA_LORA ** -0.5),
        'rwkv_g2': nrm((L, GATE_LORA, RWKV_WIDTH), GATE_LORA ** -0.5),
        'rwkv_k_k': gain((L, RWKV_WIDTH), 0.85),
        'rwkv_k_a': gain((L, RWKV_WIDTH)),
        'rwkv_r_k': gain((L, RWKV_HEADS, RWKV_HEAD_DIM), 0.5),
        'rwkv_ln_w': gain((L, RWKV_WIDTH)),
        'rwkv_ln_b': nrm((L, RWKV_WIDTH), 0.02),
        'q_norm': gain((L, DIFF_HEAD_DIM)),
        'k_norm': gain((L, DIFF_HEAD_DIM)),
        'lambda_q1': nrm((L, DIFF_HEAD_DIM), 0.1),
        'lambda_k1': nrm((L, DIFF_HEAD_DIM), 0.1),
        'lambda_q2': nrm((L, DIFF_HEAD_DIM), 0.1),
        'lambda_k2': nrm((L, DIFF_HEAD_DIM), 0.1),
        'subln_w': gain((L, DIFF_V_DIM)),
        'w_branch_rwkv': nrm((L, RWKV_WIDTH, D_MODEL), RWKV_WIDTH ** -0.5),
        'w_branch_diff': nrm((L, DIFF_V_WIDTH, D_MODEL), DIFF_V_WIDTH ** -0.5),
        'w_out': nrm((L, D_MODEL, D_MODEL), D_MODEL ** -0.5),
        'norm_ffn': gain((L, D_MODEL)),
        'w_group': nrm((L, D_MODEL, N_GROUPS), D_MODEL ** -0.5),
        'b_group': nrm((L, N_GROUPS), 0.01),
        'w_expert_router': nrm((L, D_MODEL, N_EXPERTS), D_MODEL ** -0.5),
        'b_expert_router': nrm((L, N_EXPERTS), 0.01),
        'w_gate': nrm((L, N_EXPERTS, D_MODEL, EXPERT_FF), D_MODEL ** -0.5),
        'w_up': nrm((L, N_EXPERTS, D_MODEL, EXPERT_FF), D_MODEL ** -0.5),
        'w_down': nrm((L, N_EXPERTS, EXPERT_FF, D_MODEL), EXPERT_FF ** -0.5),
        'norm_ple': gain((L, D_MODEL)),
        'w_ple_gate': nrm((L, D_MODEL, D_MODEL), D_MODEL ** -0.5),
        'w_ple_proj': nrm((L, PLE_DIM, D_MODEL), PLE_DIM ** -0.5),
    }

def first_block(x, p, norm_mix, w_in, rwkv_mu, rwkv_w0, rwkv_w2, rwkv_a0, rwkv_a2, rwkv_g2,
              rwkv_k_k, rwkv_k_a, rwkv_r_k, rwkv_ln_w, rwkv_ln_b, q_norm, k_norm,
              lambda_q1, lambda_k1, lambda_q2, lambda_k2, subln_w, w_branch_rwkv,
              w_branch_diff, w_out, norm_ffn, w_group, b_group, w_expert_router,
              b_expert_router, w_gate, w_up, w_down, norm_ple, w_ple_gate, w_ple_proj):
    seq = x.shape[1]
    cos, sin = rope_tables(seq, DIFF_HEAD_DIM)
    for l in range(DEPTH):
        lam_init = 0.8 - 0.6 * math.exp(-0.3 * l)
        h = rms_norm(x, norm_mix[l])
        proj = h @ w_in[l]
        p_rwkv = proj[..., :RWKV_COLS]
        p_diff = proj[..., RWKV_COLS:RWKV_COLS + DIFF_COLS]
        g_rwkv, g_diff = jnp.split(proj[..., RWKV_COLS + DIFF_COLS:], 2, axis=-1)
        o_rwkv = rwkv7_branch(p_rwkv, rwkv_mu[l], rwkv_w0[l], rwkv_w2[l], rwkv_a0[l], rwkv_a2[l],
                              rwkv_g2[l], rwkv_k_k[l], rwkv_k_a[l], rwkv_r_k[l], rwkv_ln_w[l],
                              rwkv_ln_b[l])
        o_diff = diff_attention_branch(p_diff, q_norm[l], k_norm[l], lambda_q1[l], lambda_k1[l],
                                       lambda_q2[l], lambda_k2[l], subln_w[l], lam_init, cos, sin)
        mixed = (jax.nn.sigmoid(g_rwkv) * (o_rwkv @ w_branch_rwkv[l])
                 + jax.nn.sigmoid(g_diff) * (o_diff @ w_branch_diff[l]))
        x = x + mixed @ w_out[l]
        x = x + hierarchical_moe(rms_norm(x, norm_ffn[l]), w_group[l], b_group[l],
                                 w_expert_router[l], b_expert_router[l], w_gate[l], w_up[l],
                                 w_down[l])
        ple_gate = jax.nn.sigmoid(rms_norm(x, norm_ple[l]) @ w_ple_gate[l])
        x = x + ple_gate * (p[l] @ w_ple_proj[l])
    return x


DEPTH_2 = 2

GRID_W = 64
CTX_LEN = 256
EPS = 1e-6
N_MOD = 6

A_HEADS = 8
A_KV_HEADS = 2
A_GROUP = A_HEADS // A_KV_HEADS
A_HEAD_DIM = 64
A_WIDTH = A_HEADS * A_HEAD_DIM
A_KV_WIDTH = A_KV_HEADS * A_HEAD_DIM
A_SCALE = A_HEAD_DIM ** -0.5
ROPE_FREQS = A_HEAD_DIM // 4

B_GROUPS = 4
B_WIDTH = D_MODEL // 2
B_GROUP_DIM = B_WIDTH // B_GROUPS
POOL_WINDOWS = (2, 4, 8, 16)

EVEN_IN = A_WIDTH + 2 * A_KV_WIDTH + B_WIDTH
EVEN_OUT = A_WIDTH + B_WIDTH

C_HEADS = 16
C_HEAD_DIM = D_MODEL // C_HEADS
C_WIDTH = C_HEADS * C_HEAD_DIM
C_SCALE = C_HEAD_DIM ** -0.5
NA_ROWS_MAX = 8
NA_COLS = 16

E_PER_GROUP = 8
N_EXPERTS_2 = N_GROUPS * E_PER_GROUP
D_EXPERT = D_MODEL // 2
MOE_BLOCK = 128


def rmsnorm(x, g):
    xf = x.astype(jnp.float32)
    y = xf * lax.rsqrt(jnp.mean(xf * xf, axis=-1, keepdims=True) + EPS)
    return (y * g.astype(jnp.float32)).astype(x.dtype)

def modulate(h, shift, scale):
    return h * (1 + scale) + shift

def axial_rope_tables(n_tok):
    t = jnp.arange(n_tok, dtype=jnp.int32)
    pos = jnp.stack([t // GRID_W, t % GRID_W], axis=-1).astype(jnp.float32)
    inv = ROPE_THETA ** (-jnp.arange(ROPE_FREQS, dtype=jnp.float32) / ROPE_FREQS)
    ang = pos[:, :, None] * inv
    return jnp.cos(ang), jnp.sin(ang)

def apply_axial_rope(x, cos, sin):
    sh = x.shape
    xr = x.reshape(sh[:-1] + (2, 2, ROPE_FREQS)).astype(jnp.float32)
    x1, x2 = xr[..., 0, :], xr[..., 1, :]
    out = jnp.stack([x1 * cos - x2 * sin, x1 * sin + x2 * cos], axis=-2)
    return out.reshape(sh).astype(x.dtype)

def gqa_queries(q, gain):
    B, L, _ = q.shape
    q = rmsnorm(q.reshape(B, L, A_KV_HEADS, A_GROUP, A_HEAD_DIM), gain)
    return q.transpose(0, 2, 3, 1, 4)

def gqa_keys(k, gain):
    B, L, _ = k.shape
    return rmsnorm(k.reshape(B, L, A_KV_HEADS, A_HEAD_DIM), gain).transpose(0, 2, 1, 3)

def gqa_values(v):
    B, L, _ = v.shape
    return v.reshape(B, L, A_KV_HEADS, A_HEAD_DIM).transpose(0, 2, 1, 3)

def pool_mixer(u, pool_w, pool_scale):
    B, L, _ = u.shape
    ug = u.reshape(B, L, B_GROUPS, B_GROUP_DIM).astype(jnp.float32)
    cs = jnp.concatenate([jnp.zeros((B, 1, B_GROUPS, B_GROUP_DIM), jnp.float32), jnp.cumsum(ug, axis=1)], axis=1)
    t = jnp.arange(L, dtype=jnp.int32)
    means = []
    for g, w in enumerate(POOL_WINDOWS):
        lo = jnp.clip(t - w // 2, 0, L)
        hi = jnp.clip(t - w // 2 + w, 0, L)
        cnt = (hi - lo).astype(jnp.float32)
        cs_g = cs[:, :, g]
        means.append((cs_g[:, hi] - cs_g[:, lo]) / cnt[None, :, None])
    pooled = (jnp.stack(means, axis=2) - ug).astype(u.dtype)
    mixed = jnp.einsum('blgc,gcd->blgd', pooled, pool_w)
    return mixed.reshape(B, L, B_WIDTH) * pool_scale

def even_mixer(h, hc, w_in, w_out, q_gain, k_gain, pool_w, pool_scale, cos, sin, ctx_out):
    B, S, _ = h.shape
    cuts = (A_WIDTH, A_WIDTH + A_KV_WIDTH, A_WIDTH + 2 * A_KV_WIDTH)
    q, k, v, u = jnp.split(h @ w_in, cuts, axis=-1)
    if ctx_out:
        qc, kc, vc, uc = jnp.split(hc @ w_in, cuts, axis=-1)
    else:
        kc, vc = jnp.split(hc @ w_in[:, A_WIDTH:A_WIDTH + 2 * A_KV_WIDTH], 2, axis=-1)
    kc_h = gqa_keys(kc, k_gain)
    vc_h = gqa_values(vc)
    q_h = apply_axial_rope(gqa_queries(q, q_gain), cos, sin)
    k_h = apply_axial_rope(gqa_keys(k, k_gain), cos, sin)
    k_all = jnp.concatenate([kc_h, k_h], axis=2)
    v_all = jnp.concatenate([vc_h, gqa_values(v)], axis=2)
    nb = S // Q_BLOCK
    qb = q_h.reshape(B, A_KV_HEADS, A_GROUP, nb, Q_BLOCK, A_HEAD_DIM).transpose(3, 0, 1, 2, 4, 5)

    def attend_block(qblk):
        s = jnp.einsum('bhgqd,bhkd->bhgqk', qblk, k_all).astype(jnp.float32) * A_SCALE
        p = jax.nn.softmax(s, axis=-1).astype(v_all.dtype)
        return jnp.einsum('bhgqk,bhkd->bhgqd', p, v_all)

    o = lax.map(attend_block, qb)
    a_lat = o.transpose(1, 0, 4, 2, 3, 5).reshape(B, S, A_WIDTH)
    b_lat = pool_mixer(u, pool_w, pool_scale)
    y = jnp.concatenate([a_lat, b_lat], axis=-1) @ w_out
    if not ctx_out:
        return y, None
    Lc = hc.shape[1]
    qc_h = gqa_queries(qc, q_gain)
    s = jnp.einsum('bhgqd,bhkd->bhgqk', qc_h, kc_h).astype(jnp.float32) * A_SCALE
    p = jax.nn.softmax(s, axis=-1).astype(vc_h.dtype)
    a_ctx = jnp.einsum('bhgqk,bhkd->bhgqd', p, vc_h).transpose(0, 3, 1, 2, 4).reshape(B, Lc, A_WIDTH)
    b_ctx = pool_mixer(uc, pool_w, pool_scale)
    yc = jnp.concatenate([a_ctx, b_ctx], axis=-1) @ w_out
    return y, yc

def c_heads(t):
    B, L, _ = t.shape
    return t.reshape(B, L, C_HEADS, C_HEAD_DIM).transpose(0, 2, 1, 3)

def odd_mixer(h, hc, w_in, w_out, rel_bias, ctx_out):
    B, S, _ = h.shape
    rows = S // GRID_W
    kh = min(NA_ROWS_MAX, rows)
    q, k, v = jnp.split(h @ w_in, 3, axis=-1)
    if ctx_out:
        qc, kc, vc = jnp.split(hc @ w_in, 3, axis=-1)
    else:
        kc, vc = jnp.split(hc @ w_in[:, C_WIDTH:], 2, axis=-1)
    kc_h, vc_h = c_heads(kc), c_heads(vc)

    def grid(t):
        return t.reshape(B, rows, GRID_W, C_HEADS, C_HEAD_DIM).transpose(0, 3, 1, 2, 4)

    qg, kg, vg = grid(q), grid(k), grid(v)
    cols = jnp.arange(GRID_W, dtype=jnp.int32)
    col_start = jnp.clip(cols - NA_COLS // 2, 0, GRID_W - NA_COLS)
    col_idx = col_start[:, None] + jnp.arange(NA_COLS, dtype=jnp.int32)[None, :]
    col_off = col_idx - cols[:, None] + (NA_COLS - 1)
    n_loc = kh * NA_COLS

    def row_block(r):
        rs = jnp.clip(r - kh // 2, 0, rows - kh)
        qr = lax.dynamic_index_in_dim(qg, r, axis=2, keepdims=False)
        kr = lax.dynamic_slice_in_dim(kg, rs, kh, axis=2)
        vr = lax.dynamic_slice_in_dim(vg, rs, kh, axis=2)
        kw = kr[:, :, :, col_idx]
        vw = vr[:, :, :, col_idx]
        row_off = rs + jnp.arange(kh, dtype=jnp.int32) - r + (NA_ROWS_MAX - 1)
        bias = rel_bias[:, row_off][:, :, col_off].transpose(0, 2, 1, 3)
        s_loc = jnp.einsum('bhqd,bhiqjd->bhqij', qr, kw).astype(jnp.float32) * C_SCALE + bias.astype(jnp.float32)
        s_ctx = jnp.einsum('bhqd,bhkd->bhqk', qr, kc_h).astype(jnp.float32) * C_SCALE
        s = jnp.concatenate([s_loc.reshape(B, C_HEADS, GRID_W, n_loc), s_ctx], axis=-1)
        p = jax.nn.softmax(s, axis=-1).astype(vw.dtype)
        p_loc = p[..., :n_loc].reshape(B, C_HEADS, GRID_W, kh, NA_COLS)
        return (jnp.einsum('bhqij,bhiqjd->bhqd', p_loc, vw)
                + jnp.einsum('bhqk,bhkd->bhqd', p[..., n_loc:], vc_h))

    o = lax.map(row_block, jnp.arange(rows, dtype=jnp.int32))
    y = o.transpose(1, 0, 3, 2, 4).reshape(B, S, C_WIDTH) @ w_out
    if not ctx_out:
        return y, None
    Lc = hc.shape[1]
    qc_h = c_heads(qc)
    s = jnp.einsum('bhqd,bhkd->bhqk', qc_h, kc_h).astype(jnp.float32) * C_SCALE
    p = jax.nn.softmax(s, axis=-1).astype(vc_h.dtype)
    yc = jnp.einsum('bhqk,bhkd->bhqd', p, vc_h).transpose(0, 2, 1, 3).reshape(B, Lc, C_WIDTH) @ w_out
    return y, yc

def hier_moe(xt, wg, bg, we, be, w1, w3, w2):
    T, D = xt.shape
    xf = xt.astype(jnp.float32)
    g_logits = xf @ wg.astype(jnp.float32) + bg.astype(jnp.float32)
    g_prob = jax.nn.softmax(g_logits, axis=-1)
    g_idx = jnp.argmax(g_logits, axis=-1)
    g_w = jnp.take_along_axis(g_prob, g_idx[:, None], axis=1)[:, 0]
    e_logits = (xf @ we.astype(jnp.float32) + be.astype(jnp.float32)).reshape(T, N_GROUPS, E_PER_GROUP)
    e_logits = jnp.take_along_axis(e_logits, g_idx[:, None, None], axis=1)[:, 0]
    top_p, top_e = lax.top_k(jax.nn.softmax(e_logits, axis=-1), TOP_K)
    top_p = top_p / jnp.sum(top_p, axis=-1, keepdims=True)
    weights = (g_w[:, None] * top_p).reshape(-1)
    flat_e = (g_idx[:, None] * E_PER_GROUP + top_e).reshape(-1)
    n_assign = T * TOP_K
    order = jnp.argsort(flat_e)
    sorted_e = flat_e[order]
    tok = order // TOP_K
    counts = jnp.bincount(flat_e, length=N_EXPERTS_2)
    start = jnp.cumsum(counts) - counts
    padded = (counts + MOE_BLOCK - 1) // MOE_BLOCK * MOE_BLOCK
    pend = jnp.cumsum(padded)
    pstart = pend - padded
    dest = pstart[sorted_e] + jnp.arange(n_assign, dtype=jnp.int32) - start[sorted_e]
    n_blocks = -(-n_assign // MOE_BLOCK) + N_EXPERTS_2
    xpad = jnp.zeros((n_blocks * MOE_BLOCK, D), xt.dtype).at[dest].set(xt[tok])
    block_e = jnp.minimum(jnp.searchsorted(pend, jnp.arange(n_blocks, dtype=jnp.int32) * MOE_BLOCK, side='right'), N_EXPERTS_2 - 1)

    def expert_block(args):
        xb, e = args
        hb = jax.nn.silu(xb @ w1[e]) * (xb @ w3[e])
        return hb @ w2[e]

    ypad = lax.map(expert_block, (xpad.reshape(n_blocks, MOE_BLOCK, D), block_e))
    y = ypad.reshape(-1, D)[dest] * weights[order][:, None].astype(xt.dtype)
    return jnp.zeros_like(xt).at[tok].add(y)

def second_inputs(seed: int = 0) -> dict:
    key = jax.random.key(seed)
    ks = iter(jax.random.split(key, 32))
    n_even = (DEPTH_2 + 1) // 2
    n_odd = DEPTH_2 // 2
    D = D_MODEL

    def nrm(shape, scale):
        return jax.random.normal(next(ks), shape, jnp.float32) * scale

    return {
        'x': nrm((BATCH, SEQ, D), 1.0),
        'c': nrm((BATCH, D), 1.0),
        'ctx': nrm((BATCH, CTX_LEN, D), 1.0),
        'c_ctx': nrm((D,), 1.0),
        'ada_w': nrm((DEPTH_2, D, N_MOD * D), 0.5 * D ** -0.5),
        'ada_b': nrm((DEPTH_2, N_MOD * D), 0.02),
        'norm_mix_g': 1.0 + nrm((DEPTH_2, D), 0.1),
        'norm_ffn_g': 1.0 + nrm((DEPTH_2, D), 0.1),
        'even_w_in': nrm((n_even, D, EVEN_IN), D ** -0.5),
        'even_w_out': nrm((n_even, EVEN_OUT, D), EVEN_OUT ** -0.5),
        'a_q_gain': 1.0 + nrm((n_even, A_HEAD_DIM), 0.1),
        'a_k_gain': 1.0 + nrm((n_even, A_HEAD_DIM), 0.1),
        'pool_w': nrm((n_even, B_GROUPS, B_GROUP_DIM, B_GROUP_DIM), B_GROUP_DIM ** -0.5),
        'pool_scale': 1.0 + nrm((n_even, B_WIDTH), 0.1),
        'odd_w_in': nrm((n_odd, D, 3 * C_WIDTH), D ** -0.5),
        'odd_w_out': nrm((n_odd, C_WIDTH, D), C_WIDTH ** -0.5),
        'na_rel_bias': nrm((n_odd, C_HEADS, 2 * NA_ROWS_MAX - 1, 2 * NA_COLS - 1), 0.5),
        'moe_w_group': nrm((DEPTH_2, D, N_GROUPS), D ** -0.5),
        'moe_b_group': nrm((DEPTH_2, N_GROUPS), 0.01),
        'moe_w_expert': nrm((DEPTH_2, D, N_EXPERTS_2), D ** -0.5),
        'moe_b_expert': nrm((DEPTH_2, N_EXPERTS_2), 0.01),
        'moe_w1': nrm((DEPTH_2, N_EXPERTS_2, D, D_EXPERT), D ** -0.5),
        'moe_w3': nrm((DEPTH_2, N_EXPERTS_2, D, D_EXPERT), D ** -0.5),
        'moe_w2': nrm((DEPTH_2, N_EXPERTS_2, D_EXPERT, D), D_EXPERT ** -0.5),
        'final_g': 1.0 + nrm((D,), 0.1),
    }

def second_block(x, c, ctx, c_ctx, ada_w, ada_b, norm_mix_g, norm_ffn_g, even_w_in, even_w_out, a_q_gain, a_k_gain,
              pool_w, pool_scale, odd_w_in, odd_w_out, na_rel_bias, moe_w_group, moe_b_group, moe_w_expert,
              moe_b_expert, moe_w1, moe_w3, moe_w2, final_g):
    B, S, D = x.shape
    Lc = ctx.shape[1]
    cos, sin = axial_rope_tables(S)
    for l in range(DEPTH_2):
        last = l == DEPTH_2 - 1
        mod = jax.nn.silu(c) @ ada_w[l] + ada_b[l]
        mod_c = jax.nn.silu(c_ctx) @ ada_w[l] + ada_b[l]
        sh1, sc1, g1, sh2, sc2, g2 = jnp.split(mod[:, None, :], N_MOD, axis=-1)
        csh1, csc1, cg1, csh2, csc2, cg2 = jnp.split(mod_c, N_MOD, axis=-1)
        h = modulate(rmsnorm(x, norm_mix_g[l]), sh1, sc1)
        hc = modulate(rmsnorm(ctx, norm_mix_g[l]), csh1, csc1)
        if l % 2 == 0:
            i = l // 2
            y, yc = even_mixer(h, hc, even_w_in[i], even_w_out[i], a_q_gain[i], a_k_gain[i], pool_w[i],
                               pool_scale[i], cos, sin, not last)
        else:
            i = l // 2
            y, yc = odd_mixer(h, hc, odd_w_in[i], odd_w_out[i], na_rel_bias[i], not last)
        x = x + g1 * y
        h2 = modulate(rmsnorm(x, norm_ffn_g[l]), sh2, sc2)
        moe_args = (moe_w_group[l], moe_b_group[l], moe_w_expert[l], moe_b_expert[l], moe_w1[l], moe_w3[l], moe_w2[l])
        if not last:
            ctx = ctx + cg1 * yc
            hc2 = modulate(rmsnorm(ctx, norm_ffn_g[l]), csh2, csc2)
            f = hier_moe(jnp.concatenate([h2.reshape(B * S, D), hc2.reshape(B * Lc, D)], axis=0), *moe_args)
            x = x + g2 * f[:B * S].reshape(B, S, D)
            ctx = ctx + cg2 * f[B * S:].reshape(B, Lc, D)
        else:
            f = hier_moe(h2.reshape(B * S, D), *moe_args)
            x = x + g2 * f.reshape(B, S, D)
    return rmsnorm(x, final_g)


def setup_inputs(seed=0):
    out = dict(first_inputs(seed))
    for name, value in second_inputs(seed + 1).items():
        if name != "x":
            out[name + "_2"] = value
    return out


def reference(
    x, p, norm_mix, w_in, rwkv_mu, rwkv_w0, rwkv_w2, rwkv_a0, rwkv_a2, rwkv_g2, rwkv_k_k,
    rwkv_k_a, rwkv_r_k, rwkv_ln_w, rwkv_ln_b, q_norm, k_norm, lambda_q1, lambda_k1, lambda_q2,
    lambda_k2, subln_w, w_branch_rwkv, w_branch_diff, w_out, norm_ffn, w_group, b_group,
    w_expert_router, b_expert_router, w_gate, w_up, w_down, norm_ple, w_ple_gate, w_ple_proj,
    c_2, ctx_2, c_ctx_2, ada_w_2, ada_b_2, norm_mix_g_2, norm_ffn_g_2, even_w_in_2,
    even_w_out_2, a_q_gain_2, a_k_gain_2, pool_w_2, pool_scale_2, odd_w_in_2, odd_w_out_2,
    na_rel_bias_2, moe_w_group_2, moe_b_group_2, moe_w_expert_2, moe_b_expert_2, moe_w1_2,
    moe_w3_2, moe_w2_2, final_g_2,
):
    x = first_block(
        x, p, norm_mix, w_in, rwkv_mu, rwkv_w0, rwkv_w2, rwkv_a0, rwkv_a2, rwkv_g2, rwkv_k_k,
        rwkv_k_a, rwkv_r_k, rwkv_ln_w, rwkv_ln_b, q_norm, k_norm, lambda_q1, lambda_k1,
        lambda_q2, lambda_k2, subln_w, w_branch_rwkv, w_branch_diff, w_out, norm_ffn, w_group,
        b_group, w_expert_router, b_expert_router, w_gate, w_up, w_down, norm_ple, w_ple_gate,
        w_ple_proj,
    )
    return second_block(
        x, c_2, ctx_2, c_ctx_2, ada_w_2, ada_b_2, norm_mix_g_2, norm_ffn_g_2, even_w_in_2,
        even_w_out_2, a_q_gain_2, a_k_gain_2, pool_w_2, pool_scale_2, odd_w_in_2, odd_w_out_2,
        na_rel_bias_2, moe_w_group_2, moe_b_group_2, moe_w_expert_2, moe_b_expert_2, moe_w1_2,
        moe_w3_2, moe_w2_2, final_g_2,
    )


_drawn_inputs = setup_inputs


def setup_inputs(seed=0):
    import zlib

    import numpy as np

    out = dict(_drawn_inputs(seed))
    spreads = {}
    factors = {'rwkv_ln_b': 4.137,
     'lambda_k1': 2.88,
     'lambda_q2': 3.226,
     'lambda_k2': 4.467,
     'b_group': 3.788,
     'b_expert_router': 3.394,
     'norm_ple': 2.911,
     'norm_mix_g_2': 2.849,
     'a_q_gain_2': 8.0,
     'a_k_gain_2': 8.0,
     'pool_scale_2': 3.295,
     'na_rel_bias_2': 5.908,
     'moe_b_group_2': 36.584,
     'moe_b_expert_2': 28.186}
    for name, (base, spread) in spreads.items():
        noise = np.random.default_rng([zlib.crc32(name.encode()), seed]).standard_normal(out[name].shape)
        drawn = base * np.exp(spread * noise) if base else spread * noise
        out[name] = jnp.asarray(drawn.astype(out[name].dtype))
    for name, factor in factors.items():
        out[name] = (out[name] * factor).astype(out[name].dtype)
    return out
```

```python
import math
from contextlib import ExitStack

import numpy as np

import concourse.bass as bass
from concourse import mybir

ALU = mybir.AluOpType
ACT = mybir.ActivationFunctionType
AX = mybir.AxisListType
F32 = mybir.dt.float32
I32 = mybir.dt.int32
U32 = mybir.dt.uint32

P = 128
D = 1024
KD = D // P
SEQ = 512
CTXL = 256
XT0 = CTXL // P
NT = SEQ // P
NTA = NT + XT0
EPS = 1e-6
NEG = -1e30

RW = 512
HD = 64
CH = 64
NCH = SEQ // CH
GN_EPS = 64e-5
LVL = 6

NE = 32
FF = 512
KF = FF // P
NG = 4
EPG = 8
MAXOV = 2 * NTA
SLOTS = (NE + MAXOV) * P

C_IDENT = 0
C_TRI = C_IDENT + P
C_ONES = C_TRI + P
C_BLK = C_ONES + P
C_CAUS = C_BLK + P
C_HIND = C_CAUS + P
C_SCAN = C_HIND + 2
C_UNIT = C_SCAN + SEQ
C_LVL = C_UNIT + 4 * P
C_IO = C_LVL + LVL * P
C_COL = C_IO + NE
C_END = C_COL + HD


def constants():
    p = np.arange(P)
    c = np.zeros((P, C_END), np.float32)
    c[:, C_IDENT:C_IDENT + P] = np.eye(P)
    s, t = p[:, None], p[None, :]
    c[:, C_TRI:C_TRI + P] = s < t
    c[:, C_ONES:C_ONES + P] = 1
    c[:, C_BLK:C_BLK + P] = s // HD == t // HD
    c[:, C_CAUS:C_CAUS + P] = np.where(t <= s, 0, NEG)
    c[:, C_HIND:C_HIND + 2] = p[:, None] // HD == np.arange(2)[None, :]
    c[:, C_SCAN:C_SCAN + SEQ] = (np.arange(SEQ) % CH != 0)[None, :]
    same = s // CH == t // CH
    for j, m in enumerate((same & (s < t), -1.0 * (same & (s <= t)), same & (s < t), same & (s <= t))):
        c[:, C_UNIT + j * P:C_UNIT + (j + 1) * P] = m
    for l in range(LVL):
        b = 1 << l
        c[:, C_LVL + l * P:C_LVL + (l + 1) * P] = (s // (2 * b) == t // (2 * b)) & (s // b % 2 == 0) & (t // b % 2 == 1)
    c[:, C_IO:C_IO + NE] = np.arange(NE)
    q = p % HD
    start = np.clip(q - 8, 0, HD - 16)
    j = np.arange(HD)[None, :]
    c[:, C_COL:C_COL + HD] = np.where((j >= start[:, None]) & (j < start[:, None] + 16), 0, NEG)

    f = np.float32
    inv1 = (f(10000.0) ** (-np.arange(0, 64, 2, dtype=f) / f(64))).astype(f)
    ang1 = np.arange(SEQ, dtype=f)[:, None] * inv1[None, :]
    inv2 = (f(10000.0) ** (-np.arange(16, dtype=f) / f(16))).astype(f)
    tt = np.arange(SEQ)
    pos = np.stack([tt // 64, tt % 64], -1).astype(f)
    ang2 = (pos[:, :, None] * inv2).reshape(SEQ, 32)
    rope = np.stack([np.concatenate([np.cos(a), np.sin(a)], 1) for a in (ang1, ang2)]).astype(f)

    def bands(L):
        out = np.zeros((4, L, L), np.float32)
        t = np.arange(L)
        for g, w in enumerate((2, 4, 8, 16)):
            lo, hi = np.clip(t - w // 2, 0, L), np.clip(t - w // 2 + w, 0, L)
            ss = np.arange(L)[:, None]
            out[g] = ((ss >= lo) & (ss < hi)) / (hi - lo).astype(np.float32) - np.eye(L)
        return out

    return {"table": c, "rope": rope, "band_x": bands(SEQ), "band_c": bands(CTXL)}


class Scope:

    used = []

    def __init__(self, nc, name):
        self.nc, self.name, self.stack, self.sems = nc, name, ExitStack(), []

    def __enter__(self):
        return self

    def __exit__(self, *a):
        self.stack.__exit__(*a)
        Scope.used += self.sems
        if len(Scope.used) > 120:
            self.nc.clear_and_free_semaphores(Scope.used)
            self.nc.all_engine_barrier()
            Scope.used = []

    def sb(self, name, shape, dt=F32):
        return self.stack.enter_context(self.nc.sbuf_tensor(f"{self.name}_{name}", shape, dt))

    def ps(self, name, banks=1):
        return self.stack.enter_context(self.nc.psum_tensor(f"{self.name}_psum_{name}", [P, 512 * banks], F32))

    def sem(self, name):
        self.sems.append(self.nc.alloc_semaphore(f"{self.name}_{name}"))
        return self.sems[-1]

    def block(self):
        return self.stack.enter_context(self.nc.Block())


class Chain:

    def __init__(self, eng, sem):
        self.eng, self.sem, self.n = eng, sem, 0

    def __call__(self, ins):
        self.n += 1
        ins.then_inc(self.sem, 1)
        self.eng.wait_ge(self.sem, self.n)


def bc_row(ap, n):
    return ap.rearrange("(a n) -> a n", a=1).to_broadcast([P, n])


def norm_phase(nc, name, xs, tab, gain, hT=None, htok=None, mods=None):
    n = len(xs)
    with Scope(nc, name) as s:
        G = s.sb("gain", [P, D])
        rows = []
        for m in mods or []:
            if not any(m is r for r in rows):
                rows.append(m)
        SC = [s.sb(f"scale{i}", [P, D]) for i in range(len(rows))]
        SH = [s.sb(f"shift{i}", [P, D]) for i in range(len(rows))]
        H = htok if htok is not None else s.sb("h", [P, n, D])
        sq = s.sb("sq", [P, D])
        ss = s.sb("ss", [P, 3, n])
        pt = [s.ps(f"pt{i}", 2) for i in range(2)]
        rows_in, ssq_done, ms_done, root_done, h_done = (s.sem(k) for k in ("rows", "ssq", "ms", "root", "h"))
        t_done, evac_a, evac_v, v_own, a_own = (s.sem(k) for k in ("t", "eva", "evv", "vown", "aown"))
        nrows = 1 + 2 * len(rows)
        block = s.block()

        @block.sync
        def _(sp):
            sp.dma_start(G[:, :], bc_row(gain, D)).then_inc(rows_in, 16)
            for i, (sc, sh) in enumerate(rows):
                sp.dma_start(SC[i][:, :], bc_row(sc, D)).then_inc(rows_in, 16)
                sp.dma_start(SH[i][:, :], bc_row(sh, D)).then_inc(rows_in, 16)

        @block.scalar
        def _(act):
            link = Chain(act, a_own)
            for t in range(n):
                link(act.activation(sq[:, :], xs[t], ACT.Square, accum_out=ss[:, 0, t:t + 1]))
            act.activation(ss[0:1, 2, 0:1], ss[0:1, 0, 0:1], ACT.Copy).then_inc(ssq_done, 1)
            act.wait_ge(ms_done, 1)
            act.activation(ss[:, 2, :], ss[:, 1, :], ACT.Sqrt).then_inc(root_done, 1)
            if hT is not None:
                for t in range(n):
                    act.wait_ge(t_done, 2 * t + 1)
                    act.activation(hT[:, 0:4, t * P:(t + 1) * P], pt[t % 2][:, 0:512].rearrange("p (k t) -> p k t", k=4),
                                   ACT.Copy).then_inc(evac_a, 1)

        @block.vector
        def _(v):
            link = Chain(v, v_own)
            v.wait_ge(ssq_done, 1)
            v.tensor_scalar(ss[:, 1, :], ss[:, 0, :], 1.0 / D, EPS, ALU.mult, ALU.add).then_inc(ms_done, 1)
            v.wait_ge(rows_in, 16 * nrows)
            for i in range(len(rows)):
                link(v.scalar_tensor_tensor(out=SC[i][:, :], in0=SC[i][:, :], scalar=1.0, in1=G[:, :], op0=ALU.add, op1=ALU.mult))
            v.wait_ge(root_done, 1)
            link(v.reciprocal(ss[:, 0, :], ss[:, 2, :]))

            def evac(t):
                v.wait_ge(t_done, 2 * t + 2)
                v.tensor_copy(hT[:, 4:8, t * P:(t + 1) * P],
                              pt[t % 2][:, 512:1024].rearrange("p (k t) -> p k t", k=4)).then_inc(evac_v, 1)

            for t in range(n):
                i = [k for k, m in enumerate(rows) if mods and m is mods[t]]
                g = SC[i[0]] if i else G
                ins = v.scalar_tensor_tensor(out=H[:, t, :], in0=xs[t], scalar=ss[:, 0, t:t + 1], in1=g[:, :],
                                             op0=ALU.mult, op1=ALU.mult)
                if i:
                    link(ins)
                    ins = v.tensor_tensor(H[:, t, :], H[:, t, :], SH[i[0]][:, :], ALU.add)
                ins.then_inc(h_done, 1)
                if hT is not None and t >= 1:
                    evac(t - 1)
            if hT is not None:
                evac(n - 1)

        if hT is not None:
            @block.tensor
            def _(pe):
                for t in range(n):
                    pe.wait_ge(h_done, t + 1)
                    if t >= 2:
                        pe.wait_ge(evac_a, t - 1)
                        pe.wait_ge(evac_v, t - 1)
                    for k in range(KD):
                        mm = pe.transpose(pt[t % 2][:, k * P:(k + 1) * P], H[:, t, k * P:(k + 1) * P],
                                          tab[:, C_IDENT:C_IDENT + P])
                        if k % 4 == 3:
                            mm.then_inc(t_done, 1)


def linear_phase(nc, name, lhs, nk, tiles, W, cols, evac, on="v", loads=()):
    nch = (cols + 511) // 512
    RING, BANKS = 3, 6
    jobs = [(c, t) for c in range(nch) for t in tiles(c)]
    last_of = {c: max(i for i, j in enumerate(jobs) if j[0] == c) for c in range(nch)}
    with Scope(nc, name) as s:
        w = [s.sb(f"w{i}", [P, nk, 512]) for i in range(RING)]
        banks = [s.ps(f"acc{i}") for i in range(BANKS)]
        w_in = [s.sem(f"w{i}") for i in range(RING)]
        mm_done, out_done, own, pre_in = s.sem("mm"), s.sem("out"), s.sem("own"), s.sem("pre")
        block = s.block()

        @block.sync
        def _(sp):
            for c in range(nch):
                n = min(512, cols - c * 512)
                if c >= RING:
                    sp.wait_ge(mm_done, last_of[c - RING] + 1)
                sp.dma_start(w[c % RING][:, :, 0:n], W[:, c * 512:c * 512 + n].rearrange("(k p) n -> p k n", p=P)
                             ).then_inc(w_in[c % RING], 16)
                if c == 0:
                    for dst, src in loads:
                        sp.dma_start(dst, src).then_inc(pre_in, 16)

        @block.tensor
        def _(pe):
            for i, (c, t) in enumerate(jobs):
                n = min(512, cols - c * 512)
                pe.wait_ge(w_in[c % RING], 16 * (c // RING + 1))
                if i >= BANKS:
                    pe.wait_ge(out_done, i - BANKS + 1)
                for k in range(nk):
                    mm = pe.matmul(banks[i % BANKS][:, 0:n], lhs(k, t), w[c % RING][:, k, 0:n],
                                   start=(k == 0), stop=(k == nk - 1))
                mm.then_inc(mm_done, 1)

        def finish(eng):
            link = Chain(eng, own)
            if loads:
                eng.wait_ge(pre_in, 16 * len(loads))
            for i, (c, t) in enumerate(jobs):
                n = min(512, cols - c * 512)
                eng.wait_ge(mm_done, i + 1)
                evac(eng, link, banks[i % BANKS][:, 0:n], t, c).then_inc(out_done, 1)

        if on == "v":
            @block.vector
            def _(v):
                finish(v)
        else:
            @block.scalar
            def _(act):
                finish(act)


def transpose_phase(nc, name, src, nt, nk, dst, tab):
    pieces = [(t, k) for t in range(nt) for k in range(nk)]
    groups = [pieces[i:i + 4] for i in range(0, len(pieces), 4)]
    assert nk % 4 == 0
    with Scope(nc, name) as s:
        banks = [s.ps(f"pt{i}") for i in range(4)]
        t_done, ev = s.sem("t"), [s.sem("eva"), s.sem("evv")]
        block = s.block()

        @block.tensor
        def _(pe):
            for i, g in enumerate(groups):
                if i >= 4:
                    pe.wait_ge(ev[i % 2], (i - 4) // 2 + 1)
                for j, (t, k) in enumerate(g):
                    mm = pe.transpose(banks[i % 4][:, j * P:(j + 1) * P], src(t, k), tab[:, C_IDENT:C_IDENT + P])
                mm.then_inc(t_done, 1)

        def evac(i):
            t, k = groups[i][0]
            return dst[:, k:k + 4, t * P:(t + 1) * P], banks[i % 4][:, :].rearrange("p (k t) -> p k t", k=4)

        @block.scalar
        def _(act):
            for i in range(0, len(groups), 2):
                act.wait_ge(t_done, i + 1)
                act.activation(*evac(i), ACT.Copy).then_inc(ev[0], 1)

        @block.vector
        def _(v):
            for i in range(1, len(groups), 2):
                v.wait_ge(t_done, i + 1)
                v.tensor_copy(*evac(i)).then_inc(ev[1], 1)


def heads_phase(nc, name, tab, items, T):
    with Scope(nc, name) as s:
        mh = max(i["heads"] for i in items)
        nj = sum(len(i["tiles"]) for i in items)
        tmp = s.sb("tmp", [P, mh * 32])
        tmp2 = s.sb("tmp2", [P, mh * 32])
        sqt = s.sb("sq", [P, mh * 64])
        work = [s.sb(f"work{i}", [P, mh * 64]) for i in range(2)]
        st = s.sb("stat", [P, nj, mh])
        st2 = s.sb("stat2", [P, nj, mh])
        gains = [s.sb(f"gain{i}", [P, 64]) for i in range(len(items))]
        rope = s.sb("rope", [P, 4, 64])
        pt = [s.ps(f"pt{i}", 2) for i in range(2)]
        loaded, ss_done, root_done, y_done, t_done, evac = (s.sem(k) for k in ("ld", "ss", "root", "y", "t", "evac"))
        own = s.sem("own")
        loads = []
        for i, it in enumerate(items):
            if it["gain"] is not None:
                loads.append((gains[i][:, :], bc_row(it["gain"], 64)))
        rsrc = [it["rope_src"] for it in items if it["rope_src"] is not None]
        if rsrc:
            loads.append((rope[:, :, :], rsrc[0].rearrange("(t p) c -> p t c", p=P)))
        jobs = [(i, t) for i in range(len(items)) for t in items[i]["tiles"]]
        block = s.block()

        @block.sync
        def _(sp):
            for d, sr in loads:
                sp.dma_start(d, sr).then_inc(loaded, 16)

        @block.vector
        def _(v):
            link = Chain(v, own)
            normed = any(it["gain"] is not None for it in items)
            if normed:
                for j, (i, t) in enumerate(jobs):
                    it = items[i]
                    h = it["heads"]
                    sq = sqt[:, 0:h * 64].rearrange("p (h d) -> p h d", d=64)
                    link(v.tensor_tensor(sq, it["src"](t), it["src"](t), ALU.mult))
                    link(v.tensor_reduce(st[:, j, 0:h], sq, AX.X, ALU.add))
                    if h < mh:
                        link(v.memset(st[:, j, h:mh], 1.0))
                v.tensor_scalar(st2[:, :, :], st[:, :, :], 1.0 / 64, EPS, ALU.mult, ALU.add).then_inc(ss_done, 1)
                v.wait_ge(root_done, 1)
                link(v.reciprocal(st2[:, :, :], st[:, :, :]))
            if loads:
                v.wait_ge(loaded, 16 * len(loads))
            for j, (i, t) in enumerate(jobs):
                it = items[i]
                h = it["heads"]
                src = it["src"](t)
                if j >= 2:
                    v.wait_ge(t_done, j - 1)
                y = work[j % 2][:, 0:h * 64].rearrange("p (h d) -> p h d", d=64)
                if it["gain"] is None:
                    v.tensor_scalar(y, src, it["scale"], None, ALU.mult).then_inc(y_done, 1)
                    continue
                link(v.tensor_tensor(src, src, st2[:, j, 0:h].unsqueeze(2).to_broadcast([P, h, 64]), ALU.mult))
                g = gains[i][:, :].unsqueeze(1).to_broadcast([P, h, 64])
                if it["rope"] is None:
                    link(v.tensor_scalar(src, src, it["scale"], None, ALU.mult))
                    v.tensor_tensor(y, src, g, ALU.mult).then_inc(y_done, 1)
                    continue
                link(v.tensor_tensor(src, src, g, ALU.mult))
                A, F = it["axes"], 32 // it["axes"]
                for a in range(A):
                    x1, x2 = src[:, :, 2 * F * a:2 * F * a + F], src[:, :, 2 * F * a + F:2 * F * (a + 1)]
                    y1, y2 = y[:, :, 2 * F * a:2 * F * a + F], y[:, :, 2 * F * a + F:2 * F * (a + 1)]
                    r = it["rope"](t)
                    co = rope[:, r, F * a:F * (a + 1)].unsqueeze(1).to_broadcast([P, h, F])
                    si = rope[:, r, 32 + F * a:32 + F * (a + 1)].unsqueeze(1).to_broadcast([P, h, F])
                    u = tmp[:, 0:h * F].rearrange("p (h f) -> p h f", f=F)
                    w = tmp2[:, 0:h * F].rearrange("p (h f) -> p h f", f=F)
                    v.tensor_tensor(u, x1, co, ALU.mult).then_inc(own, 1)
                    link.n += 1
                    link(v.tensor_tensor(w, x2, si, ALU.mult))
                    link(v.tensor_tensor(y1, u, w, ALU.subtract))
                    v.tensor_tensor(u, x2, co, ALU.mult).then_inc(own, 1)
                    link.n += 1
                    link(v.tensor_tensor(w, x1, si, ALU.mult))
                    link(v.tensor_tensor(y2, u, w, ALU.add))
                v.tensor_scalar(y, y, it["scale"], None, ALU.mult).then_inc(y_done, 1)

        @block.scalar
        def _(act):
            if any(it["gain"] is not None for it in items):
                act.wait_ge(ss_done, 1)
                act.activation(st[:, :, :], st2[:, :, :], ACT.Sqrt).then_inc(root_done, 1)
            for j, (i, t) in enumerate(jobs):
                act.wait_ge(t_done, j + 1)
                m = items[i]["heads"] // 2
                act.activation(items[i]["dst"](t), pt[j % 2][:, 0:m * P].rearrange("p (m t) -> p m t", m=m),
                               ACT.Copy).then_inc(evac, 1)

        @block.tensor
        def _(pe):
            for j, (i, t) in enumerate(jobs):
                pe.wait_ge(y_done, j + 1)
                if j >= 2:
                    pe.wait_ge(evac, j - 1)
                m = items[i]["heads"] // 2
                for k in range(m):
                    mm = pe.transpose(pt[j % 2][:, k * P:(k + 1) * P], work[j % 2][:, k * P:(k + 1) * P],
                                      tab[:, C_IDENT:C_IDENT + P])
                mm.then_inc(t_done, 1)


def attention_phase(nc, name, tab, jobs, bias=None):
    nj = len(jobs)
    for j in jobs:
        j["nt"] = j["keys"] // P
        j["na"] = min(j["nt"], 4)
    cum_v = np.cumsum([1 if j["nt"] > j["na"] else 0 for j in jobs]).tolist()
    with Scope(nc, name) as s:
        psS = [s.ps(f"score{i}", 2) for i in range(2)]
        psT = s.ps("turned", 2)
        psO = [s.ps(f"out{i}") for i in range(2)]
        pr = [s.sb(f"prob{i}", [P, 768]) for i in range(2)]
        prT = [s.sb(f"probT{i}", [P, 768]) for i in range(2)]
        mx = s.sb("max", [P, nj])
        nm = s.sb("negmax", [P, nj])
        sm = s.sb("sum", [P, nj])
        rs = s.sb("rsum", [P, nj])
        s_done, max_done, exp_done, t_done, ev_a, ev_v, pv_done, post_done, own = (
            s.sem(k) for k in ("s", "max", "exp", "t", "eva", "evv", "pv", "post", "own"))
        if bias:
            bload, bheads, per = bias["load"], bias["heads"], bias["per"]
            bt = [s.sb(f"bias{i}", [P, 16, 64]) for i in range(2)]
            b_in = [s.sem(f"bin{i}") for i in range(2)]
            b_ready = s.sem("bready")
        block = s.block()

        if bias:
            @block.sync
            def _(sp):
                for h in range(bheads):
                    if h >= 2:
                        sp.wait_ge(max_done, per * (h - 1))
                    for dst, src in bload(h, bt[h % 2]):
                        sp.dma_start(dst, src).then_inc(b_in[h % 2], 16)

        @block.tensor
        def _(pe):
            def scores(j):
                if j >= 2:
                    pe.wait_ge(exp_done, j - 1)
                jb = jobs[j]
                for c in range(0, jb["keys"], 512):
                    n = min(512, jb["keys"] - c)
                    mm = pe.matmul(psS[j % 2][:, c:c + n], jb["q"], jb["k"][:, c:c + n], start=True, stop=True)
                mm.then_inc(s_done, 1)

            def turn(j):
                pe.wait_ge(exp_done, j + 1)
                if j >= 1:
                    pe.wait_ge(ev_a, j)
                    if cum_v[j - 1]:
                        pe.wait_ge(ev_v, cum_v[j - 1])
                for k in range(jobs[j]["nt"]):
                    mm = pe.transpose(psT[:, k * P:(k + 1) * P], pr[j % 2][:, k * P:(k + 1) * P],
                                      tab[:, C_IDENT:C_IDENT + P])
                mm.then_inc(t_done, 1)

            def values(j):
                jb = jobs[j]
                pe.wait_ge(ev_a, j + 1)
                if cum_v[j]:
                    pe.wait_ge(ev_v, cum_v[j])
                if j >= 2:
                    pe.wait_ge(post_done, j - 1)
                for k in range(jb["nt"]):
                    mm = pe.matmul(psO[j % 2][:, 0:jb["dv"]], prT[j % 2][:, k * P:(k + 1) * P], jb["v"](k),
                                   start=(k == 0), stop=(k == jb["nt"] - 1))
                mm.then_inc(pv_done, 1)

            for j in range(nj + 2):
                if j < nj:
                    scores(j)
                if 1 <= j <= nj:
                    turn(j - 1)
                if j >= 2:
                    values(j - 2)

        @block.scalar
        def _(act):
            for j in range(nj + 1):
                if j < nj:
                    act.wait_ge(max_done, j + 1)
                    if j >= 2:
                        act.wait_ge(t_done, j - 1)
                    act.activation(pr[j % 2][:, 0:jobs[j]["keys"]], psS[j % 2][:, 0:jobs[j]["keys"]], ACT.Exp,
                                   bias=nm[:, j:j + 1], accum_out=sm[:, j:j + 1]).then_inc(exp_done, 1)
                if j >= 1:
                    i = j - 1
                    n = jobs[i]["na"] * P
                    act.wait_ge(t_done, i + 1)
                    if i >= 2:
                        act.wait_ge(pv_done, i - 1)
                    act.activation(prT[i % 2][:, 0:n], psT[:, 0:n], ACT.Copy).then_inc(ev_a, 1)

        @block.vector
        def _(v):
            link = Chain(v, own)
            for j in range(nj + 2):
                if j < nj:
                    jb = jobs[j]
                    if bias and j % per == 0:
                        h = j // per
                        v.wait_ge(b_in[h % 2], 16 * 2 * (h // 2 + 1))
                        cm = tab[:, C_COL:C_COL + HD].unsqueeze(1).to_broadcast([P, 14, HD])
                        link(v.tensor_tensor(bt[h % 2][:, 1:15, :], bt[h % 2][:, 1:15, :], cm, ALU.add))
                    v.wait_ge(s_done, j + 1)
                    for c, n, ap in jb["add"](bt[(j // per) % 2] if bias else None):
                        link(v.tensor_tensor(psS[j % 2][:, c:c + n], psS[j % 2][:, c:c + n], ap, ALU.add))
                    link(v.tensor_reduce(mx[:, j:j + 1], psS[j % 2][:, 0:jb["keys"]], AX.X, ALU.max))
                    v.tensor_scalar(nm[:, j:j + 1], mx[:, j:j + 1], -1.0, None, ALU.mult).then_inc(max_done, 1)
                if 1 <= j <= nj:
                    i = j - 1
                    a, b = jobs[i]["na"] * P, jobs[i]["nt"] * P
                    if b > a:
                        v.wait_ge(t_done, i + 1)
                        if i >= 2:
                            v.wait_ge(pv_done, i - 1)
                        v.tensor_copy(prT[i % 2][:, a:b], psT[:, a:b]).then_inc(ev_v, 1)
                if j >= 2:
                    i = j - 2
                    v.wait_ge(pv_done, i + 1)
                    link(v.reciprocal(rs[:, i:i + 1], sm[:, i:i + 1]))
                    jobs[i]["post"](v, link, psO[i % 2], rs[:, i:i + 1]).then_inc(post_done, 1)


def feature_phase(nc, name, hT, W, jobs):
    RING, BANKS = 3, 4
    chunks = sorted({j[0] // 2 for j in jobs})
    last_of = {c: max(i for i, j in enumerate(jobs) if j[0] // 2 == c) for c in chunks}
    with Scope(nc, name) as s:
        w = [s.sb(f"w{i}", [P, KD, 256]) for i in range(RING)]
        banks = [s.ps(f"acc{i}") for i in range(BANKS)]
        w_in = [s.sem(f"w{i}") for i in range(RING)]
        mm_done, ev = s.sem("mm"), s.sem("ev")
        block = s.block()

        @block.sync
        def _(sp):
            for c in chunks:
                if c >= RING:
                    sp.wait_ge(mm_done, last_of[c - RING] + 1)
                sp.dma_start(w[c % RING][:, :, :], W[:, c * 256:(c + 1) * 256].rearrange("(k p) n -> p k n", p=P)
                             ).then_inc(w_in[c % RING], 16)

        @block.tensor
        def _(pe):
            for i, (m, c0, n, _, _) in enumerate(jobs):
                c = m // 2
                pe.wait_ge(w_in[c % RING], 16 * (c // RING + 1))
                if i >= BANKS:
                    pe.wait_ge(ev, i - BANKS + 1)
                for k in range(KD):
                    mm = pe.matmul(banks[i % BANKS][:, 0:n], w[c % RING][:, k, (m % 2) * P:(m % 2 + 1) * P],
                                   hT[:, k, c0:c0 + n], start=(k == 0), stop=(k == KD - 1))
                mm.then_inc(mm_done, 1)

        @block.vector
        def _(v):
            for i, (m, c0, n, dst, scale) in enumerate(jobs):
                v.wait_ge(mm_done, i + 1)
                v.tensor_scalar(dst, banks[i % BANKS][:, 0:n], scale, None, ALU.mult).then_inc(ev, 1)


def rwkv_prepare(nc, tab, pr, A, KR, BT, KDT, Vt, KDt, Bt, PC, bonus, gate):
    NPR = 4
    E05 = math.exp(-0.5)
    with Scope(nc, "rr") as s:
        par = s.sb("par", [P, 14 + 6 * NPR])
        w2 = s.sb("w2", [P, RW])
        g2 = s.sb("g2", [P, RW])
        a = s.sb("a", [P, NPR, SEQ])
        ld = s.sb("ld", [P, NPR, SEQ])
        cs = s.sb("cs", [P, NPR, SEQ])
        t1 = s.sb("t1", [P, SEQ])
        t2 = s.sb("t2", [P, SEQ])
        t3 = s.sb("t3", [P, SEQ])
        psA = [s.ps(f"a{i}") for i in range(4)]
        psB = s.ps("b")
        psT = [s.ps(f"t{i}") for i in range(2)]
        in_par, in_w, shift_done, low_done, lora_mm, lora_ev = (s.sem(k) for k in ("par", "w", "sh", "low", "lm", "le"))
        exps_in, exps_out, sq_done, sq_mm, kk_root, root_in = (s.sem(k) for k in ("ei", "eo", "sq", "sm", "kr", "ri"))
        prod_done, bon_mm, fact_done, t_done, t_ev, g_mm, v_own, a_own, z_ev = (
            s.sem(k) for k in ("pd", "bm", "fd", "td", "te", "gm", "vo", "ao", "ze"))
        mu0, W0, A0, KK, KA, RK = 0, 14, 18, 22, 26, 30
        block = s.block()

        def col(o):
            return par[:, o:o + 1]

        @block.sync
        def _(sp):
            sp.dma_start(par[:, 0:14], A["rwkv_mu"].rearrange("(m p) -> p m", p=P)).then_inc(in_par, 16)
            for o, n in ((W0, "rwkv_w0"), (A0, "rwkv_a0"), (KK, "rwkv_k_k"), (KA, "rwkv_k_a"), (RK, "rwkv_r_k")):
                sp.dma_start(par[:, o:o + 4], A[n].rearrange("(m p) -> p m", p=P)).then_inc(in_par, 16)
            sp.dma_start(w2[0:64, :], A["rwkv_w2"]).then_inc(in_w, 16)
            sp.dma_start(w2[64:128, :], A["rwkv_a2"]).then_inc(in_w, 16)
            sp.dma_start(g2[:, :], A["rwkv_g2"]).then_inc(in_w, 16)

        @block.vector
        def _(v):
            link = Chain(v, v_own)
            v.wait_ge(in_par, 96)
            for n, m in enumerate([12, 13] + list(range(12))):
                x = pr[:, m, :]
                v.tensor_tensor(t1[:, 1:SEQ], x[:, 0:SEQ - 1], x[:, 1:SEQ], ALU.subtract).then_inc(v_own, 1)
                link.n += 1
                link(v.tensor_scalar(t1[:, 0:1], x[:, 0:1], -1.0, None, ALU.mult))
                v.scalar_tensor_tensor(out=x, in0=t1[:, :], scalar=col(mu0 + m), in1=x, op0=ALU.mult,
                                       op1=ALU.add).then_inc(shift_done, 1)
                v.wait_ge(shift_done, n + 1)
            for i in range(NPR):
                v.wait_ge(lora_ev, 2 * i + 1)
                link(v.tensor_scalar(ld[:, i, :], ld[:, i, :], -E05, None, ALU.mult))
                link(v.tensor_tensor_scan(cs[:, i, :], tab[:, C_SCAN:C_SCAN + SEQ], ld[:, i, :], 0.0, ALU.mult, ALU.add))
                v.tensor_tensor(ld[:, i, :], cs[:, i, :], ld[:, i, :], ALU.subtract).then_inc(exps_in, 1)
                k, r = pr[:, 4 + i, :], pr[:, i, :]
                kk = t1[:, :]
                link(v.tensor_scalar(kk, k, col(KK + i), None, ALU.mult))
                if i >= 1:
                    v.wait_ge(sq_mm, i)
                v.tensor_tensor(t2[:, :], kk, kk, ALU.mult).then_inc(sq_done, 1)
                v.wait_ge(kk_root, i + 1)
                link(v.tensor_scalar(t3[:, :], t3[:, :], 1e-12, None, ALU.max))
                link(v.reciprocal(t3[:, :], t3[:, :]))
                link(v.tensor_tensor(kk, kk, t3[:, :], ALU.mult))
                v.wait_ge(lora_ev, 2 * i + 2)
                link(v.tensor_scalar(t2[:, :], a[:, i, :], 1.0, col(KA + i), ALU.subtract, ALU.mult))
                link(v.scalar_tensor_tensor(out=k, in0=t2[:, :], scalar=1.0, in1=k, op0=ALU.add, op1=ALU.mult))
                link(v.tensor_tensor(t2[:, :], r, k, ALU.mult))
                if i >= 1:
                    v.wait_ge(bon_mm, i)
                v.tensor_scalar(t3[:, :], t2[:, :], col(RK + i), None, ALU.mult).then_inc(prod_done, 1)
                link(v.tensor_tensor(a[:, i, :], a[:, i, :], kk, ALU.mult))
                v.wait_ge(exps_out, i + 1)
                v.tensor_copy(PC[:, i, :], KR[:, i, 1, :].rearrange("p (c t) -> p c t", t=CH)[:, :, CH - 1]).then_inc(v_own, 1)
                link.n += 1
                v.wait_ge(v_own, link.n)
                link(v.tensor_tensor(KR[:, i, 0, :], KR[:, i, 0, :], kk, ALU.mult))
                link(v.tensor_tensor(KR[:, i, 1, :], KR[:, i, 1, :], r, ALU.mult))
                link(v.tensor_tensor(KDT[:, i, :], BT[:, i, :], k, ALU.mult))
                v.tensor_tensor(BT[:, i, :], BT[:, i, :], a[:, i, :], ALU.mult).then_inc(fact_done, 1)
                v.wait_ge(bon_mm, i + 1)
            v.wait_ge(bon_mm, NPR)
            v.tensor_copy(bonus[:, :], psB[:, 0:32]).then_inc(v_own, 1)
            for t in range(NT):
                v.wait_ge(g_mm, t + 1)
                v.tensor_copy(gate[:, t, :], psA[t][:, :]).then_inc(v_own, 1)

        @block.scalar
        def _(act):
            act.wait_ge(shift_done, 2)
            act.activation(pr[0:64, 12, :], pr[0:64, 12, :], ACT.Tanh).then_inc(low_done, 1)
            act.activation(pr[:, 13, :], pr[:, 13, :], ACT.Sigmoid).then_inc(low_done, 1)
            for i in range(NPR):
                act.wait_ge(lora_mm, 2 * i + 1)
                act.activation(ld[:, i, :], psA[(2 * i) % 4][:, :], ACT.Sigmoid, bias=col(W0 + i)).then_inc(lora_ev, 1)
                act.wait_ge(lora_mm, 2 * i + 2)
                act.activation(a[:, i, :], psA[(2 * i + 1) % 4][:, :], ACT.Sigmoid, bias=col(A0 + i)).then_inc(lora_ev, 1)
            for i in range(NPR):
                act.wait_ge(exps_in, i + 1)
                act.activation(KR[:, i, 1, :], cs[:, i, :], ACT.Exp).then_inc(a_own, 1)
                act.activation(KR[:, i, 0, :], ld[:, i, :], ACT.Exp).then_inc(a_own, 1)
                act.activation(BT[:, i, :], cs[:, i, :], ACT.Exp, scale=-1.0).then_inc(exps_out, 1)
                act.wait_ge(sq_mm, i + 1)
                if i >= 1:
                    act.wait_ge(bon_mm, i)
                act.activation(t3[:, :], psT[i % 2][:, :], ACT.Sqrt).then_inc(kk_root, 1)
            for n in range(3 * NT):
                src, t = divmod(n, NT)
                act.wait_ge(t_done, n + 1)
                dst = (Vt, KDt, Bt)[src]
                act.activation(dst[:, t, :], psT[n % 2][:, :], ACT.Copy, scale=(-1.0 if src == 2 else 1.0)).then_inc(t_ev, 1)

        @block.tensor
        def _(pe):
            pe.wait_ge(in_w, 48)
            pe.wait_ge(low_done, 2)
            for i in range(NPR):
                for half in range(2):
                    n = 2 * i + half
                    if n >= 4:
                        pe.wait_ge(lora_ev, n - 3)
                    rows = slice(64 * half, 64 * half + 64)
                    pe.matmul(psA[n % 4][:, :], w2[rows, i * P:(i + 1) * P], pr[rows, 12, :], start=True,
                              stop=True).then_inc(lora_mm, 1)
            for i in range(NPR):
                pe.wait_ge(sq_done, i + 1)
                if i >= 2:
                    pe.wait_ge(kk_root, i - 1)
                pe.matmul(psT[i % 2][:, :], tab[:, C_BLK:C_BLK + P], t2[:, :], start=True, stop=True).then_inc(sq_mm, 1)
                pe.wait_ge(prod_done, i + 1)
                for t in range(NT):
                    mm = pe.matmul(psB[:, t * 8 + 2 * i:t * 8 + 2 * i + 2], t3[:, t * P:(t + 1) * P],
                                   tab[:, C_HIND:C_HIND + 2], start=True, stop=True)
                mm.then_inc(bon_mm, 1)
            pe.wait_ge(lora_ev, 8)
            for t in range(NT):
                pe.matmul(psA[t][:, :], pr[:, 13, t * P:(t + 1) * P], g2[:, :], start=True, stop=True).then_inc(g_mm, 1)
            pe.wait_ge(fact_done, NPR)
            pe.wait_ge(kk_root, NPR)
            for n in range(3 * NT):
                src, t = divmod(n, NT)
                if n >= 2:
                    pe.wait_ge(t_ev, n - 1)
                for i in range(NPR):
                    x = (pr[:, 8 + i, :], KDT[:, i, :], BT[:, i, :])[src]
                    mm = pe.transpose(psT[n % 2][:, i * P:(i + 1) * P], x[:, t * P:(t + 1) * P], tab[:, C_IDENT:C_IDENT + P])
                mm.then_inc(t_done, 1)


def rwkv_chunks(nc, tab, KR, BT, KDT, U):
    NU = 32
    with Scope(nc, "rc") as s:
        ps = [s.ps(f"m{i}") for i in range(2)]
        mm_done, ev = s.sem("mm"), s.sem("ev")
        block = s.block()

        @block.tensor
        def _(pe):
            for u in range(NU):
                t, h = divmod(u, 8)
                i, hp = h // 2, 64 * (h % 2)
                if u >= 2:
                    pe.wait_ge(ev, u - 1)
                rhs = KR[hp:hp + 64, i, :, t * P:(t + 1) * P]
                pe.matmul(ps[u % 2][:, 0:256], BT[hp:hp + 64, i, t * P:(t + 1) * P], rhs, start=True, stop=True)
                pe.matmul(ps[u % 2][:, 256:512], KDT[hp:hp + 64, i, t * P:(t + 1) * P], rhs, start=True,
                          stop=True).then_inc(mm_done, 1)

        @block.vector
        def _(v):
            for u in range(NU):
                v.wait_ge(mm_done, u + 1)
                v.tensor_tensor(U[:, u, :], ps[u % 2][:, :], tab[:, C_UNIT:C_UNIT + 512], ALU.mult).then_inc(ev, 1)

    with Scope(nc, "ri") as s:
        G = 2
        NB = NU // 4
        X = [s.sb(f"x{i}", [P, 4, P]) for i in range(G)]
        XT = [s.sb(f"xt{i}", [P, 4, P]) for i in range(G)]
        LT = [s.sb(f"lt{i}", [P, 4, P]) for i in range(G)]
        Y = [s.sb(f"y{i}", [P, 4, P]) for i in range(G)]
        p1 = [s.ps(f"p1{i}") for i in range(G)]
        p2 = [s.ps(f"p2{i}") for i in range(G)]
        p3 = [s.ps(f"p3{i}") for i in range(G)]
        lt_done, m1, y_done, m2, x_done = ([s.sem(f"{k}{i}") for i in range(G)] for k in ("lt", "m1", "y", "m2", "x"))
        own = s.sem("own")
        block = s.block()
        steps = [(b, l) for r in range(NB // G) for l in range(LVL) for b in range(r * G, (r + 1) * G)]

        @block.gpsimd
        def _(pool):
            for b, l in steps:
                g = b % G
                n = (b // G) * LVL + l
                if n >= 1:
                    pool.wait_ge(m1[g], n)
                mask = tab[:, C_LVL + l * P:C_LVL + (l + 1) * P].unsqueeze(1).to_broadcast([P, 4, P])
                pool.tensor_tensor(LT[g][:, :, :], U[:, 4 * b:4 * b + 4, 0:P], mask, ALU.mult).then_inc(lt_done[g], 1)

        @block.tensor
        def _(pe):
            def first(b, l):
                g, n = b % G, (b // G) * LVL + l
                pe.wait_ge(lt_done[g], n + 1)
                pe.wait_ge(x_done[g], n + 1 + b // G)
                for j in range(4):
                    mm = pe.matmul(p1[g][:, j * P:(j + 1) * P], LT[g][:, j, :], X[g][:, j, :], start=True, stop=True)
                mm.then_inc(m1[g], 1)

            def second(b, l):
                g, n = b % G, (b // G) * LVL + l
                pe.wait_ge(y_done[g], n + 1)
                for j in range(4):
                    pe.matmul(p2[g][:, j * P:(j + 1) * P], XT[g][:, j, :], Y[g][:, j, :], start=True, stop=True)
                for j in range(4):
                    mm = pe.matmul(p3[g][:, j * P:(j + 1) * P], Y[g][:, j, :], XT[g][:, j, :], start=True, stop=True)
                mm.then_inc(m2[g], 1)

            for k in range(0, len(steps), G):
                for b, l in steps[k:k + G]:
                    first(b, l)
                for b, l in steps[k:k + G]:
                    second(b, l)

        @block.scalar
        def _(act):
            for b, l in steps:
                g, n = b % G, (b // G) * LVL + l
                act.wait_ge(m1[g], n + 1)
                act.activation(Y[g][:, :, :], p1[g][:, :].rearrange("p (j t) -> p j t", j=4), ACT.Copy).then_inc(y_done[g], 1)

        @block.vector
        def _(v):
            link = Chain(v, own)
            I4 = tab[:, C_IDENT:C_IDENT + P].unsqueeze(1).to_broadcast([P, 4, P])

            def start(b):
                g = b % G
                link(v.tensor_copy(X[g][:, :, :], I4))
                v.tensor_copy(XT[g][:, :, :], I4).then_inc(x_done[g], 1)

            for b in range(G):
                start(b)
            for b, l in steps:
                g, n = b % G, (b // G) * LVL + l
                v.wait_ge(m2[g], n + 1)
                v.wait_ge(x_done[g], n + 1 + b // G)
                d2, d3 = (q[g][:, :].rearrange("p (j t) -> p j t", j=4) for q in (p2, p3))
                if l < LVL - 1:
                    link(v.tensor_tensor(X[g][:, :, :], X[g][:, :, :], d2, ALU.subtract))
                    v.tensor_tensor(XT[g][:, :, :], XT[g][:, :, :], d3, ALU.subtract).then_inc(x_done[g], 1)
                else:
                    v.tensor_tensor(U[:, 4 * b:4 * b + 4, 0:P], XT[g][:, :, :], d3, ALU.subtract).then_inc(x_done[g], 1)
                    if b + G < NB:
                        start(b + G)


def rwkv_scan(nc, tab, U, KR, Vt, KDt, Bt, PC, y):
    PW = 2 * HD
    with Scope(nc, "rs") as s:
        ST = s.sb("state", [P, 4, PW])
        R = s.sb("R", [P, RW])
        Uc = [s.sb(f"U{i}", [P, RW]) for i in range(2)]
        Vc = [s.sb(f"V{i}", [P, RW]) for i in range(2)]
        PM = s.sb("PM", [P, 4, PW])
        tmp = s.sb("tmp", [P, 4, PW])
        psR, psU, psY, psS = (s.ps(k) for k in "RUYS")
        st_done, zeroed, v_ready, pm_ready, r_mm, r_ev, u_mm, u_ev, y_mm, y_ev, s_mm, own = (
            s.sem(k) for k in ("st", "zero", "vr", "pm", "rm", "re", "um", "ue", "ym", "ye", "sm", "own"))
        block = s.block()

        @block.gpsimd
        def _(pool):
            pool.wait_ge(zeroed, 5)
            for c in range(NCH):
                t, q = divmod(c, 2)
                rows = slice(64 * q, 64 * q + 64)
                if c >= 2:
                    pool.wait_ge(y_mm, c - 1)
                    pool.wait_ge(pm_ready, c)
                elif c:
                    pool.wait_ge(pm_ready, c)
                pool.tensor_copy(Vc[q][rows, :], Vt[rows, t, :]).then_inc(v_ready, 1)
                pool.wait_ge(v_ready, c + 1)
                if c >= 1:
                    pool.wait_ge(st_done, c + 1)
                pool.tensor_tensor(PM[:, :, :], tab[:, C_BLK:C_BLK + P].unsqueeze(1).to_broadcast([P, 4, PW]),
                                   PC[:, :, c:c + 1].to_broadcast([P, 4, PW]), ALU.mult).then_inc(pm_ready, 1)

        @block.tensor
        def _(pe):
            for c in range(NCH):
                t, q = divmod(c, 2)
                p0 = 64 * q
                ts = slice(c * CH, (c + 1) * CH)
                rows = slice(p0, p0 + 64)

                def unit(h, j):
                    return U[:, t * 8 + h, j * P + p0:j * P + p0 + 64]

                pe.wait_ge(st_done, c + 1)
                pe.wait_ge(v_ready, c + 1)
                if c:
                    pe.wait_ge(r_ev, c)
                for i in range(4):
                    pc = slice(i * PW, (i + 1) * PW)
                    pe.matmul(psR[rows, pc], KR[:, i, 0, ts], ST[:, i, :], start=True, stop=False)
                    for h in (2 * i, 2 * i + 1):
                        hc = slice(h * HD, (h + 1) * HD)
                        mm = pe.matmul(psR[rows, hc], unit(h, 2), Vc[q][:, hc], start=False, stop=(h % 2 == 1))
                mm.then_inc(r_mm, 1)
                pe.wait_ge(r_ev, c + 1)
                if c:
                    pe.wait_ge(u_ev, c)
                for h in range(8):
                    hc = slice(h * HD, (h + 1) * HD)
                    mm = pe.matmul(psU[rows, hc], unit(h, 0), R[:, hc], start=True, stop=True)
                mm.then_inc(u_mm, 1)
                pe.wait_ge(u_ev, c + 1)
                for i in range(4):
                    pc = slice(i * PW, (i + 1) * PW)
                    pe.matmul(psS[:, pc], KDt[:, t, pc], Vc[q][:, pc], start=True, stop=False)
                    mm = pe.matmul(psS[:, pc], Bt[:, t, pc], Uc[q][:, pc], start=False, stop=True)
                mm.then_inc(s_mm, 1)
                if c:
                    pe.wait_ge(y_ev, c)
                for i in range(4):
                    pc = slice(i * PW, (i + 1) * PW)
                    pe.matmul(psY[rows, pc], KR[:, i, 1, ts], ST[:, i, :], start=True, stop=False)
                    for h in (2 * i, 2 * i + 1):
                        hc = slice(h * HD, (h + 1) * HD)
                        pe.matmul(psY[rows, hc], unit(h, 3), Vc[q][:, hc], start=False, stop=False)
                        mm = pe.matmul(psY[rows, hc], unit(h, 1), Uc[q][:, hc], start=False, stop=(h % 2 == 1))
                mm.then_inc(y_mm, 1)

        @block.scalar
        def _(act):
            act.wait_ge(zeroed, 5)
            for c in range(NCH):
                t, q = divmod(c, 2)
                rows = slice(64 * q, 64 * q + 64)
                act.wait_ge(r_mm, c + 1)
                act.activation(R[rows, :], psR[rows, :], ACT.Copy).then_inc(r_ev, 1)
                act.wait_ge(y_mm, c + 1)
                act.activation(y[rows, t, :], psY[rows, :], ACT.Copy).then_inc(y_ev, 1)

        @block.vector
        def _(v):
            link = Chain(v, own)
            for z in (R, Uc[0], Uc[1], Vc[0], Vc[1]):
                v.memset(z[:, :], 0.0).then_inc(zeroed, 1)
            v.memset(ST[:, :, :], 0.0).then_inc(st_done, 1)
            v.wait_ge(st_done, 1)
            v.wait_ge(zeroed, 5)
            for c in range(NCH):
                q = c % 2
                rows = slice(64 * q, 64 * q + 64)
                v.wait_ge(u_mm, c + 1)
                v.tensor_copy(Uc[q][rows, :], psU[rows, :]).then_inc(u_ev, 1)
                v.wait_ge(s_mm, c + 1)
                link(v.tensor_tensor(tmp[:, :, :], psS[:, :].rearrange("p (i v) -> p i v", i=4), ST[:, :, :], ALU.add))
                v.wait_ge(y_mm, c + 1)
                v.wait_ge(pm_ready, c + 1)
                v.tensor_tensor(ST[:, :, :], tmp[:, :, :], PM[:, :, :], ALU.mult).then_inc(st_done, 1)
                v.wait_ge(st_done, c + 2)


def rwkv_finish(nc, tab, A, y, Vt, bonus, gate):
    with Scope(nc, "rf") as s:
        lw = s.sb("lnw", [P, RW])
        lb = s.sb("lnb", [P, RW])
        sq = s.sb("sq", [P, NT, RW])
        st = s.sb("st", [P, 3, NT * 8])
        ld, ss, root, own = (s.sem(k) for k in ("ld", "ss", "root", "own"))
        block = s.block()

        @block.sync
        def _(sp):
            sp.dma_start(lw[:, :], bc_row(A["rwkv_ln_w"], RW)).then_inc(ld, 16)
            sp.dma_start(lb[:, :], bc_row(A["rwkv_ln_b"], RW)).then_inc(ld, 16)

        @block.scalar
        def _(act):
            act.wait_ge(ss, 1)
            act.activation(st[:, 2, :], st[:, 1, :], ACT.Sqrt).then_inc(root, 1)

        @block.vector
        def _(v):
            link = Chain(v, own)
            y3 = y[:, :, :].rearrange("p t (h d) -> p (t h) d", d=HD)
            q3 = sq[:, :, :].rearrange("p t (h d) -> p (t h) d", d=HD)
            wide = [P, NT * 8, HD]
            link(v.tensor_reduce(st[:, 0, :], y3, AX.X, ALU.add))
            link(v.tensor_scalar(st[:, 0, :], st[:, 0, :], 1.0 / HD, None, ALU.mult))
            link(v.tensor_tensor(y3, y3, st[:, 0, :].unsqueeze(2).to_broadcast(wide), ALU.subtract))
            link(v.tensor_tensor(q3, y3, y3, ALU.mult))
            link(v.tensor_reduce(st[:, 1, :], q3, AX.X, ALU.add))
            link(v.tensor_scalar(st[:, 1, :], st[:, 1, :], 1.0 / HD, GN_EPS, ALU.mult, ALU.add))
            v.tensor_copy(st[0:1, 0, 0:1], st[0:1, 1, 0:1]).then_inc(ss, 1)
            v.wait_ge(root, 1)
            link(v.reciprocal(st[:, 1, :], st[:, 2, :]))
            link(v.tensor_tensor(y3, y3, st[:, 1, :].unsqueeze(2).to_broadcast(wide), ALU.mult))
            v.wait_ge(ld, 32)
            link(v.tensor_tensor(y[:, :, :], y[:, :, :], lw[:, :].unsqueeze(1).to_broadcast([P, NT, RW]), ALU.mult))
            link(v.tensor_tensor(y[:, :, :], y[:, :, :], lb[:, :].unsqueeze(1).to_broadcast([P, NT, RW]), ALU.add))
            v3 = Vt[:, :, :].rearrange("p t (h d) -> p (t h) d", d=HD)
            link(v.tensor_tensor(q3, v3, bonus[:, :].unsqueeze(2).to_broadcast(wide), ALU.mult))
            link(v.tensor_tensor(y[:, :, :], y[:, :, :], sq[:, :, :], ALU.add))
            link(v.tensor_tensor(y[:, :, :], y[:, :, :], gate[:, :, :], ALU.mult))


def route_phase(nc, name, tab, hT, nt, wg, bg, we, be, wts, slots, ovid, nov):
    NL = NG + NE
    with Scope(nc, name) as s:
        wr = s.sb("wr", [P, KD, NL])
        br = s.sb("br", [P, NL])
        L = s.sb("L", [P, nt, NL])
        G8 = s.sb("G8", [P, nt, 8])
        gm, em = s.sb("gm", [P, nt, 8]), s.sb("em", [P, nt, 8])
        gi, ei = s.sb("gi", [P, nt, 8], U32), s.sb("ei", [P, nt, 8], U32)
        gf, ef = s.sb("gf", [P, nt]), s.sb("ef", [P, nt, 2])
        goh = s.sb("goh", [P, nt, NG])
        ge = s.sb("ge", [P, nt, NG])
        gs = s.sb("gs", [P, nt])
        emk = s.sb("emk", [P, nt, NG, EPG])
        es = s.sb("es", [P, nt, EPG])
        e2 = s.sb("e2", [P, nt])
        oh = [s.sb(f"oh{k}", [P, nt, NE]) for k in range(2)]
        oh01 = s.sb("oh01", [P, nt, NE])
        cum = s.sb("cum", [P, nt, NE])
        z = s.sb("z", [P, nt, NE])
        cnt, nb, inc_, dlt = (s.sb(k, [P, NE]) for k in ("cnt", "nb", "inc", "dlt"))
        sf = s.sb("sf", [P, nt, 2])
        oc = s.sb("oc", [P, MAXOV, NE])
        of = s.sb("of", [P, MAXOV])
        nf = s.sb("nf", [P, 1])
        psL, psC = s.ps("L"), s.ps("C")
        ld, lg, ev, a_in, a_out, oh_done, c_mm, own = (s.sem(k) for k in ("ld", "lg", "ev", "ai", "ao", "oh", "cm", "own"))
        block = s.block()

        @block.sync
        def _(sp):
            sp.dma_start(wr[:, :, 0:NG], wg.rearrange("(k p) n -> p k n", p=P)).then_inc(ld, 16)
            sp.dma_start(wr[:, :, NG:NL], we.rearrange("(k p) n -> p k n", p=P)).then_inc(ld, 16)
            sp.dma_start(br[:, 0:NG], bc_row(bg, NG)).then_inc(ld, 16)
            sp.dma_start(br[:, NG:NL], bc_row(be, NE)).then_inc(ld, 16)

        @block.tensor
        def _(pe):
            pe.wait_ge(ld, 64)
            for t in range(nt):
                for k in range(KD):
                    mm = pe.matmul(psL[:, t * NL:(t + 1) * NL], hT[:, k, t * P:(t + 1) * P], wr[:, k, :],
                                   start=(k == 0), stop=(k == KD - 1))
            mm.then_inc(lg, 1)
            pe.wait_ge(oh_done, 1)
            for t in range(nt):
                for u in range(t + 1):
                    w = C_TRI if u == t else C_ONES
                    pe.matmul(psC[:, t * NE:(t + 1) * NE], tab[:, w:w + P], oh01[:, u, :], start=(u == 0), stop=(u == t))
            for u in range(nt):
                mm = pe.matmul(psC[:, nt * NE:(nt + 1) * NE], tab[:, C_ONES:C_ONES + P], oh01[:, u, :],
                               start=(u == 0), stop=(u == nt - 1))
            mm.then_inc(c_mm, 1)

        @block.scalar
        def _(act):
            act.wait_ge(a_in, 1)
            act.activation(ge[:, :, :], ge[:, :, :], ACT.Exp).then_inc(a_out, 1)
            act.wait_ge(a_in, 2)
            act.activation(e2[:, :], e2[:, :], ACT.Exp).then_inc(a_out, 1)

        @block.vector
        def _(v):
            link = Chain(v, own)
            io = tab[:, C_IO:C_IO + NE]
            link(v.memset(G8[:, :, :], NEG))
            v.wait_ge(lg, 1)
            v.wait_ge(ld, 64)
            link(v.tensor_tensor(L[:, :, :], psL[:, 0:nt * NL].rearrange("p (t n) -> p t n", n=NL),
                                 br[:, :].unsqueeze(1).to_broadcast([P, nt, NL]), ALU.add))
            link(v.tensor_copy(G8[:, :, 0:NG], L[:, :, 0:NG]))
            for t in range(nt):
                link(v.max(gm[:, t, :], G8[:, t, :]))
                link(v.max_index(gi[:, t, :], gm[:, t, :], G8[:, t, :]))
            link(v.tensor_copy(gf[:, :], gi[:, :, 0]))
            link(v.tensor_tensor(goh[:, :, :], io[:, 0:NG].unsqueeze(1).to_broadcast([P, nt, NG]),
                                 gf[:, :].unsqueeze(2).to_broadcast([P, nt, NG]), ALU.is_equal))
            v.tensor_tensor(ge[:, :, :], L[:, :, 0:NG], gm[:, :, 0:1].to_broadcast([P, nt, NG]),
                            ALU.subtract).then_inc(a_in, 1)
            for t in range(nt):
                link(v.tensor_tensor(emk[:, t, :, :], L[:, t, NG:NL].rearrange("p (g j) -> p g j", j=EPG),
                                     goh[:, t, :].unsqueeze(2).to_broadcast([P, NG, EPG]), ALU.mult))
                link(v.tensor_reduce(es[:, t, :], emk[:, t, :, :].rearrange("p g j -> p j g"), AX.X, ALU.add))
                link(v.max(em[:, t, :], es[:, t, :]))
                link(v.max_index(ei[:, t, :], em[:, t, :], es[:, t, :]))
            v.tensor_tensor(e2[:, :], em[:, :, 1], em[:, :, 0], ALU.subtract).then_inc(a_in, 1)
            link(v.tensor_copy(ef[:, :, :], ei[:, :, 0:2]))
            link(v.scalar_tensor_tensor(out=ef[:, :, :], in0=gf[:, :].unsqueeze(2).to_broadcast([P, nt, 2]), scalar=float(EPG),
                                        in1=ef[:, :, :], op0=ALU.mult, op1=ALU.add))
            for k in range(2):
                link(v.tensor_tensor(oh[k][:, :, :], io.unsqueeze(1).to_broadcast([P, nt, NE]),
                                     ef[:, :, k:k + 1].to_broadcast([P, nt, NE]), ALU.is_equal))
            v.tensor_tensor(oh01[:, :, :], oh[0][:, :, :], oh[1][:, :, :], ALU.add).then_inc(oh_done, 1)
            v.wait_ge(a_out, 2)
            link(v.tensor_reduce(gs[:, :], ge[:, :, :], AX.X, ALU.add))
            link(v.scalar_tensor_tensor(out=gs[:, :], in0=e2[:, :], scalar=1.0, in1=gs[:, :], op0=ALU.add, op1=ALU.mult))
            link(v.reciprocal(wts[:, :, 0], gs[:, :]))
            link(v.tensor_tensor(wts[:, :, 1], wts[:, :, 0], e2[:, :], ALU.mult))
            v.wait_ge(c_mm, 1)
            link(v.tensor_copy(cum[:, :, :], psC[:, 0:nt * NE].rearrange("p (t e) -> p t e", e=NE)))
            link(v.tensor_copy(cnt[:, :], psC[:, nt * NE:(nt + 1) * NE]))
            link(v.tensor_scalar(nb[:, :], cnt[:, :], float(P), None, ALU.is_gt))
            for m in range(2, nt):
                link(v.scalar_tensor_tensor(out=nb[:, :], in0=cnt[:, :], scalar=float(m * P), in1=nb[:, :],
                                            op0=ALU.is_gt, op1=ALU.add))
            link(v.tensor_tensor_scan(inc_[:, :], tab[:, C_ONES:C_ONES + NE], nb[:, :], 0.0, ALU.mult, ALU.add))
            link(v.tensor_tensor(dlt[:, :], inc_[:, :], nb[:, :], ALU.subtract))
            link(v.tensor_tensor(dlt[:, :], dlt[:, :], io, ALU.subtract))
            link(v.tensor_scalar(dlt[:, :], dlt[:, :], float(NE - 1), float(P), ALU.add, ALU.mult))
            link(v.tensor_scalar(z[:, :, :], cum[:, :, :], float(P), None, ALU.is_ge))
            link(v.tensor_tensor(z[:, :, :], z[:, :, :], dlt[:, :].unsqueeze(1).to_broadcast([P, nt, NE]), ALU.mult))
            link(v.tensor_tensor(z[:, :, :], z[:, :, :], cum[:, :, :], ALU.add))
            link(v.scalar_tensor_tensor(out=z[:, :, :], in0=io.unsqueeze(1).to_broadcast([P, nt, NE]), scalar=float(P),
                                        in1=z[:, :, :], op0=ALU.mult, op1=ALU.add))
            for k in range(2):
                link(v.tensor_tensor(oh[k][:, :, :], oh[k][:, :, :], z[:, :, :], ALU.mult))
                link(v.tensor_reduce(sf[:, :, k], oh[k][:, :, :], AX.X, ALU.add))
            link(v.tensor_copy(slots[:, :, :], sf[:, :, :]))
            jj = tab[:, C_IO:C_IO + MAXOV].unsqueeze(2).to_broadcast([P, MAXOV, NE])
            link(v.tensor_tensor(oc[:, :, :], inc_[:, :].unsqueeze(1).to_broadcast([P, MAXOV, NE]), jj, ALU.is_le))
            link(v.tensor_reduce(of[:, :], oc[:, :, :], AX.X, ALU.add))
            link(v.tensor_scalar(of[:, :], of[:, :], float(NE - 1), None, ALU.min))
            link(v.tensor_copy(ovid[:, :], of[:, :]))
            link(v.tensor_copy(nf[:, :], inc_[:, NE - 1:NE]))
            link(v.tensor_copy(nov[:, :], nf[:, :]))


def scatter_phase(nc, name, htok, nt, slots, xbuf):
    with Scope(nc, name) as s:
        sent = s.sem("sent")
        block = s.block()

        @block.gpsimd
        def _(pool):
            for t in range(nt):
                for k in range(2):
                    pool.indirect_dma_start(out=xbuf, out_offset=bass.IndirectOffsetOnAxis(ap=slots[:, t, k:k + 1], axis=0),
                                            in_=htok[:, t, :], in_offset=None).then_inc(sent, 16)
            pool.wait_ge(sent, 32 * nt)


def experts_phase(nc, name, tab, w1d, w3d, w2d, xbuf, ybuf, ovid, nov):
    R1 = w1d.rearrange("e (k p) n -> e p k n", p=P)
    R3 = w3d.rearrange("e (k p) n -> e p k n", p=P)
    R2 = w2d.rearrange("e (k p) n -> e p k n", p=P)
    xb = xbuf.rearrange("(b p) d -> b p d", p=P)
    yb = ybuf.rearrange("(b p) d -> b p d", p=P)
    ident = tab[:, C_IDENT:C_IDENT + P]
    with Scope(nc, name) as s:
        W1 = [s.sb(f"w1{i}", [P, KD, FF]) for i in range(2)]
        W3 = [s.sb(f"w3{i}", [P, KD, FF]) for i in range(2)]
        W2 = [s.sb(f"w2{i}", [P, KF, D]) for i in range(2)]
        xin = s.sb("xin", [P, D])
        xT = s.sb("xT", [P, D])
        sg = s.sb("sig", [P, FF])
        h = s.sb("h", [P, FF])
        hT = s.sb("hT", [P, FF])
        y = s.sb("y", [P, D])
        pg, pu, ph = s.ps("gate"), s.ps("up"), s.ps("hT")
        px, py = s.ps("xT", 2), s.ps("y", 2)
        w1_in, w3_in, w2_in = ([s.sem(f"{k}{i}") for i in range(2)] for k in ("w1", "w3", "w2"))
        x_in, xt_done, xt_a, xt_v, gu_done, sig_done, h_done = (
            s.sem(k) for k in ("xin", "xt", "xta", "xtv", "gu", "sig", "h"))
        ht_done, ht_ev, dn_done, y_a, y_v, y_out = (s.sem(k) for k in ("ht", "hte", "dn", "ya", "yv", "yo"))
        sil_own = s.sem("silown")

        def turn_x(pe):
            for k in range(KD):
                mm = pe.transpose(px[:, k * P:(k + 1) * P], xin[:, k * P:(k + 1) * P], ident)
            return mm

        def gate_up(pe, q, w3_wait):
            for k in range(KD):
                pe.matmul(pg[:, :], xT[:, k * P:(k + 1) * P], W1[q][:, k, :], start=(k == 0), stop=(k == KD - 1))
            w3_wait()
            for k in range(KD):
                mm = pe.matmul(pu[:, :], xT[:, k * P:(k + 1) * P], W3[q][:, k, :], start=(k == 0), stop=(k == KD - 1))
            return mm

        def turn_h(pe):
            for k in range(KF):
                mm = pe.transpose(ph[:, k * P:(k + 1) * P], h[:, k * P:(k + 1) * P], ident)
            return mm

        def down(pe, q):
            for half in range(2):
                for k in range(KF):
                    mm = pe.matmul(py[:, half * 512:(half + 1) * 512], hT[:, k * P:(k + 1) * P],
                                   W2[q][:, k, half * 512:(half + 1) * 512], start=(k == 0), stop=(k == KF - 1))
            return mm

        block = s.block()
        PAIRS = NE // 2

        @block.sync
        def _(sp):
            for q in range(2):
                if q:
                    sp.wait_ge(xt_done, q)
                sp.dma_start(xin[:, :], xb[q]).then_inc(x_in, 16)
                sp.dma_start(W1[q][:, :, :], R1[q]).then_inc(w1_in[q], 16)
                sp.dma_start(W3[q][:, :, :], R3[q]).then_inc(w3_in[q], 16)
                sp.dma_start(W2[q][:, :, :], R2[q]).then_inc(w2_in[q], 16)

            def hold(sem, value):
                sp.wait_ge(sem, value)
                sp.wait_ge(sem, 1)

            with sp.Fori(1, PAIRS) as i:
                for q in range(2):
                    e = sp.snap(2 * i + q)
                    freed = sp.snap(2 * i - 1 + q)
                    hold(xt_done, e)
                    sp.dma_start(xin[:, :], xb[bass.ds(e, 1), :, :].rearrange("b p d -> p (b d)")).then_inc(x_in, 16)
                    hold(gu_done, freed)
                    sp.dma_start(W1[q][:, :, :], R1[bass.ds(e, 1), :, :, :].rearrange("e p k n -> p (e k) n")).then_inc(w1_in[q], 16)
                    sp.dma_start(W3[q][:, :, :], R3[bass.ds(e, 1), :, :, :].rearrange("e p k n -> p (e k) n")).then_inc(w3_in[q], 16)
                    hold(dn_done, freed)
                    sp.dma_start(W2[q][:, :, :], R2[bass.ds(e, 1), :, :, :].rearrange("e p k n -> p (e k) n")).then_inc(w2_in[q], 16)

        @block.tensor
        def _(pe):
            def body(i, q, first, last):
                pe.wait_ge(xt_a, 2 * i + q + 1)
                pe.wait_ge(xt_v, 2 * i + q + 1)
                pe.wait_ge(w1_in[q], 16 * i + 16)
                if not first:
                    pe.wait_ge(h_done, 2 * i + q)
                gate_up(pe, q, lambda: pe.wait_ge(w3_in[q], 16 * i + 16)).then_inc(gu_done, 1)
                if not last:
                    pe.wait_ge(x_in, 32 * i + 16 * q + 32)
                    turn_x(pe).then_inc(xt_done, 1)
                if not first:
                    lower(i, q)
                pe.wait_ge(h_done, 2 * i + q + 1)
                turn_h(pe).then_inc(ht_done, 1)

            def lower(i, q):
                pe.wait_ge(ht_ev, 2 * i + q)
                pe.wait_ge(w2_in[1 - q], 16 * i + 16 * q)
                if not (isinstance(i, int) and 2 * i + q == 1):
                    pe.wait_ge(y_v, 2 * i + q - 1)
                down(pe, 1 - q).then_inc(dn_done, 1)

            pe.wait_ge(x_in, 16)
            turn_x(pe).then_inc(xt_done, 1)
            body(0, 0, True, False)
            body(0, 1, False, False)
            with pe.Fori(1, PAIRS - 1) as i:
                body(i, 0, False, False)
                body(i, 1, False, False)
            body(PAIRS - 1, 0, False, False)
            body(PAIRS - 1, 1, False, True)
            lower(PAIRS, 0)

        @block.scalar
        def _(act):
            def take_x(n):
                act.wait_ge(xt_done, n)
                act.activation(xT[:, 0:512], px[:, 0:512], ACT.Copy).then_inc(xt_a, 1)

            def store(n, b):
                act.wait_ge(dn_done, n)
                act.activation(y[:, 512:1024], py[:, 512:1024], ACT.Copy).then_inc(y_a, 1)
                act.wait_ge(y_a, n)
                act.wait_ge(y_v, n)
                act.dma_start(b, y[:, :]).then_inc(y_out, 16)

            def body(i, q, first, last):
                act.wait_ge(gu_done, 2 * i + q + 1)
                act.activation(sg[:, :], pg[:, :], ACT.Silu).then_inc(sig_done, 1)
                if not last:
                    take_x(2 * i + q + 2)
                if not first:
                    lower(i, q)
                act.wait_ge(ht_done, 2 * i + q + 1)
                act.activation(hT[:, :], ph[:, :], ACT.Copy).then_inc(ht_ev, 1)

            def lower(i, q):
                if isinstance(i, int):
                    dst = yb[2 * i + q - 1]
                    if 2 * i + q - 1 > 0:
                        act.wait_ge(y_out, 16 * (2 * i + q - 1))
                else:
                    b = act.snap(2 * i + q - 1)
                    need = act.snap(16 * (2 * i + q - 1))
                    act.wait_ge(y_out, need)
                    dst = yb[bass.ds(b, 1), :, :].rearrange("b p d -> p (b d)")
                store(2 * i + q, dst)

            take_x(1)
            body(0, 0, True, False)
            body(0, 1, False, False)
            with act.Fori(1, PAIRS - 1) as i:
                body(i, 0, False, False)
                body(i, 1, False, False)
            body(PAIRS - 1, 0, False, False)
            body(PAIRS - 1, 1, False, True)
            lower(PAIRS, 0)
            act.wait_ge(y_out, 16 * NE)

        @block.vector
        def _(v):
            def take_x(n):
                v.wait_ge(xt_done, n)
                v.tensor_copy(xT[:, 512:1024], px[:, 512:1024]).then_inc(xt_v, 1)

            def body(i, q, first, last):
                v.wait_ge(sig_done, 2 * i + q + 1)
                v.tensor_tensor(h[:, :], sg[:, :], pu[:, :], ALU.mult).then_inc(h_done, 1)
                if not last:
                    take_x(2 * i + q + 2)
                if not first:
                    lower(i, q)

            def lower(i, q):
                v.wait_ge(dn_done, 2 * i + q)
                if isinstance(i, int):
                    if 2 * i + q - 1 > 0:
                        v.wait_ge(y_out, 16 * (2 * i + q - 1))
                else:
                    v.wait_ge(y_out, 16 * (2 * i + q - 1))
                v.tensor_copy(y[:, 0:512], py[:, 0:512]).then_inc(y_v, 1)

            take_x(1)
            body(0, 0, True, False)
            body(0, 1, False, False)
            with v.Fori(1, PAIRS - 1) as i:
                body(i, 0, False, False)
                body(i, 1, False, False)
            body(PAIRS - 1, 0, False, False)
            body(PAIRS - 1, 1, False, True)
            lower(PAIRS, 0)

    with Scope(nc, name + "o") as s:
        W1, W3 = s.sb("w1", [P, KD, FF]), s.sb("w3", [P, KD, FF])
        W2 = s.sb("w2", [P, KF, D])
        xin, xT, y = (s.sb(k, [P, D]) for k in ("xin", "xT", "y"))
        sg, h, hT = (s.sb(k, [P, FF]) for k in ("sig", "h", "hT"))
        pg, pu, ph = s.ps("gate"), s.ps("up"), s.ps("hT")
        px, py = s.ps("xT", 2), s.ps("y", 2)
        w_in, xt, xta, gu, sig, hd, ht, hte, dn, ye, yo = (
            s.sem(k) for k in ("w", "xt", "xta", "gu", "sig", "hd", "ht", "hte", "dn", "ye", "yo"))
        block = s.block()

        @block.sync
        def _(sp):
            n = sp.value_load(nov[0:1, 0:1], min_val=0, max_val=MAXOV)
            with sp.If(n > 0):
                with sp.Fori(0, n) as j:
                    e = sp.value_load(ovid[0:1, bass.ds(j, 1)], min_val=0, max_val=NE - 1)
                    b = sp.snap(j + NE)
                    free = sp.snap(j + 1)
                    sp.wait_ge(dn, free)
                    sp.wait_ge(dn, 1)
                    sp.dma_start(xin[:, :], xb[bass.ds(b, 1), :, :].rearrange("b p d -> p (b d)")).then_inc(w_in, 16)
                    sp.dma_start(W1[:, :, :], R1[bass.ds(e, 1), :, :, :].rearrange("e p k n -> p (e k) n")).then_inc(w_in, 16)
                    sp.dma_start(W3[:, :, :], R3[bass.ds(e, 1), :, :, :].rearrange("e p k n -> p (e k) n")).then_inc(w_in, 16)
                    sp.dma_start(W2[:, :, :], R2[bass.ds(e, 1), :, :, :].rearrange("e p k n -> p (e k) n")).then_inc(w_in, 16)

        @block.tensor
        def _(pe):
            n = pe.value_load(nov[0:1, 0:1], min_val=0, max_val=MAXOV)
            with pe.If(n > 0):
                with pe.Fori(0, n) as j:
                    pe.wait_ge(w_in, 64 * j + 64)
                    for k in range(KD):
                        mm = pe.transpose(px[:, k * P:(k + 1) * P], xin[:, k * P:(k + 1) * P], ident)
                    mm.then_inc(xt, 1)
                    pe.wait_ge(xta, j + 1)
                    for ps, w in ((pg, W1), (pu, W3)):
                        for k in range(KD):
                            mm = pe.matmul(ps[:, :], xT[:, k * P:(k + 1) * P], w[:, k, :], start=(k == 0), stop=(k == KD - 1))
                    mm.then_inc(gu, 1)
                    pe.wait_ge(hd, j + 1)
                    for k in range(KF):
                        mm = pe.transpose(ph[:, k * P:(k + 1) * P], h[:, k * P:(k + 1) * P], ident)
                    mm.then_inc(ht, 1)
                    pe.wait_ge(hte, j + 1)
                    for half in range(2):
                        for k in range(KF):
                            mm = pe.matmul(py[:, half * 512:(half + 1) * 512], hT[:, k * P:(k + 1) * P],
                                           W2[:, k, half * 512:(half + 1) * 512], start=(k == 0), stop=(k == KF - 1))
                    mm.then_inc(dn, 1)

        @block.scalar
        def _(act):
            n = act.value_load(nov[0:1, 0:1], min_val=0, max_val=MAXOV)
            with act.If(n > 0):
                with act.Fori(0, n) as j:
                    b = act.snap(j + NE)
                    act.wait_ge(gu, j + 1)
                    act.activation(sg[:, :], pg[:, :], ACT.Silu).then_inc(sig, 1)
                    act.wait_ge(ye, j + 1)
                    act.dma_start(yb[bass.ds(b, 1), :, :].rearrange("b p d -> p (b d)"), y[:, :]).then_inc(yo, 16)

        @block.vector
        def _(v):
            v.memset(y[:, 0:1], 0.0).then_inc(dn, 1)
            n = v.value_load(nov[0:1, 0:1], min_val=0, max_val=MAXOV)
            with v.If(n > 0):
                with v.Fori(0, n) as j:
                    v.wait_ge(xt, j + 1)
                    v.tensor_copy(xT[:, :], px[:, :]).then_inc(xta, 1)
                    v.wait_ge(sig, j + 1)
                    v.tensor_tensor(h[:, :], sg[:, :], pu[:, :], ALU.mult).then_inc(hd, 1)
                    v.wait_ge(ht, j + 1)
                    v.tensor_copy(hT[:, :], ph[:, :]).then_inc(hte, 1)
                    v.wait_ge(dn, j + 2)
                    v.tensor_copy(y[:, :], py[:, :]).then_inc(ye, 1)
                    v.wait_ge(yo, 16 * j + 16)


def combine_phase(nc, name, xs, slots, wts, ybuf, gates=None):
    n = len(xs)
    with Scope(nc, name) as s:
        Y = [[s.sb(f"y{i}{k}", [P, D]) for k in range(2)] for i in range(2)]
        acc = s.sb("acc", [P, D])
        rows = []
        for g in gates or []:
            if not any(g is r for r in rows):
                rows.append(g)
        G = [s.sb(f"g{i}", [P, D]) for i in range(len(rows))]
        y_in = [[s.sem(f"y{i}{k}") for k in range(2)] for i in range(2)]
        g_in, used, own = s.sem("g"), s.sem("used"), s.sem("own")
        block = s.block()

        @block.sync
        def _(sp):
            for i, r in enumerate(rows):
                sp.dma_start(G[i][:, :], bc_row(r, D)).then_inc(g_in, 16)

        @block.gpsimd
        def _(pool):
            for t in range(n):
                if t >= 2:
                    pool.wait_ge(used, t - 1)
                for k in range(2):
                    pool.indirect_dma_start(out=Y[t % 2][k][:, :], out_offset=None, in_=ybuf,
                                            in_offset=bass.IndirectOffsetOnAxis(ap=slots[:, t, k:k + 1], axis=0)
                                            ).then_inc(y_in[t % 2][k], 16)

        @block.vector
        def _(v):
            link = Chain(v, own)
            if rows:
                v.wait_ge(g_in, 16 * len(rows))
            for t in range(n):
                for k in range(2):
                    v.wait_ge(y_in[t % 2][k], 16 * (t // 2 + 1))
                y0, y1 = Y[t % 2]
                if t:
                    v.wait_ge(used, t)
                link(v.tensor_scalar(acc[:, :], y0[:, :], wts[:, t, 0:1], None, ALU.mult))
                if rows:
                    link(v.scalar_tensor_tensor(out=acc[:, :], in0=y1[:, :], scalar=wts[:, t, 1:2], in1=acc[:, :],
                                                op0=ALU.mult, op1=ALU.add))
                    i = [k for k, r in enumerate(rows) if r is gates[t]][0]
                    link(v.tensor_tensor(acc[:, :], acc[:, :], G[i][:, :], ALU.mult))
                    v.tensor_tensor(xs[t], xs[t], acc[:, :], ALU.add).then_inc(used, 1)
                else:
                    link(v.scalar_tensor_tensor(out=acc[:, :], in0=y1[:, :], scalar=wts[:, t, 1:2], in1=acc[:, :],
                                                op0=ALU.mult, op1=ALU.add))
                    v.tensor_tensor(xs[t], xs[t], acc[:, :], ALU.add).then_inc(used, 1)


def moe(nc, name, tab, xs, gain, mods, gates, wg, bg, we, be, w1, w3, w2, xbuf, ybuf):
    n = len(xs)
    with Scope(nc, name) as o:
        wts, slots = o.sb("wts", [P, n, 2]), o.sb("slots", [P, n, 2], I32)
        ovid, nov = o.sb("ovid", [P, MAXOV], I32), o.sb("nov", [P, 1], I32)
        with Scope(nc, name + "h") as s:
            htok = s.sb("tok", [P, n, D])
            hT = s.sb("T", [P, KD, n * P])
            norm_phase(nc, name + "n", xs, tab, gain, hT=hT, htok=htok, mods=mods)
            route_phase(nc, name + "r", tab, hT, n, wg, bg, we, be, wts, slots, ovid, nov)
            scatter_phase(nc, name + "s", htok, n, slots, xbuf)
        experts_phase(nc, name + "e", tab, w1, w3, w2, xbuf, ybuf, ovid, nov)
        combine_phase(nc, name + "c", xs, slots, wts, ybuf, gates)


def modulation_phase(nc, tab, c, cc, w, b, modD):
    L, N = b.shape
    CHN = N // 512
    RING = 4
    with Scope(nc, "ada") as s:
        cT = s.sb("cT", [P, KD, 2])
        sT = s.sb("sT", [P, KD, 2])
        br = s.sb("b", [2, L, N])
        row = s.sb("row", [2, L, N])
        W = [s.sb(f"w{i}", [P, KD, 512]) for i in range(RING)]
        ps = [s.ps(f"acc{i}") for i in range(4)]
        c_in, b_in, sil, mm_done, ev, out = (s.sem(k) for k in ("c", "b", "sil", "mm", "ev", "out"))
        w_in = [s.sem(f"w{i}") for i in range(RING)]
        block = s.block()

        @block.sync
        def _(sp):
            with nc.allow_non_contiguous_dma("1024 numbers, once"):
                sp.dma_start(cT[:, :, 0], c.rearrange("(k p) -> p k", p=P)).then_inc(c_in, 16)
                sp.dma_start(cT[:, :, 1], cc.rearrange("(k p) -> p k", p=P)).then_inc(c_in, 16)
            for n in range(L * CHN):
                l, j = divmod(n, CHN)
                if n >= RING:
                    sp.wait_ge(mm_done, n - RING + 1)
                sp.dma_start(W[n % RING][:, :, :], w[l, :, j * 512:(j + 1) * 512].rearrange("(k p) n -> p k n", p=P)
                             ).then_inc(w_in[n % RING], 16)
                if n == 0:
                    for l2 in range(L):
                        sp.dma_start(br[:, l2, :], b[l2].rearrange("(a n) -> a n", a=1).to_broadcast([2, N])).then_inc(b_in, 16)
            for l in range(L):
                sp.wait_ge(ev, CHN * (l + 1))
                sp.dma_start(modD[l], row[:, l, :]).then_inc(out, 16)
            sp.wait_ge(out, 16 * L)

        @block.scalar
        def _(act):
            act.wait_ge(c_in, 32)
            act.activation(sT[:, :, :], cT[:, :, :], ACT.Silu).then_inc(sil, 1)

        @block.tensor
        def _(pe):
            pe.wait_ge(sil, 1)
            for n in range(L * CHN):
                pe.wait_ge(w_in[n % RING], 16 * (n // RING + 1))
                if n >= 4:
                    pe.wait_ge(ev, n - 3)
                for k in range(KD):
                    mm = pe.matmul(ps[n % 4][0:2, :], sT[:, k, :], W[n % RING][:, k, :], start=(k == 0), stop=(k == KD - 1))
                mm.then_inc(mm_done, 1)

        @block.vector
        def _(v):
            v.wait_ge(b_in, 16 * L)
            for n in range(L * CHN):
                l, j = divmod(n, CHN)
                v.wait_ge(mm_done, n + 1)
                v.tensor_tensor(row[:, l, j * 512:(j + 1) * 512], ps[n % 4][0:2, :], br[:, l, j * 512:(j + 1) * 512],
                                ALU.add).then_inc(ev, 1)


def clear_phase(nc, tab, xbuf, ybuf, na, relpad):
    with Scope(nc, "clr") as s:
        z = s.sb("z", [P, 4, D])
        rp = s.sb("rp", [120, 2, 128])
        zd, rin, out = s.sem("zd"), s.sem("rin"), s.sem("out")
        block = s.block()
        rel = na.rearrange("h r c -> (h r) c")

        @block.vector
        def _(v):
            v.memset(rp[:, :, :], 0.0).then_inc(zd, 1)
            v.memset(z[:, :, :], 0.0).then_inc(zd, 1)

        @block.sync
        def _(sp):
            sp.wait_ge(zd, 2)
            for i in range(2):
                sp.dma_start(rp[:, i, 48:79], rel[i * 120:(i + 1) * 120, :]).then_inc(rin, 16)
            for i in range(SLOTS // 512):
                sp.dma_start(xbuf[i * 512:(i + 1) * 512, :].rearrange("(p j) d -> p j d", j=4), z[:, :, :]).then_inc(out, 16)
            for i in range(MAXOV * P // 512):
                r0 = NE * P + i * 512
                sp.dma_start(ybuf[r0:r0 + 512, :].rearrange("(p j) d -> p j d", j=4), z[:, :, :]).then_inc(out, 16)
            sp.wait_ge(rin, 32)
            for i in range(2):
                sp.dma_start(relpad[i * 120:(i + 1) * 120, :].rearrange("r (c n) -> r c n", n=P),
                             rp[:, i, :].unsqueeze(1).to_broadcast([120, HD, P])).then_inc(out, 16)
            sp.wait_ge(out, 16 * (SLOTS // 512 + MAXOV * P // 512 + 2))


def pool_phase(nc, name, band, pw, pscale, u, nt, dst):
    T = nt * P
    with Scope(nc, name) as s:
        bd = [s.sb(f"band{i}", [P, nt, T]) for i in range(2)]
        w = s.sb("w", [P, 4, P])
        sc = s.sb("sc", [P, 4])
        pl = [s.sb(f"pl{i}", [P, T]) for i in range(2)]
        ps1, ps2 = [s.ps(f"a{i}") for i in range(2)], [s.ps(f"b{i}") for i in range(2)]
        b_in, w_in = [s.sem(f"b{i}") for i in range(2)], s.sem("w")
        m1, ev1, m2, ev2 = (s.sem(k) for k in ("m1", "e1", "m2", "e2"))
        block = s.block()

        @block.sync
        def _(sp):
            sp.dma_start(w[:, :, :], pw.rearrange("g c d -> c g d")).then_inc(w_in, 16)
            with nc.allow_non_contiguous_dma("512 numbers, once"):
                sp.dma_start(sc[:, :], pscale.rearrange("(g p) -> p g", p=P)).then_inc(w_in, 16)
            for g in range(4):
                if g >= 2:
                    sp.wait_ge(m1, g - 1)
                sp.dma_start(bd[g % 2][:, :, :], band[g].rearrange("(t p) n -> p t n", p=P)).then_inc(b_in[g % 2], 16)

        @block.tensor
        def _(pe):
            def mix(g):
                pe.wait_ge(ev1, g + 1)
                if g >= 2:
                    pe.wait_ge(ev2, g - 1)
                pe.matmul(ps2[g % 2][:, 0:T], w[:, g, :], pl[g % 2][:, :], start=True, stop=True).then_inc(m2, 1)

            pe.wait_ge(w_in, 32)
            for g in range(4):
                pe.wait_ge(b_in[g % 2], 16 * (g // 2 + 1))
                if g >= 2:
                    pe.wait_ge(ev1, g - 1)
                for t in range(nt):
                    mm = pe.matmul(ps1[g % 2][:, 0:T], u(t)[:, g * P:(g + 1) * P], bd[g % 2][:, t, :], start=(t == 0), stop=(t == nt - 1))
                mm.then_inc(m1, 1)
                if g >= 1:
                    mix(g - 1)
            mix(3)

        @block.vector
        def _(v):
            def second(g):
                v.wait_ge(m2, g + 1)
                v.tensor_scalar(dst[:, g, :], ps2[g % 2][:, 0:T], sc[:, g:g + 1], None, ALU.mult).then_inc(ev2, 1)

            v.wait_ge(w_in, 32)
            for g in range(4):
                v.wait_ge(m1, g + 1)
                if g >= 2:
                    v.wait_ge(m2, g - 1)
                v.tensor_copy(pl[g % 2][:, :], ps1[g % 2][:, 0:T]).then_inc(ev1, 1)
                if g >= 1:
                    second(g - 1)
            second(3)


def load_phase(nc, name, pairs):
    with Scope(nc, name) as s:
        done = s.sem("in")
        block = s.block()

        @block.sync
        def _(sp):
            with nc.allow_non_contiguous_dma("parameters"):
                for d, r in pairs:
                    sp.dma_start(d, r).then_inc(done, 16)
            sp.wait_ge(done, 16 * len(pairs))


def lambda_phase(nc, A, nlam, lam_init):
    with Scope(nc, "lam") as s:
        r = s.sb("r", [P, 4, HD])
        d = s.sb("d", [P, 2])
        pr = s.sb("p", [P, 2, HD])
        ld, dd, ee, own = (s.sem(k) for k in ("ld", "dd", "ee", "own"))
        block = s.block()

        @block.sync
        def _(sp):
            for i, n in enumerate(("lambda_q1", "lambda_k1", "lambda_q2", "lambda_k2")):
                sp.dma_start(r[:, i, :], bc_row(A[n], HD)).then_inc(ld, 16)

        @block.vector
        def _(v):
            link = Chain(v, own)
            v.wait_ge(ld, 64)
            link(v.tensor_tensor(pr[:, 0, :], r[:, 0, :], r[:, 1, :], ALU.mult))
            link(v.tensor_tensor(pr[:, 1, :], r[:, 2, :], r[:, 3, :], ALU.mult))
            v.tensor_reduce(d[:, :], pr[:, :, :], AX.X, ALU.add).then_inc(dd, 1)
            v.wait_ge(ee, 1)
            link(v.tensor_tensor(nlam[:, :], d[:, 1:2], d[:, 0:1], ALU.subtract))
            link(v.tensor_scalar(nlam[:, :], nlam[:, :], -lam_init, None, ALU.add))

        @block.scalar
        def _(act):
            act.wait_ge(dd, 1)
            act.activation(d[:, :], d[:, :], ACT.Exp).then_inc(ee, 1)


def subln_phase(nc, tab, o, w, factor):
    n = NT * 4
    with Scope(nc, "sub") as s:
        g = s.sb("g", [P, P])
        sq = s.sb("sq", [P, n, P])
        st = s.sb("st", [P, 2, n])
        ld, ms, rt, own = (s.sem(k) for k in ("ld", "ms", "rt", "own"))
        block = s.block()
        o3 = o[:, :, :].rearrange("p t (h d) -> p (t h) d", d=P)

        @block.sync
        def _(sp):
            sp.dma_start(g[:, :], bc_row(w, P)).then_inc(ld, 16)

        @block.scalar
        def _(act):
            act.wait_ge(ms, 1)
            act.activation(st[:, 1, :], st[:, 0, :], ACT.Sqrt).then_inc(rt, 1)

        @block.vector
        def _(v):
            link = Chain(v, own)
            link(v.tensor_tensor(sq[:, :, :], o3, o3, ALU.mult))
            link(v.tensor_reduce(st[:, 0, :], sq[:, :, :], AX.X, ALU.add))
            v.tensor_scalar(st[:, 0, :], st[:, 0, :], 1.0 / P, EPS, ALU.mult, ALU.add).then_inc(ms, 1)
            v.wait_ge(rt, 1)
            link(v.reciprocal(st[:, 0, :], st[:, 1, :]))
            link(v.tensor_tensor(o3, o3, st[:, 0, :].unsqueeze(2).to_broadcast([P, n, P]), ALU.mult))
            v.wait_ge(ld, 16)
            link(v.tensor_scalar(g[:, :], g[:, :], factor, None, ALU.mult))
            link(v.tensor_tensor(o3, o3, g[:, :].unsqueeze(1).to_broadcast([P, n, P]), ALU.mult))


def copy_evac(dst):
    def evac(eng, link, ps, t, c):
        return eng.tensor_copy(dst(t, c), ps)
    return evac


def add_evac(xs):
    def evac(v, link, ps, t, c):
        x = xs[t][:, c * 512:(c + 1) * 512]
        return v.tensor_tensor(x, x, ps, ALU.add)
    return evac


def first_mixer(nc, tab, A, xs):
    with Scope(nc, "m1") as m:
        o1 = m.sb("orT", [P, 4, SEQ])
        hT = m.sb("hT", [P, KD, SEQ])
        norm_phase(nc, "n1", xs, tab, A["norm_mix"], hT=hT)
        win = A["w_in"]
        with Scope(nc, "m2") as f:
            KR = f.sb("KR", [P, 4, 2, SEQ])
            BT, KDT = f.sb("BT", [P, 4, SEQ]), f.sb("KDT", [P, 4, SEQ])
            Vt, KDt, Bt = (f.sb(k, [P, NT, RW]) for k in ("Vt", "KDt", "Bt"))
            gate = f.sb("gate", [P, NT, RW])
            PC = f.sb("PC", [P, 4, NCH])
            bonus = f.sb("bonus", [P, NT * 8])
            with Scope(nc, "m3") as q:
                pr = q.sb("pr", [P, 14, SEQ])
                feature_phase(nc, "rp", hT, win[:, 0:1792], [(m, 0, SEQ, pr[:, m, :], 1.0) for m in range(14)])
                rwkv_prepare(nc, tab, pr, A, KR, BT, KDT, Vt, KDt, Bt, PC, bonus, gate)
            with Scope(nc, "m4") as q:
                U = q.sb("U", [P, 32, 512])
                rwkv_chunks(nc, tab, KR, BT, KDT, U)
                y = q.sb("y", [P, NT, RW])
                rwkv_scan(nc, tab, U, KR, Vt, KDt, Bt, PC, y)
                rwkv_finish(nc, tab, A, y, Vt, bonus, gate)
                transpose_phase(nc, "ty", lambda t, k: y[:, t, k * P:(k + 1) * P], NT, 4, o1, tab)
        gates = m.sb("gates", [P, NT, 2 * D])
        o2 = m.sb("odT", [P, 4, SEQ])
        with Scope(nc, "m5") as q:
            qkv = q.sb("qkv", [P, NT, 1536])
            o = q.sb("o", [P, NT, 512])
            nlam = q.sb("nlam", [P, 1])
            allt = lambda c: range(NT)
            lhs = lambda k, t: hT[:, k, t * P:(t + 1) * P]
            linear_phase(nc, "l1", lhs, KD, allt, win[:, 1792:3328], 1536, copy_evac(lambda t, c: qkv[:, t, c * 512:(c + 1) * 512]))

            def gate_evac(act, link, ps, t, c):
                return act.activation(gates[:, t, c * 512:(c + 1) * 512], ps, ACT.Sigmoid)
            linear_phase(nc, "l2", lhs, KD, allt, win[:, 3328:5376], 2048, gate_evac, on="a")
            lam_init = 0.8 - 0.6 * math.exp(-0.3 * 0)
            lambda_phase(nc, A, nlam, lam_init)
            qT, kT = q.sb("qT", [P, 4, SEQ]), q.sb("kT", [P, 4, SEQ])
            part = lambda c0: (lambda t: qkv[:, t, c0:c0 + 512].rearrange("p (h d) -> p h d", d=64))
            turned = lambda d: (lambda t: d[:, :, t * P:(t + 1) * P])
            rope = A["rope"][0]
            heads_phase(nc, "h1", tab, [
                dict(src=part(0), heads=8, tiles=range(NT), gain=A["q_norm"], rope=lambda t: t, rope_src=rope, axes=1,
                     scale=0.125, dst=turned(qT)),
                dict(src=part(512), heads=8, tiles=range(NT), gain=A["k_norm"], rope=lambda t: t, rope_src=None, axes=1,
                     scale=1.0, dst=turned(kT))], SEQ)
            jobs = []
            for h in range(4):
                for t in range(NT):
                    for c in range(2):
                        def post(v, link, ps, r, h=h, t=t, c=c):
                            dst = o[:, t, h * P:(h + 1) * P]
                            if c == 0:
                                return v.tensor_scalar(dst, ps[:, 0:P], r, None, ALU.mult)
                            link(v.tensor_scalar(r, r, nlam[:, 0:1], None, ALU.mult))
                            return v.scalar_tensor_tensor(out=dst, in0=ps[:, 0:P], scalar=r, in1=dst, op0=ALU.mult, op1=ALU.add)
                        rows = slice(64 * c, 64 * c + 64)
                        jobs.append(dict(
                            q=qT[rows, h, t * P:(t + 1) * P], k=kT[rows, h, :], keys=(t + 1) * P, dv=P, post=post,
                            add=lambda b, t=t: [(t * P, P, tab[:, C_CAUS:C_CAUS + P])],
                            v=lambda k, h=h: qkv[:, k, 1024 + h * P:1024 + (h + 1) * P]))
            attention_phase(nc, "a1", tab, jobs)
            subln_phase(nc, tab, o, A["subln_w"], 1.0 - lam_init)
            transpose_phase(nc, "to", lambda t, k: o[:, t, k * P:(k + 1) * P], NT, 4, o2, tab)
        with Scope(nc, "m6") as q:
            mixed = q.sb("mixed", [P, NT, D])
            mT = q.sb("mT", [P, KD, SEQ])
            allt = lambda c: range(NT)

            def mix1(v, link, ps, t, c):
                return v.tensor_tensor(mixed[:, t, c * 512:(c + 1) * 512], ps, gates[:, t, c * 512:(c + 1) * 512], ALU.mult)

            def mix2(v, link, ps, t, c):
                g = gates[:, t, D + c * 512:D + (c + 1) * 512]
                link(v.tensor_tensor(g, ps, g, ALU.mult))
                mx = mixed[:, t, c * 512:(c + 1) * 512]
                return v.tensor_tensor(mx, mx, g, ALU.add)
            linear_phase(nc, "l3", lambda k, t: o1[:, k, t * P:(t + 1) * P], 4, allt, A["w_branch_rwkv"], D, mix1)
            linear_phase(nc, "l4", lambda k, t: o2[:, k, t * P:(t + 1) * P], 4, allt, A["w_branch_diff"], D, mix2)
            transpose_phase(nc, "tm", lambda t, k: mixed[:, t, k * P:(k + 1) * P], NT, KD, mT, tab)
            linear_phase(nc, "l5", lambda k, t: mT[:, k, t * P:(t + 1) * P], KD, allt, A["w_out"], D, add_evac(xs))


def ple(nc, tab, A, xs):
    allt = lambda c: range(NT)
    with Scope(nc, "pl") as m:
        hT = m.sb("hT", [P, KD, SEQ])
        g = m.sb("g", [P, NT, D])
        pt = m.sb("p", [P, NT, 256])
        pT = m.sb("pT", [P, 2, SEQ])
        norm_phase(nc, "np", xs, tab, A["norm_ple"], hT=hT)

        def gate_evac(act, link, ps, t, c):
            return act.activation(g[:, t, c * 512:(c + 1) * 512], ps, ACT.Sigmoid)
        linear_phase(nc, "lg", lambda k, t: hT[:, k, t * P:(t + 1) * P], KD, allt, A["w_ple_gate"], D, gate_evac, on="a")
        load_phase(nc, "lp", [(pt[:, :, :], A["p"].rearrange("(t p) d -> p t d", p=P))])
        with Scope(nc, "pq") as s:
            ps = s.ps("pt", 2)
            td, ev = s.sem("td"), s.sem("ev")
            block = s.block()

            @block.tensor
            def _(pe):
                for t in range(NT):
                    for k in range(2):
                        mm = pe.transpose(ps[:, (k * NT + t) * P:(k * NT + t + 1) * P], pt[:, t, k * P:(k + 1) * P],
                                          tab[:, C_IDENT:C_IDENT + P])
                mm.then_inc(td, 1)

            @block.vector
            def _(v):
                v.wait_ge(td, 1)
                v.tensor_copy(pT[:, :, :], ps[:, :].rearrange("p (k t) -> p k t", k=2)).then_inc(ev, 1)

        def add(v, link, ps, t, c):
            gg = g[:, t, c * 512:(c + 1) * 512]
            link(v.tensor_tensor(gg, ps, gg, ALU.mult))
            x = xs[t][:, c * 512:(c + 1) * 512]
            return v.tensor_tensor(x, x, gg, ALU.add)
        linear_phase(nc, "lq", lambda k, t: pT[:, k, t * P:(t + 1) * P], 2, allt, A["w_ple_proj"], D, add)


def gated_add(rows_of, xs, G):
    def evac(v, link, ps, t, c):
        cs = slice(c * 512, (c + 1) * 512)
        link(v.tensor_tensor(ps, ps, G[rows_of(t)][:, cs], ALU.mult))
        return v.tensor_tensor(xs[t][:, cs], xs[t][:, cs], ps, ALU.add)
    return evac


def even_mixer(nc, tab, A, xs, mod):
    is_x = lambda t: 0 if t >= XT0 else 1
    with Scope(nc, "e1") as m:
        oT = m.sb("oT", [P, 8, NTA * P])
        with Scope(nc, "e2") as q:
            pj = q.sb("pj", [P, NTA, 1280])
            with Scope(nc, "e3") as r:
                hT = r.sb("hT", [P, KD, NTA * P])
                mods = [(mod(j, 1), mod(j, 0)) for j in range(2)]
                norm_phase(nc, "ne", xs, tab, A["norm_mix_g_2"][0], hT=hT, mods=[mods[is_x(t)] for t in range(NTA)])

                def evac(v, link, ps, t, c):
                    n = min(512, 1280 - 512 * c)
                    return v.tensor_copy(pj[:, t, c * 512:c * 512 + n], ps)
                linear_phase(nc, "le", lambda k, t: hT[:, k, t * P:(t + 1) * P], KD, lambda c: range(NTA),
                             A["even_w_in_2"], 1280, evac)
            dx, dc = oT[:, 4:8, XT0 * P:], oT[:, 4:8, 0:XT0 * P]
            pool_phase(nc, "px", A["band_x"], A["pool_w_2"], A["pool_scale_2"], lambda t: pj[:, XT0 + t, 768:1280], NT, dx)
            pool_phase(nc, "pc", A["band_c"], A["pool_w_2"], A["pool_scale_2"], lambda t: pj[:, t, 768:1280], XT0, dc)
            qT, kT = q.sb("qT", [P, 4, NTA * P]), q.sb("kT", [P, 2, NTA * P])
            kd = q.sb("kd", [P, NTA, 4, 64])
            o = q.sb("o", [P, NTA, 512])
            with Scope(nc, "e4") as s:
                dn = s.sem("dn")
                block = s.block()

                @block.vector
                def _(v):
                    for t in range(NTA):
                        src = pj[:, t, 512:640].rearrange("p (h d) -> p h d", d=64).unsqueeze(2).to_broadcast([P, 2, 2, 64])
                        v.tensor_copy(kd[:, t, :, :].rearrange("p (h e) d -> p h e d", e=2), src).then_inc(dn, 1)
            part = lambda t: pj[:, t, 0:512].rearrange("p (h d) -> p h d", d=64)
            turned = lambda d: (lambda t: d[:, :, t * P:(t + 1) * P])
            rope = A["rope"][1]
            rx, rc = range(XT0, NTA), range(XT0)
            common = dict(axes=2)
            heads_phase(nc, "he", tab, [
                dict(src=part, heads=8, tiles=rx, gain=A["a_q_gain_2"], rope=lambda t: t - XT0, rope_src=rope, scale=0.125,
                     dst=turned(qT), **common),
                dict(src=lambda t: kd[:, t, :, :], heads=4, tiles=rx, gain=A["a_k_gain_2"], rope=lambda t: t - XT0,
                     rope_src=None, scale=1.0, dst=turned(kT), **common),
                dict(src=part, heads=8, tiles=rc, gain=A["a_q_gain_2"], rope=None, rope_src=None, scale=0.125,
                     dst=turned(qT), **common),
                dict(src=lambda t: kd[:, t, :, :], heads=4, tiles=rc, gain=A["a_k_gain_2"], rope=None, rope_src=None,
                     scale=1.0, dst=turned(kT), **common)], NTA * P)
            jobs = []
            for h in range(8):
                rows = slice(64 * (h % 2), 64 * (h % 2) + 64)
                for t in range(NTA):
                    def post(v, link, ps, r, h=h, t=t):
                        return v.tensor_scalar(o[:, t, h * 64:(h + 1) * 64], ps[:, 0:64], r, None, ALU.mult)
                    jobs.append(dict(q=qT[rows, h // 2, t * P:(t + 1) * P], k=kT[rows, h // 4, :],
                                     keys=CTXL if t < XT0 else NTA * P, dv=64, post=post, add=lambda b: [],
                                     v=lambda k, h=h: pj[:, k, 640 + 64 * (h // 4):704 + 64 * (h // 4)]))
            attention_phase(nc, "ae", tab, jobs)
            transpose_phase(nc, "te", lambda t, k: o[:, t, k * P:(k + 1) * P], NTA, 4, oT, tab)
        G = [m.sb(f"G{j}", [P, D]) for j in range(2)]
        linear_phase(nc, "lf", lambda k, t: oT[:, k, t * P:(t + 1) * P], 8, lambda c: range(NTA), A["even_w_out_2"], D,
                     gated_add(is_x, xs, G), loads=[(G[j][:, :], bc_row(mod(j, 2), D)) for j in range(2)])


def odd_mixer(nc, tab, A, xs, mod, relpad):
    is_x = lambda t: 0 if t >= XT0 else 1
    H = 16
    with Scope(nc, "o1") as m:
        oT = m.sb("oT", [P, 8, SEQ])
        with Scope(nc, "o2") as q:
            vv = q.sb("vv", [P, NTA, D])
            qT, kT = q.sb("qT", [P, 8, SEQ]), q.sb("kT", [P, 8, NTA * P])
            with Scope(nc, "o3") as r:
                hT = r.sb("hT", [P, KD, NTA * P])
                mods = [(mod(j, 1), mod(j, 0)) for j in range(2)]
                norm_phase(nc, "no", xs, tab, A["norm_mix_g_2"][1], hT=hT, mods=[mods[is_x(t)] for t in range(NTA)])
                C = XT0 * P
                feature_phase(nc, "lo", hT, A["odd_w_in_2"],
                              [(m, C, SEQ, qT[:, m, :], 0.125) for m in range(8)]
                              + [(8 + m, c0, n, kT[:, m, c0:c0 + n], 1.0) for m in range(8) for c0, n in ((0, C), (C, SEQ))])
                linear_phase(nc, "lv", lambda k, t: hT[:, k, t * P:(t + 1) * P], KD, lambda c: range(NTA),
                             A["odd_w_in_2"][:, 2 * D:3 * D], D, copy_evac(lambda t, c: vv[:, t, c * 512:(c + 1) * 512]))
            o = q.sb("o", [P, NT, D])
            jobs = []
            for h in range(H):
                rows = slice(64 * (h % 2), 64 * (h % 2) + 64)
                for t in range(NT):
                    def post(v, link, ps, r, h=h, t=t):
                        return v.tensor_scalar(o[:, t, h * 64:(h + 1) * 64], ps[:, 0:64], r, None, ALU.mult)
                    jobs.append(dict(q=qT[rows, h // 2, t * P:(t + 1) * P], k=kT[rows, h // 2, :], keys=NTA * P, dv=64,
                                     post=post, v=lambda k, h=h: vv[:, k, 64 * h:64 * h + 64],
                                     add=lambda b, t=t: [(CTXL, SEQ, b[:, 7 - 2 * t:15 - 2 * t, :].rearrange("p r c -> p (r c)"))]))

            def load(h, bt):
                base = relpad[h * 15:(h + 1) * 15, :]

                def window(r):
                    return bass.AP(tensor=base.tensor, offset=base.offset + HD * P * r + HD - 1,
                                   ap=[[P - 1, HD], [HD * P, 14], [1, HD]])
                return [(bt[0:64, 1:15, :], window(1)), (bt[64:128, 1:15, :], window(0))]
            attention_phase(nc, "ao", tab, jobs, bias=dict(load=load, heads=H, per=NT))
            transpose_phase(nc, "tp", lambda t, k: o[:, t, k * P:(k + 1) * P], NT, 8, oT, tab)
        G = [m.sb("G0", [P, D])]
        xq = xs[XT0:]
        linear_phase(nc, "lr", lambda k, t: oT[:, k, t * P:(t + 1) * P], 8, lambda c: range(NT), A["odd_w_out_2"], D,
                     gated_add(lambda t: 0, xq, G), loads=[(G[0][:, :], bc_row(mod(0, 2), D))])


def fused_blocks(nc, A, out, upto=None):
    Scope.used = []
    xbuf = nc.dram_tensor("xbuf", [SLOTS, D], F32, kind="Internal").ap()
    ybuf = nc.dram_tensor("ybuf", [SLOTS, D], F32, kind="Internal").ap()
    modD = nc.dram_tensor("modD", [2, 2, 6 * D], F32, kind="Internal").ap()
    relpad = nc.dram_tensor("relpad", [240, HD * P], F32, kind="Internal").ap()

    with nc.allow_non_contiguous_dma("parameter vectors, once"), Scope(nc, "g") as g:
        tab = g.sb("tab", [P, C_END])
        x = g.sb("x", [P, NT, D])
        xq = [x[:, t, :] for t in range(NT)]

        def stage(n):
            return upto is None or n in upto
        load_phase(nc, "ld", [(tab[:, :], A["table"]),
                              (x[:, :, :], A["x"].rearrange("(t p) d -> p t d", p=P))])
        clear_phase(nc, tab, xbuf, ybuf, A["na_rel_bias_2"], relpad)
        if stage("mix1"):
            first_mixer(nc, tab, A, xq)
        if stage("moe1"):
            moe(nc, "f1", tab, xq, A["norm_ffn"], None, None, A["w_group"], A["b_group"], A["w_expert_router"],
                A["b_expert_router"], A["w_gate"], A["w_up"], A["w_down"], xbuf, ybuf)
        if stage("ple"):
            ple(nc, tab, A, xq)
        if stage("ada"):
            modulation_phase(nc, tab, A["c_2"], A["c_ctx_2"], A["ada_w_2"], A["ada_b_2"], modD)
        ctx = g.sb("ctx", [P, XT0, D])
        xs = [ctx[:, t, :] for t in range(XT0)] + xq
        load_phase(nc, "lc", [(ctx[:, :, :], A["ctx_2"].rearrange("(t p) d -> p t d", p=P))])
        for l in range(2):
            rows = [[modD[l, j, i * D:(i + 1) * D] for i in range(6)] for j in range(2)]
            mod = lambda j, i, rows=rows: rows[j][i]
            moe_w = [A[k][l] for k in ("moe_w_group_2", "moe_b_group_2", "moe_w_expert_2", "moe_b_expert_2", "moe_w1_2",
                                       "moe_w3_2", "moe_w2_2")]
            pair = [(mod(j, 4), mod(j, 3)) for j in range(2)]
            if l == 0:
                if stage("mix2"):
                    even_mixer(nc, tab, A, xs, mod)
                if stage("moe2"):
                    moe(nc, "f2", tab, xs, A["norm_ffn_g_2"][0], [pair[1]] * XT0 + [pair[0]] * NT,
                        [mod(1, 5)] * XT0 + [mod(0, 5)] * NT, *moe_w, xbuf, ybuf)
            else:
                if stage("mix3"):
                    odd_mixer(nc, tab, A, xs, mod, relpad)
                if stage("moe3"):
                    moe(nc, "f3", tab, xq, A["norm_ffn_g_2"][1], [pair[0]] * NT, [mod(0, 5)] * NT, *moe_w, xbuf, ybuf)
        if stage("fin"):
            with Scope(nc, "fn") as s:
                h = s.sb("h", [P, NT, D])
                norm_phase(nc, "nf", xq, tab, A["final_g_2"], htok=h)
                store_phase(nc, h, out)
        else:
            store_phase(nc, x, out)


def store_phase(nc, h, out):
    with Scope(nc, "st") as s:
        done = s.sem("out")
        block = s.block()

        @block.sync
        def _(sp):
            sp.dma_start(out.rearrange("(t p) d -> p t d", p=P), h[:, :, :]).then_inc(done, 16)
            sp.wait_ge(done, 16)


_INS = """x p norm_mix w_in rwkv_mu rwkv_w0 rwkv_w2 rwkv_a0 rwkv_a2 rwkv_g2 rwkv_k_k rwkv_k_a rwkv_r_k rwkv_ln_w
rwkv_ln_b q_norm k_norm lambda_q1 lambda_k1 lambda_q2 lambda_k2 subln_w w_branch_rwkv w_branch_diff w_out norm_ffn
w_group b_group w_expert_router b_expert_router w_gate w_up w_down norm_ple w_ple_gate w_ple_proj c_2 ctx_2 c_ctx_2
ada_w_2 ada_b_2 norm_mix_g_2 norm_ffn_g_2 even_w_in_2 even_w_out_2 a_q_gain_2 a_k_gain_2 pool_w_2 pool_scale_2
odd_w_in_2 odd_w_out_2 na_rel_bias_2 moe_w_group_2 moe_b_group_2 moe_w_expert_2 moe_b_expert_2 moe_w1_2 moe_w3_2
moe_w2_2 final_g_2""".split()
_DROP = {"x": 1, "p": 2, "rwkv_r_k": 1, "c_2": 1, "ctx_2": 1}
_KEEP = {"c_ctx_2", "ada_w_2", "ada_b_2", "norm_mix_g_2", "norm_ffn_g_2", "final_g_2"}


def views(name, ap):
    if name in _KEEP or name.startswith("moe_"):
        return ap
    for _ in range(_DROP.get(name, 1)):
        ap = ap[0]
    if name == "rwkv_r_k":
        ap = ap.rearrange("h d -> (h d)")
    return ap


def kernel(**inputs):
    import numpy as _np
    import concourse.bacc as _bacc
    from concourse import mybir as _mybir
    from concourse.bass_utils import run_bass_kernel_spmd as _run

    nc = _bacc.Bacc("TRN2", target_bir_lowering=False, num_devices=1)
    arrays, aps = {}, {}
    for name in _INS:
        a = _np.ascontiguousarray(inputs[name])
        arrays[f"in_{name}_dram"] = a
        ap = nc.dram_tensor(f"in_{name}_dram", a.shape, _mybir.dt.from_np(a.dtype), kind="ExternalInput").ap()
        aps[name] = views(name, ap)
    for name, a in constants().items():
        arrays[f"const_{name}_dram"] = a
        aps[name] = nc.dram_tensor(f"const_{name}_dram", a.shape, _mybir.dt.float32, kind="ExternalInput").ap()
    out = nc.dram_tensor("out_0_dram", (1, SEQ, D), _mybir.dt.float32, kind="ExternalOutput").ap()
    fused_blocks(nc, aps, out[0])
    r = _run(nc, [arrays], core_ids=[0])
    return r.results[0]["out_0_dram"]
```

```python
import math
from contextlib import ExitStack

import numpy as np

import concourse.bass as bass
from concourse import mybir

ALU = mybir.AluOpType
ACT = mybir.ActivationFunctionType
AX = mybir.AxisListType
F32 = mybir.dt.float32
F32R = mybir.dt.float32r
I32 = mybir.dt.int32
U32 = mybir.dt.uint32

P = 128
D = 1024
KD = D // P
SEQ = 512
CTXL = 256
XT0 = CTXL // P
NT = SEQ // P
NTA = NT + XT0
EPS = 1e-6
NEG = -1e30

RW = 512
HD = 64
CH = 64
NCH = SEQ // CH
GN_EPS = 64e-5
LVL = 6

NE = 32
FF = 512
KF = FF // P
NG = 4
EPG = 8
MAXOV = 2 * NTA
SLOTS = (NE + MAXOV) * P

C_IDENT = 0
C_TRI = C_IDENT + P
C_ONES = C_TRI + P
C_BLK = C_ONES + P
C_CAUS = C_BLK + P
C_HIND = C_CAUS + P
C_IO = C_HIND + 2
C_COL = C_IO + NE
C_END = C_COL + HD

R_SCAN = 0
R_UNIT = R_SCAN + SEQ
R_LVL = R_UNIT + 4 * P
R_END = R_LVL + LVL * P


def constants():
    p = np.arange(P)
    c = np.zeros((P, C_END), np.float32)
    r = np.zeros((P, R_END), np.float32)
    c[:, C_IDENT:C_IDENT + P] = np.eye(P)
    s, t = p[:, None], p[None, :]
    c[:, C_TRI:C_TRI + P] = s < t
    c[:, C_ONES:C_ONES + P] = 1
    c[:, C_BLK:C_BLK + P] = s // HD == t // HD
    c[:, C_CAUS:C_CAUS + P] = np.where(t <= s, 0, NEG)
    c[:, C_HIND:C_HIND + 2] = p[:, None] // HD == np.arange(2)[None, :]
    r[:, R_SCAN:R_SCAN + SEQ] = (np.arange(SEQ) % CH != 0)[None, :]
    same = s // CH == t // CH
    for j, m in enumerate((same & (s < t), -1.0 * (same & (s <= t)), same & (s < t), same & (s <= t))):
        r[:, R_UNIT + j * P:R_UNIT + (j + 1) * P] = m
    for l in range(LVL):
        b = 1 << l
        r[:, R_LVL + l * P:R_LVL + (l + 1) * P] = (s // (2 * b) == t // (2 * b)) & (s // b % 2 == 0) & (t // b % 2 == 1)
    c[:, C_IO:C_IO + NE] = np.arange(NE)
    q = p % HD
    start = np.clip(q - 8, 0, HD - 16)
    j = np.arange(HD)[None, :]
    c[:, C_COL:C_COL + HD] = np.where((j >= start[:, None]) & (j < start[:, None] + 16), 0, NEG)

    f = np.float32
    inv1 = (f(10000.0) ** (-np.arange(0, 64, 2, dtype=f) / f(64))).astype(f)
    ang1 = np.arange(SEQ, dtype=f)[:, None] * inv1[None, :]
    inv2 = (f(10000.0) ** (-np.arange(16, dtype=f) / f(16))).astype(f)
    tt = np.arange(SEQ)
    pos = np.stack([tt // 64, tt % 64], -1).astype(f)
    ang2 = (pos[:, :, None] * inv2).reshape(SEQ, 32)
    rope = np.stack([np.concatenate([np.cos(a), np.sin(a)], 1) for a in (ang1, ang2)]).astype(f)

    def bands(L):
        out = np.zeros((4, L, L), np.float32)
        t = np.arange(L)
        for g, w in enumerate((2, 4, 8, 16)):
            lo, hi = np.clip(t - w // 2, 0, L), np.clip(t - w // 2 + w, 0, L)
            ss = np.arange(L)[:, None]
            out[g] = ((ss >= lo) & (ss < hi)) / (hi - lo).astype(np.float32) - np.eye(L)
        return out

    return {"table": c, "rwkv_table": r, "rope": rope, "band_x": bands(SEQ), "band_c": bands(CTXL)}


class Scope:

    used = []

    def __init__(self, nc, name):
        self.nc, self.name, self.stack, self.sems = nc, name, ExitStack(), []

    def __enter__(self):
        return self

    def __exit__(self, *a):
        self.stack.__exit__(*a)
        Scope.used += self.sems
        if len(Scope.used) > 120:
            self.nc.clear_and_free_semaphores(Scope.used)
            self.nc.all_engine_barrier()
            Scope.used = []

    def sb(self, name, shape, dt=F32):
        return self.stack.enter_context(self.nc.sbuf_tensor(f"{self.name}_{name}", shape, dt))

    def pair(self, name, shape):
        return self.sb(f"{name}_hi", shape, F32R), self.sb(f"{name}_lo", shape, F32R)

    def ps(self, name, banks=1):
        return self.stack.enter_context(self.nc.psum_tensor(f"{self.name}_psum_{name}", [P, 512 * banks], F32))

    def sem(self, name):
        self.sems.append(self.nc.alloc_semaphore(f"{self.name}_{name}"))
        return self.sems[-1]

    def block(self):
        return self.stack.enter_context(self.nc.Block())


class Chain:

    def __init__(self, eng, sem):
        self.eng, self.sem, self.n = eng, sem, 0

    def __call__(self, ins):
        self.n += 1
        ins.then_inc(self.sem, 1)
        self.eng.wait_ge(self.sem, self.n)


def split_hi(act, dst, src):
    return act.activation(dst, src, ACT.Copy)


def split_lo(v, dst, src, hi):
    return v.tensor_tensor(dst, src, hi.bitcast(F32), ALU.subtract)


def products(pe, out, lhs, rhs, first, last):
    (lh, ll), (rh, rl) = lhs, rhs
    pe.matmul(out, lh, rh, start=first, stop=False)
    pe.matmul(out, lh, rl, start=False, stop=False)
    return pe.matmul(out, ll, rh, start=False, stop=last)


def bc_row(ap, n):
    return ap.rearrange("(a n) -> a n", a=1).to_broadcast([P, n])


def norm_phase(nc, name, xs, tab, gain, hT=None, htok=None, mods=None, ahead=None):
    n = len(xs)
    with Scope(nc, name) as s:
        G = s.sb("gain", [P, D])
        rows = []
        for m in mods or []:
            if not any(m is r for r in rows):
                rows.append(m)
        SC = [s.sb(f"scale{i}", [P, D]) for i in range(len(rows))]
        SH = [s.sb(f"shift{i}", [P, D]) for i in range(len(rows))]
        H = htok if htok is not None else s.sb("h", [P, n, D])
        sq = s.sb("sq", [P, D])
        ss = s.sb("ss", [P, 3, n])
        pt = [s.ps(f"pt{i}", 2) for i in range(2)]
        rows_in, ssq_done, ms_done, root_done, h_done = (s.sem(k) for k in ("rows", "ssq", "ms", "root", "h"))
        t_done, evac_a, evac_v, v_own, a_own = (s.sem(k) for k in ("t", "eva", "evv", "vown", "aown"))
        nrows = 1 + 2 * len(rows)
        pair = isinstance(hT, tuple)
        per = 2 if pair else 1

        def turned(d, t, half):
            return d[:, 4 * half:4 * half + 4, t * P:(t + 1) * P]

        def bank(t, half):
            return pt[t % 2][:, half * 512:(half + 1) * 512].rearrange("p (k t) -> p k t", k=4)

        block = s.block()

        @block.sync
        def _(sp):
            sp.dma_start(G[:, :], bc_row(gain, D)).then_inc(rows_in, 16)
            for i, (sc, sh) in enumerate(rows):
                sp.dma_start(SC[i][:, :], bc_row(sc, D)).then_inc(rows_in, 16)
                sp.dma_start(SH[i][:, :], bc_row(sh, D)).then_inc(rows_in, 16)
            if ahead:
                ahead(sp)

        @block.scalar
        def _(act):
            link = Chain(act, a_own)
            for t in range(n):
                link(act.activation(sq[:, :], xs[t], ACT.Square, accum_out=ss[:, 0, t:t + 1]))
            act.activation(ss[0:1, 2, 0:1], ss[0:1, 0, 0:1], ACT.Copy).then_inc(ssq_done, 1)
            act.wait_ge(ms_done, 1)
            act.activation(ss[:, 2, :], ss[:, 1, :], ACT.Sqrt).then_inc(root_done, 1)
            if pair:
                for t in range(n):
                    for half in range(2):
                        act.wait_ge(t_done, 2 * t + half + 1)
                        split_hi(act, turned(hT[0], t, half), bank(t, half)).then_inc(evac_a, 1)
            elif hT is not None:
                for t in range(n):
                    act.wait_ge(t_done, 2 * t + 1)
                    act.activation(turned(hT, t, 0), bank(t, 0), ACT.Copy).then_inc(evac_a, 1)

        @block.vector
        def _(v):
            link = Chain(v, v_own)
            v.wait_ge(ssq_done, 1)
            v.tensor_scalar(ss[:, 1, :], ss[:, 0, :], 1.0 / D, EPS, ALU.mult, ALU.add).then_inc(ms_done, 1)
            v.wait_ge(rows_in, 16 * nrows)
            for i in range(len(rows)):
                link(v.scalar_tensor_tensor(out=SC[i][:, :], in0=SC[i][:, :], scalar=1.0, in1=G[:, :], op0=ALU.add, op1=ALU.mult))
            v.wait_ge(root_done, 1)
            link(v.reciprocal(ss[:, 0, :], ss[:, 2, :]))

            def evac(t):
                if pair:
                    for half in range(2):
                        v.wait_ge(evac_a, 2 * t + half + 1)
                        split_lo(v, turned(hT[1], t, half), bank(t, half), turned(hT[0], t, half)).then_inc(evac_v, 1)
                else:
                    v.wait_ge(t_done, 2 * t + 2)
                    v.tensor_copy(turned(hT, t, 1), bank(t, 1)).then_inc(evac_v, 1)

            for t in range(n):
                i = [k for k, m in enumerate(rows) if mods and m is mods[t]]
                g = SC[i[0]] if i else G
                ins = v.scalar_tensor_tensor(out=H[:, t, :], in0=xs[t], scalar=ss[:, 0, t:t + 1], in1=g[:, :],
                                             op0=ALU.mult, op1=ALU.mult)
                if i:
                    link(ins)
                    ins = v.tensor_tensor(H[:, t, :], H[:, t, :], SH[i[0]][:, :], ALU.add)
                ins.then_inc(h_done, 1)
                if hT is not None and t >= 1:
                    evac(t - 1)
            if hT is not None:
                evac(n - 1)

        if hT is not None:
            @block.tensor
            def _(pe):
                for t in range(n):
                    pe.wait_ge(h_done, t + 1)
                    if t >= 2:
                        pe.wait_ge(evac_a, per * (t - 1))
                        pe.wait_ge(evac_v, per * (t - 1))
                    for k in range(KD):
                        mm = pe.transpose(pt[t % 2][:, k * P:(k + 1) * P], H[:, t, k * P:(k + 1) * P],
                                          tab[:, C_IDENT:C_IDENT + P])
                        if k % 4 == 3:
                            mm.then_inc(t_done, 1)


def linear_phase(nc, name, lhs, nk, tiles, W, cols, evac, on="v", loads=(), RING=6):
    nch = (cols + 511) // 512
    KP = 1
    NKP = nk // KP
    RAW, BANKS = 6, 8
    LAG = RING - 1
    pieces = [(c, kp) for c in range(nch) for kp in range(NKP)]
    jobs = [(c, t) for c in range(nch) for t in tiles(c)]
    index = {j: i for i, j in enumerate(jobs)}

    count = {}
    for n, (c, kp) in enumerate(pieces):
        for t in tiles(c):
            count[n, t] = len(count) + 1
    last = {n: max(v for (m, _), v in count.items() if m == n) for n in range(len(pieces))}

    def width(c):
        return min(512, cols - c * 512)

    with Scope(nc, name) as s:
        raw = [s.sb(f"raw{i}", [P, KP, 512]) for i in range(RAW)]
        w = [s.pair(f"w{i}", [P, KP, 512]) for i in range(RING)]
        banks = [s.ps(f"acc{i}") for i in range(BANKS)]
        raw_in = [s.sem(f"raw{i}") for i in range(RAW)]
        hi_done, lo_done, mm_done, out_done, own, pre_in = (s.sem(k) for k in ("hi", "lo", "mm", "out", "own", "pre"))
        block = s.block()

        @block.sync
        def _(sp):
            for n, (c, kp) in enumerate(pieces):
                if n >= RAW:
                    sp.wait_ge(lo_done, n - RAW + 1)
                src = W[kp * KP * P:(kp + 1) * KP * P, c * 512:c * 512 + width(c)]
                sp.dma_start(raw[n % RAW][:, :, 0:width(c)], src.rearrange("(k p) n -> p k n", p=P)
                             ).then_inc(raw_in[n % RAW], 16)
                if n == 0:
                    for dst, src in loads:
                        sp.dma_start(dst, src).then_inc(pre_in, 16)

        @block.tensor
        def _(pe):
            for n, (c, kp) in enumerate(pieces):
                pe.wait_ge(lo_done, n + 1)
                for t in tiles(c):
                    i = index[c, t]
                    if kp == 0 and i >= BANKS:
                        pe.wait_ge(out_done, i - BANKS + 1)
                    for k in range(KP):
                        rhs = [h[:, k, 0:width(c)] for h in w[n % RING]]
                        mm = products(pe, banks[i % BANKS][:, 0:width(c)], lhs(kp * KP + k, t), rhs,
                                      kp == 0 and k == 0, kp == NKP - 1 and k == KP - 1)
                    mm.then_inc(mm_done, 1)

        def copy_out(eng, link, n):
            c, kp = pieces[n]
            if kp == NKP - 1:
                for t in tiles(c):
                    i = index[c, t]
                    eng.wait_ge(mm_done, count[n, t])
                    evac(eng, link, banks[i % BANKS][:, 0:width(c)], t, c).then_inc(out_done, 1)

        def free(eng, n):
            if n >= RING:
                eng.wait_ge(mm_done, last[n - RING])

        @block.scalar
        def _(act):
            link = Chain(act, own)
            if loads and on == "a":
                act.wait_ge(pre_in, 16 * len(loads))
            for n in range(len(pieces) + LAG):
                if n < len(pieces):
                    c = pieces[n][0]
                    act.wait_ge(raw_in[n % RAW], 16 * (n // RAW + 1))
                    free(act, n)
                    split_hi(act, w[n % RING][0][:, :, 0:width(c)], raw[n % RAW][:, :, 0:width(c)]).then_inc(hi_done, 1)
                if on == "a" and n >= LAG:
                    copy_out(act, link, n - LAG)

        @block.vector
        def _(v):
            link = Chain(v, own)
            if loads and on == "v":
                v.wait_ge(pre_in, 16 * len(loads))
            for n in range(len(pieces) + LAG):
                if n < len(pieces):
                    c = pieces[n][0]
                    v.wait_ge(hi_done, n + 1)
                    split_lo(v, w[n % RING][1][:, :, 0:width(c)], raw[n % RAW][:, :, 0:width(c)],
                             w[n % RING][0][:, :, 0:width(c)]).then_inc(lo_done, 1)
                if on == "v" and n >= LAG:
                    copy_out(v, link, n - LAG)


def transpose_phase(nc, name, src, nt, nk, dst, tab):
    G = min(nk, 4)
    groups = [(t, k) for t in range(nt) for k in range(0, nk, G)]
    with Scope(nc, name) as s:
        banks = [s.ps(f"pt{i}") for i in range(4)]
        t_done, hi_done, lo_done = s.sem("t"), s.sem("hi"), s.sem("lo")
        block = s.block()

        def parts(i):
            t, k = groups[i]
            hi, lo = (d[:, k:k + G, t * P:(t + 1) * P] for d in dst)
            return hi, lo, banks[i % 4][:, 0:G * P].rearrange("p (k t) -> p k t", k=G)

        @block.tensor
        def _(pe):
            for i, (t, k) in enumerate(groups):
                if i >= 4:
                    pe.wait_ge(lo_done, i - 3)
                for j in range(G):
                    mm = pe.transpose(banks[i % 4][:, j * P:(j + 1) * P], src(t, k + j), tab[:, C_IDENT:C_IDENT + P])
                mm.then_inc(t_done, 1)

        @block.scalar
        def _(act):
            for i in range(len(groups)):
                hi, _, bank = parts(i)
                act.wait_ge(t_done, i + 1)
                split_hi(act, hi, bank).then_inc(hi_done, 1)

        @block.vector
        def _(v):
            for i in range(len(groups)):
                hi, lo, bank = parts(i)
                v.wait_ge(hi_done, i + 1)
                split_lo(v, lo, bank, hi).then_inc(lo_done, 1)


def heads_phase(nc, name, tab, items, T):
    with Scope(nc, name) as s:
        mh = max(i["heads"] for i in items)
        nj = sum(len(i["tiles"]) for i in items)
        tmp = s.sb("tmp", [P, mh * 32])
        tmp2 = s.sb("tmp2", [P, mh * 32])
        sqt = s.sb("sq", [P, mh * 64])
        work = [s.sb(f"work{i}", [P, mh * 64]) for i in range(2)]
        st = s.sb("stat", [P, nj, mh])
        st2 = s.sb("stat2", [P, nj, mh])
        gains = [s.sb(f"gain{i}", [P, 64]) for i in range(len(items))]
        rope = s.sb("rope", [P, 4, 64])
        pt = [s.ps(f"pt{i}", 2) for i in range(2)]
        loaded, ss_done, root_done, y_done, t_done, evac = (s.sem(k) for k in ("ld", "ss", "root", "y", "t", "evac"))
        own = s.sem("own")
        loads = []
        for i, it in enumerate(items):
            if it["gain"] is not None:
                loads.append((gains[i][:, :], bc_row(it["gain"], 64)))
        rsrc = [it["rope_src"] for it in items if it["rope_src"] is not None]
        if rsrc:
            loads.append((rope[:, :, :], rsrc[0].rearrange("(t p) c -> p t c", p=P)))
        jobs = [(i, t) for i in range(len(items)) for t in items[i]["tiles"]]
        block = s.block()

        @block.sync
        def _(sp):
            for d, sr in loads:
                sp.dma_start(d, sr).then_inc(loaded, 16)

        @block.vector
        def _(v):
            link = Chain(v, own)
            normed = any(it["gain"] is not None for it in items)
            if normed:
                for j, (i, t) in enumerate(jobs):
                    it = items[i]
                    h = it["heads"]
                    sq = sqt[:, 0:h * 64].rearrange("p (h d) -> p h d", d=64)
                    link(v.tensor_tensor(sq, it["src"](t), it["src"](t), ALU.mult))
                    link(v.tensor_reduce(st[:, j, 0:h], sq, AX.X, ALU.add))
                    if h < mh:
                        link(v.memset(st[:, j, h:mh], 1.0))
                v.tensor_scalar(st2[:, :, :], st[:, :, :], 1.0 / 64, EPS, ALU.mult, ALU.add).then_inc(ss_done, 1)
                v.wait_ge(root_done, 1)
                link(v.reciprocal(st2[:, :, :], st[:, :, :]))
            if loads:
                v.wait_ge(loaded, 16 * len(loads))
            for j, (i, t) in enumerate(jobs):
                it = items[i]
                h = it["heads"]
                src = it["src"](t)
                if j >= 2:
                    v.wait_ge(t_done, j - 1)
                y = work[j % 2][:, 0:h * 64].rearrange("p (h d) -> p h d", d=64)
                if it["gain"] is None:
                    v.tensor_scalar(y, src, it["scale"], None, ALU.mult).then_inc(y_done, 1)
                    continue
                link(v.tensor_tensor(src, src, st2[:, j, 0:h].unsqueeze(2).to_broadcast([P, h, 64]), ALU.mult))
                g = gains[i][:, :].unsqueeze(1).to_broadcast([P, h, 64])
                if it["rope"] is None:
                    link(v.tensor_scalar(src, src, it["scale"], None, ALU.mult))
                    v.tensor_tensor(y, src, g, ALU.mult).then_inc(y_done, 1)
                    continue
                link(v.tensor_tensor(src, src, g, ALU.mult))
                A, F = it["axes"], 32 // it["axes"]
                for a in range(A):
                    x1, x2 = src[:, :, 2 * F * a:2 * F * a + F], src[:, :, 2 * F * a + F:2 * F * (a + 1)]
                    y1, y2 = y[:, :, 2 * F * a:2 * F * a + F], y[:, :, 2 * F * a + F:2 * F * (a + 1)]
                    r = it["rope"](t)
                    co = rope[:, r, F * a:F * (a + 1)].unsqueeze(1).to_broadcast([P, h, F])
                    si = rope[:, r, 32 + F * a:32 + F * (a + 1)].unsqueeze(1).to_broadcast([P, h, F])
                    u = tmp[:, 0:h * F].rearrange("p (h f) -> p h f", f=F)
                    w = tmp2[:, 0:h * F].rearrange("p (h f) -> p h f", f=F)
                    v.tensor_tensor(u, x1, co, ALU.mult).then_inc(own, 1)
                    link.n += 1
                    link(v.tensor_tensor(w, x2, si, ALU.mult))
                    link(v.tensor_tensor(y1, u, w, ALU.subtract))
                    v.tensor_tensor(u, x2, co, ALU.mult).then_inc(own, 1)
                    link.n += 1
                    link(v.tensor_tensor(w, x1, si, ALU.mult))
                    link(v.tensor_tensor(y2, u, w, ALU.add))
                v.tensor_scalar(y, y, it["scale"], None, ALU.mult).then_inc(y_done, 1)

        @block.scalar
        def _(act):
            if any(it["gain"] is not None for it in items):
                act.wait_ge(ss_done, 1)
                act.activation(st[:, :, :], st2[:, :, :], ACT.Sqrt).then_inc(root_done, 1)
            for j, (i, t) in enumerate(jobs):
                act.wait_ge(t_done, j + 1)
                m = items[i]["heads"] // 2
                act.activation(items[i]["dst"](t), pt[j % 2][:, 0:m * P].rearrange("p (m t) -> p m t", m=m),
                               ACT.Copy).then_inc(evac, 1)

        @block.tensor
        def _(pe):
            for j, (i, t) in enumerate(jobs):
                pe.wait_ge(y_done, j + 1)
                if j >= 2:
                    pe.wait_ge(evac, j - 1)
                m = items[i]["heads"] // 2
                for k in range(m):
                    mm = pe.transpose(pt[j % 2][:, k * P:(k + 1) * P], work[j % 2][:, k * P:(k + 1) * P],
                                      tab[:, C_IDENT:C_IDENT + P])
                mm.then_inc(t_done, 1)


def attention_phase(nc, name, tab, jobs, bias=None):
    nj = len(jobs)
    for j in jobs:
        j["nt"] = j["keys"] // P
        j["na"] = min(j["nt"], 4)
    cum_v = np.cumsum([1 if j["nt"] > j["na"] else 0 for j in jobs]).tolist()
    with Scope(nc, name) as s:
        psS = [s.ps(f"score{i}", 2) for i in range(2)]
        psT = s.ps("turned", 2)
        psO = [s.ps(f"out{i}") for i in range(2)]
        pr = [s.sb(f"prob{i}", [P, 768]) for i in range(2)]
        prT = [s.sb(f"probT{i}", [P, 768]) for i in range(2)]
        mx = s.sb("max", [P, nj])
        nm = s.sb("negmax", [P, nj])
        sm = s.sb("sum", [P, nj])
        rs = s.sb("rsum", [P, nj])
        s_done, max_done, exp_done, t_done, ev_a, ev_v, pv_done, post_done, own = (
            s.sem(k) for k in ("s", "max", "exp", "t", "eva", "evv", "pv", "post", "own"))
        if bias:
            bload, bheads, per = bias["load"], bias["heads"], bias["per"]
            bt = [s.sb(f"bias{i}", [P, 16, 64]) for i in range(2)]
            b_in = [s.sem(f"bin{i}") for i in range(2)]
            b_ready = s.sem("bready")
        block = s.block()

        if bias:
            @block.sync
            def _(sp):
                for h in range(bheads):
                    if h >= 2:
                        sp.wait_ge(max_done, per * (h - 1))
                    for dst, src in bload(h, bt[h % 2]):
                        sp.dma_start(dst, src).then_inc(b_in[h % 2], 16)

        @block.tensor
        def _(pe):
            def scores(j):
                if j >= 2:
                    pe.wait_ge(exp_done, j - 1)
                jb = jobs[j]
                for c in range(0, jb["keys"], 512):
                    n = min(512, jb["keys"] - c)
                    mm = pe.matmul(psS[j % 2][:, c:c + n], jb["q"], jb["k"][:, c:c + n], start=True, stop=True)
                mm.then_inc(s_done, 1)

            def turn(j):
                pe.wait_ge(exp_done, j + 1)
                if j >= 1:
                    pe.wait_ge(ev_a, j)
                    if cum_v[j - 1]:
                        pe.wait_ge(ev_v, cum_v[j - 1])
                for k in range(jobs[j]["nt"]):
                    mm = pe.transpose(psT[:, k * P:(k + 1) * P], pr[j % 2][:, k * P:(k + 1) * P],
                                      tab[:, C_IDENT:C_IDENT + P])
                mm.then_inc(t_done, 1)

            def values(j):
                jb = jobs[j]
                pe.wait_ge(ev_a, j + 1)
                if cum_v[j]:
                    pe.wait_ge(ev_v, cum_v[j])
                if j >= 2:
                    pe.wait_ge(post_done, j - 1)
                for k in range(jb["nt"]):
                    mm = pe.matmul(psO[j % 2][:, 0:jb["dv"]], prT[j % 2][:, k * P:(k + 1) * P], jb["v"](k),
                                   start=(k == 0), stop=(k == jb["nt"] - 1))
                mm.then_inc(pv_done, 1)

            for j in range(nj + 2):
                if j < nj:
                    scores(j)
                if j >= 2:
                    values(j - 2)
                if 1 <= j <= nj:
                    turn(j - 1)

        @block.scalar
        def _(act):
            for j in range(nj + 1):
                if j >= 1:
                    i = j - 1
                    n = jobs[i]["na"] * P
                    act.wait_ge(t_done, i + 1)
                    if i >= 2:
                        act.wait_ge(pv_done, i - 1)
                    act.activation(prT[i % 2][:, 0:n], psT[:, 0:n], ACT.Copy).then_inc(ev_a, 1)
                if j < nj:
                    act.wait_ge(max_done, j + 1)
                    act.activation(pr[j % 2][:, 0:jobs[j]["keys"]], psS[j % 2][:, 0:jobs[j]["keys"]], ACT.Exp,
                                   bias=nm[:, j:j + 1], accum_out=sm[:, j:j + 1]).then_inc(exp_done, 1)

        @block.vector
        def _(v):
            link = Chain(v, own)
            for j in range(nj + 2):
                if j < nj:
                    jb = jobs[j]
                    if bias and j % per == 0:
                        h = j // per
                        v.wait_ge(b_in[h % 2], 16 * 2 * (h // 2 + 1))
                        cm = tab[:, C_COL:C_COL + HD].unsqueeze(1).to_broadcast([P, 14, HD])
                        link(v.tensor_tensor(bt[h % 2][:, 1:15, :], bt[h % 2][:, 1:15, :], cm, ALU.add))
                    v.wait_ge(s_done, j + 1)
                    for c, n, ap in jb["add"](bt[(j // per) % 2] if bias else None):
                        link(v.tensor_tensor(psS[j % 2][:, c:c + n], psS[j % 2][:, c:c + n], ap, ALU.add))
                    link(v.tensor_reduce(mx[:, j:j + 1], psS[j % 2][:, 0:jb["keys"]], AX.X, ALU.max))
                    v.tensor_scalar(nm[:, j:j + 1], mx[:, j:j + 1], -1.0, None, ALU.mult).then_inc(max_done, 1)
                if 1 <= j <= nj:
                    i = j - 1
                    a, b = jobs[i]["na"] * P, jobs[i]["nt"] * P
                    if b > a:
                        v.wait_ge(t_done, i + 1)
                        if i >= 2:
                            v.wait_ge(pv_done, i - 1)
                        v.tensor_copy(prT[i % 2][:, a:b], psT[:, a:b]).then_inc(ev_v, 1)
                if j >= 2:
                    i = j - 2
                    v.wait_ge(pv_done, i + 1)
                    link(v.reciprocal(rs[:, i:i + 1], sm[:, i:i + 1]))
                    jobs[i]["post"](v, link, psO[i % 2], rs[:, i:i + 1]).then_inc(post_done, 1)


def feature_phase(nc, name, hT, W, jobs, RAW=2):
    RING, BANKS = 2, 4
    PARTS = 4
    KQ = KD // PARTS
    chunks = sorted({j[0] // 2 for j in jobs})
    last_of = {c: max(i for i, j in enumerate(jobs) if j[0] // 2 == c) for c in chunks}
    with Scope(nc, name) as s:
        raw = [s.sb(f"raw{i}", [P, KD, 256]) for i in range(RAW)]
        w = [s.pair(f"w{i}", [P, KD, 256]) for i in range(RING)]
        banks = [s.ps(f"acc{i}") for i in range(BANKS)]
        raw_in = [[s.sem(f"w{i}{j}") for j in range(PARTS)] for i in range(RAW)]
        hi_done, lo_done, mm_done, ev = (s.sem(k) for k in ("hi", "lo", "mm", "ev"))
        block = s.block()

        @block.sync
        def _(sp):
            for c in chunks:
                src = W[:, c * 256:(c + 1) * 256].rearrange("(k p) n -> p k n", p=P)
                for j in range(PARTS):
                    if c >= RAW:
                        sp.wait_ge(lo_done, PARTS * (c - RAW) + j + 1)
                    ks = slice(j * KQ, (j + 1) * KQ)
                    sp.dma_start(raw[c % RAW][:, ks, :], src[:, ks, :]).then_inc(raw_in[c % RAW][j], 16)

        @block.tensor
        def _(pe):
            for i, (m, c0, n, _, _) in enumerate(jobs):
                c = m // 2
                if i >= BANKS:
                    pe.wait_ge(ev, i - BANKS + 1)
                for k in range(KD):
                    if k % KQ == 0:
                        pe.wait_ge(lo_done, PARTS * c + k // KQ + 1)
                    mm = products(pe, banks[i % BANKS][:, 0:n], [h[:, k, (m % 2) * P:(m % 2 + 1) * P] for h in w[c % RING]],
                                  [h[:, k, c0:c0 + n] for h in hT], k == 0, k == KD - 1)
                mm.then_inc(mm_done, 1)

        def free(eng, c):
            if c >= RING:
                eng.wait_ge(mm_done, last_of[c - RING] + 1)

        @block.scalar
        def _(act):
            for c in chunks:
                free(act, c)
                for j in range(PARTS):
                    ks = slice(j * KQ, (j + 1) * KQ)
                    act.wait_ge(raw_in[c % RAW][j], 16 * (c // RAW + 1))
                    split_hi(act, w[c % RING][0][:, ks, :], raw[c % RAW][:, ks, :]).then_inc(hi_done, 1)

        @block.vector
        def _(v):
            def copy_out(c):
                for i, (m, c0, n, dst, scale) in enumerate(jobs):
                    if m // 2 == c:
                        v.wait_ge(mm_done, i + 1)
                        v.tensor_scalar(dst, banks[i % BANKS][:, 0:n], scale, None, ALU.mult).then_inc(ev, 1)

            for c in chunks:
                for j in range(PARTS):
                    ks = slice(j * KQ, (j + 1) * KQ)
                    v.wait_ge(hi_done, PARTS * c + j + 1)
                    split_lo(v, w[c % RING][1][:, ks, :], raw[c % RAW][:, ks, :], w[c % RING][0][:, ks, :]).then_inc(lo_done, 1)
                if c >= 1:
                    copy_out(c - 1)
            copy_out(chunks[-1])


def rwkv_prepare(nc, tab, rtab, clear, pr, A, KR, BT, KDT, Vt, KDt, Bt, PC, bonus, gate):
    NPR = 4
    E05 = math.exp(-0.5)
    with Scope(nc, "rr") as s:
        par = s.sb("par", [P, 14 + 6 * NPR])
        w2 = s.sb("w2", [P, RW])
        g2 = s.sb("g2", [P, RW])
        a = s.sb("a", [P, NPR, SEQ])
        ld = s.sb("ld", [P, NPR, SEQ])
        cs = s.sb("cs", [P, NPR, SEQ])
        t1 = s.sb("t1", [P, SEQ])
        t2 = s.sb("t2", [P, SEQ])
        t3 = s.sb("t3", [P, SEQ])
        psA = [s.ps(f"a{i}") for i in range(4)]
        psB = s.ps("b")
        psT = [s.ps(f"t{i}") for i in range(2)]
        in_par, in_w, shift_done, low_done, lora_mm, lora_ev = (s.sem(k) for k in ("par", "w", "sh", "low", "lm", "le"))
        exps_in, exps_out, sq_done, sq_mm, kk_root, root_in = (s.sem(k) for k in ("ei", "eo", "sq", "sm", "kr", "ri"))
        prod_done, bon_mm, fact_done, t_done, t_ev, g_mm, v_own, a_own, z_ev = (
            s.sem(k) for k in ("pd", "bm", "fd", "td", "te", "gm", "vo", "ao", "ze"))
        mu0, W0, A0, KK, KA, RK = 0, 14, 18, 22, 26, 30
        block = s.block()

        def col(o):
            return par[:, o:o + 1]

        @block.sync
        def _(sp):
            sp.dma_start(par[:, 0:14], A["rwkv_mu"].rearrange("(m p) -> p m", p=P)).then_inc(in_par, 16)
            sp.dma_start(rtab[:, :], A["rwkv_table"]).then_inc(in_par, 16)
            for o, n in ((W0, "rwkv_w0"), (A0, "rwkv_a0"), (KK, "rwkv_k_k"), (KA, "rwkv_k_a"), (RK, "rwkv_r_k")):
                sp.dma_start(par[:, o:o + 4], A[n].rearrange("(m p) -> p m", p=P)).then_inc(in_par, 16)
            sp.dma_start(w2[0:64, :], A["rwkv_w2"]).then_inc(in_w, 16)
            sp.dma_start(w2[64:128, :], A["rwkv_a2"]).then_inc(in_w, 16)
            sp.dma_start(g2[:, :], A["rwkv_g2"]).then_inc(in_w, 16)
            clear.write(sp)

        @block.vector
        def _(v):
            link = Chain(v, v_own)
            clear.zero(v)
            v.wait_ge(in_par, 112)
            for n, m in enumerate([12, 13] + list(range(12))):
                x = pr[:, m, :]
                v.tensor_tensor(t1[:, 1:SEQ], x[:, 0:SEQ - 1], x[:, 1:SEQ], ALU.subtract).then_inc(v_own, 1)
                link.n += 1
                link(v.tensor_scalar(t1[:, 0:1], x[:, 0:1], -1.0, None, ALU.mult))
                v.scalar_tensor_tensor(out=x, in0=t1[:, :], scalar=col(mu0 + m), in1=x, op0=ALU.mult,
                                       op1=ALU.add).then_inc(shift_done, 1)
                v.wait_ge(shift_done, n + 1)
            for i in range(NPR):
                v.wait_ge(lora_ev, 2 * i + 1)
                link(v.tensor_scalar(ld[:, i, :], ld[:, i, :], -E05, None, ALU.mult))
                link(v.tensor_tensor_scan(cs[:, i, :], rtab[:, R_SCAN:R_SCAN + SEQ], ld[:, i, :], 0.0, ALU.mult, ALU.add))
                v.tensor_tensor(ld[:, i, :], cs[:, i, :], ld[:, i, :], ALU.subtract).then_inc(exps_in, 1)
                k, r = pr[:, 4 + i, :], pr[:, i, :]
                kk = t1[:, :]
                link(v.tensor_scalar(kk, k, col(KK + i), None, ALU.mult))
                if i >= 1:
                    v.wait_ge(sq_mm, i)
                v.tensor_tensor(t2[:, :], kk, kk, ALU.mult).then_inc(sq_done, 1)
                v.wait_ge(kk_root, i + 1)
                link(v.tensor_scalar(t3[:, :], t3[:, :], 1e-12, None, ALU.max))
                link(v.reciprocal(t3[:, :], t3[:, :]))
                link(v.tensor_tensor(kk, kk, t3[:, :], ALU.mult))
                v.wait_ge(lora_ev, 2 * i + 2)
                link(v.tensor_scalar(t2[:, :], a[:, i, :], 1.0, col(KA + i), ALU.subtract, ALU.mult))
                link(v.scalar_tensor_tensor(out=k, in0=t2[:, :], scalar=1.0, in1=k, op0=ALU.add, op1=ALU.mult))
                link(v.tensor_tensor(t2[:, :], r, k, ALU.mult))
                if i >= 1:
                    v.wait_ge(bon_mm, i)
                v.tensor_scalar(t3[:, :], t2[:, :], col(RK + i), None, ALU.mult).then_inc(prod_done, 1)
                link(v.tensor_tensor(a[:, i, :], a[:, i, :], kk, ALU.mult))
                v.wait_ge(exps_out, i + 1)
                v.tensor_copy(PC[:, i, :], KR[:, i, 1, :].rearrange("p (c t) -> p c t", t=CH)[:, :, CH - 1]).then_inc(v_own, 1)
                link.n += 1
                v.wait_ge(v_own, link.n)
                link(v.tensor_tensor(KR[:, i, 0, :], KR[:, i, 0, :], kk, ALU.mult))
                link(v.tensor_tensor(KR[:, i, 1, :], KR[:, i, 1, :], r, ALU.mult))
                link(v.tensor_tensor(KDT[:, i, :], BT[:, i, :], k, ALU.mult))
                v.tensor_tensor(BT[:, i, :], BT[:, i, :], a[:, i, :], ALU.mult).then_inc(fact_done, 1)
                v.wait_ge(bon_mm, i + 1)
            v.wait_ge(bon_mm, NPR)
            v.tensor_copy(bonus[:, :], psB[:, 0:32]).then_inc(v_own, 1)
            for t in range(NT):
                v.wait_ge(g_mm, t + 1)
                v.tensor_copy(gate[:, t, :], psA[t][:, :]).then_inc(v_own, 1)

        @block.scalar
        def _(act):
            act.wait_ge(shift_done, 2)
            act.activation(pr[0:64, 12, :], pr[0:64, 12, :], ACT.Tanh).then_inc(low_done, 1)
            act.activation(pr[:, 13, :], pr[:, 13, :], ACT.Sigmoid).then_inc(low_done, 1)
            for i in range(NPR):
                act.wait_ge(lora_mm, 2 * i + 1)
                act.activation(ld[:, i, :], psA[(2 * i) % 4][:, :], ACT.Sigmoid, bias=col(W0 + i)).then_inc(lora_ev, 1)
                act.wait_ge(lora_mm, 2 * i + 2)
                act.activation(a[:, i, :], psA[(2 * i + 1) % 4][:, :], ACT.Sigmoid, bias=col(A0 + i)).then_inc(lora_ev, 1)
            for i in range(NPR):
                act.wait_ge(exps_in, i + 1)
                act.activation(KR[:, i, 1, :], cs[:, i, :], ACT.Exp).then_inc(a_own, 1)
                act.activation(KR[:, i, 0, :], ld[:, i, :], ACT.Exp).then_inc(a_own, 1)
                act.activation(BT[:, i, :], cs[:, i, :], ACT.Exp, scale=-1.0).then_inc(exps_out, 1)
                act.wait_ge(sq_mm, i + 1)
                if i >= 1:
                    act.wait_ge(bon_mm, i)
                act.activation(t3[:, :], psT[i % 2][:, :], ACT.Sqrt).then_inc(kk_root, 1)
            for n in range(3 * NT):
                src, t = divmod(n, NT)
                act.wait_ge(t_done, n + 1)
                dst = (Vt, KDt, Bt)[src]
                act.activation(dst[:, t, :], psT[n % 2][:, :], ACT.Copy, scale=(-1.0 if src == 2 else 1.0)).then_inc(t_ev, 1)

        @block.tensor
        def _(pe):
            pe.wait_ge(in_w, 48)
            pe.wait_ge(low_done, 2)
            for i in range(NPR):
                for half in range(2):
                    n = 2 * i + half
                    if n >= 4:
                        pe.wait_ge(lora_ev, n - 3)
                    rows = slice(64 * half, 64 * half + 64)
                    pe.matmul(psA[n % 4][:, :], w2[rows, i * P:(i + 1) * P], pr[rows, 12, :], start=True,
                              stop=True).then_inc(lora_mm, 1)
            for i in range(NPR):
                pe.wait_ge(sq_done, i + 1)
                if i >= 2:
                    pe.wait_ge(kk_root, i - 1)
                pe.matmul(psT[i % 2][:, :], tab[:, C_BLK:C_BLK + P], t2[:, :], start=True, stop=True).then_inc(sq_mm, 1)
                pe.wait_ge(prod_done, i + 1)
                for t in range(NT):
                    mm = pe.matmul(psB[:, t * 8 + 2 * i:t * 8 + 2 * i + 2], t3[:, t * P:(t + 1) * P],
                                   tab[:, C_HIND:C_HIND + 2], start=True, stop=True)
                mm.then_inc(bon_mm, 1)
            pe.wait_ge(lora_ev, 8)
            for t in range(NT):
                pe.matmul(psA[t][:, :], pr[:, 13, t * P:(t + 1) * P], g2[:, :], start=True, stop=True).then_inc(g_mm, 1)
            pe.wait_ge(fact_done, NPR)
            pe.wait_ge(kk_root, NPR)
            for n in range(3 * NT):
                src, t = divmod(n, NT)
                if n >= 2:
                    pe.wait_ge(t_ev, n - 1)
                for i in range(NPR):
                    x = (pr[:, 8 + i, :], KDT[:, i, :], BT[:, i, :])[src]
                    mm = pe.transpose(psT[n % 2][:, i * P:(i + 1) * P], x[:, t * P:(t + 1) * P], tab[:, C_IDENT:C_IDENT + P])
                mm.then_inc(t_done, 1)


def rwkv_chunks(nc, tab, rtab, KR, BT, KDT, U):
    NU = 32
    with Scope(nc, "rc") as s:
        ps = [s.ps(f"m{i}") for i in range(2)]
        mm_done, ev = s.sem("mm"), s.sem("ev")
        block = s.block()

        @block.tensor
        def _(pe):
            for u in range(NU):
                t, h = divmod(u, 8)
                i, hp = h // 2, 64 * (h % 2)
                if u >= 2:
                    pe.wait_ge(ev, u - 1)
                rhs = KR[hp:hp + 64, i, :, t * P:(t + 1) * P]
                pe.matmul(ps[u % 2][:, 0:256], BT[hp:hp + 64, i, t * P:(t + 1) * P], rhs, start=True, stop=True)
                pe.matmul(ps[u % 2][:, 256:512], KDT[hp:hp + 64, i, t * P:(t + 1) * P], rhs, start=True,
                          stop=True).then_inc(mm_done, 1)

        @block.vector
        def _(v):
            for u in range(NU):
                v.wait_ge(mm_done, u + 1)
                v.tensor_tensor(U[:, u, :], ps[u % 2][:, :], rtab[:, R_UNIT:R_UNIT + 512], ALU.mult).then_inc(ev, 1)

    with Scope(nc, "ri") as s:
        G = 2
        NB = NU // 4
        X = [s.sb(f"x{i}", [P, 4, P]) for i in range(G)]
        XT = [s.sb(f"xt{i}", [P, 4, P]) for i in range(G)]
        LT = [s.sb(f"lt{i}", [P, 4, P]) for i in range(G)]
        Y = [s.sb(f"y{i}", [P, 4, P]) for i in range(G)]
        p1 = [s.ps(f"p1{i}") for i in range(G)]
        p2 = [s.ps(f"p2{i}") for i in range(G)]
        p3 = [s.ps(f"p3{i}") for i in range(G)]
        lt_done, m1, y_done, m2, x_done = ([s.sem(f"{k}{i}") for i in range(G)] for k in ("lt", "m1", "y", "m2", "x"))
        own = s.sem("own")
        block = s.block()
        steps = [(b, l) for r in range(NB // G) for l in range(LVL) for b in range(r * G, (r + 1) * G)]

        @block.gpsimd
        def _(pool):
            for b, l in steps:
                g = b % G
                n = (b // G) * LVL + l
                if n >= 1:
                    pool.wait_ge(m1[g], n)
                mask = rtab[:, R_LVL + l * P:R_LVL + (l + 1) * P].unsqueeze(1).to_broadcast([P, 4, P])
                pool.tensor_tensor(LT[g][:, :, :], U[:, 4 * b:4 * b + 4, 0:P], mask, ALU.mult).then_inc(lt_done[g], 1)

        @block.tensor
        def _(pe):
            def first(b, l):
                g, n = b % G, (b // G) * LVL + l
                pe.wait_ge(lt_done[g], n + 1)
                pe.wait_ge(x_done[g], n + 1 + b // G)
                for j in range(4):
                    mm = pe.matmul(p1[g][:, j * P:(j + 1) * P], LT[g][:, j, :], X[g][:, j, :], start=True, stop=True)
                mm.then_inc(m1[g], 1)

            def second(b, l):
                g, n = b % G, (b // G) * LVL + l
                pe.wait_ge(y_done[g], n + 1)
                for j in range(4):
                    pe.matmul(p2[g][:, j * P:(j + 1) * P], XT[g][:, j, :], Y[g][:, j, :], start=True, stop=True)
                for j in range(4):
                    mm = pe.matmul(p3[g][:, j * P:(j + 1) * P], Y[g][:, j, :], XT[g][:, j, :], start=True, stop=True)
                mm.then_inc(m2[g], 1)

            for k in range(0, len(steps), G):
                for b, l in steps[k:k + G]:
                    first(b, l)
                for b, l in steps[k:k + G]:
                    second(b, l)

        @block.scalar
        def _(act):
            for b, l in steps:
                g, n = b % G, (b // G) * LVL + l
                act.wait_ge(m1[g], n + 1)
                act.activation(Y[g][:, :, :], p1[g][:, :].rearrange("p (j t) -> p j t", j=4), ACT.Copy).then_inc(y_done[g], 1)

        @block.vector
        def _(v):
            link = Chain(v, own)
            I4 = tab[:, C_IDENT:C_IDENT + P].unsqueeze(1).to_broadcast([P, 4, P])

            def start(b):
                g = b % G
                link(v.tensor_copy(X[g][:, :, :], I4))
                v.tensor_copy(XT[g][:, :, :], I4).then_inc(x_done[g], 1)

            for b in range(G):
                start(b)
            for b, l in steps:
                g, n = b % G, (b // G) * LVL + l
                v.wait_ge(m2[g], n + 1)
                v.wait_ge(x_done[g], n + 1 + b // G)
                d2, d3 = (q[g][:, :].rearrange("p (j t) -> p j t", j=4) for q in (p2, p3))
                if l < LVL - 1:
                    link(v.tensor_tensor(X[g][:, :, :], X[g][:, :, :], d2, ALU.subtract))
                    v.tensor_tensor(XT[g][:, :, :], XT[g][:, :, :], d3, ALU.subtract).then_inc(x_done[g], 1)
                else:
                    v.tensor_tensor(U[:, 4 * b:4 * b + 4, 0:P], XT[g][:, :, :], d3, ALU.subtract).then_inc(x_done[g], 1)
                    if b + G < NB:
                        start(b + G)


def rwkv_scan(nc, tab, U, KR, Vt, KDt, Bt, PC, y):
    PW = 2 * HD
    with Scope(nc, "rs") as s:
        ST = s.sb("state", [P, 4, PW])
        R = s.sb("R", [P, RW])
        Uc = [s.sb(f"U{i}", [P, RW]) for i in range(2)]
        Vc = [s.sb(f"V{i}", [P, RW]) for i in range(2)]
        PM = s.sb("PM", [P, 4, PW])
        tmp = s.sb("tmp", [P, 4, PW])
        psR, psU, psY, psS = (s.ps(k) for k in "RUYS")
        st_done, zeroed, v_ready, pm_ready, r_mm, r_ev, u_mm, u_ev, y_mm, y_ev, s_mm, own = (
            s.sem(k) for k in ("st", "zero", "vr", "pm", "rm", "re", "um", "ue", "ym", "ye", "sm", "own"))
        block = s.block()

        @block.gpsimd
        def _(pool):
            pool.wait_ge(zeroed, 5)
            for c in range(NCH):
                t, q = divmod(c, 2)
                rows = slice(64 * q, 64 * q + 64)
                if c >= 2:
                    pool.wait_ge(y_mm, c - 1)
                    pool.wait_ge(pm_ready, c)
                elif c:
                    pool.wait_ge(pm_ready, c)
                pool.tensor_copy(Vc[q][rows, :], Vt[rows, t, :]).then_inc(v_ready, 1)
                pool.wait_ge(v_ready, c + 1)
                if c >= 1:
                    pool.wait_ge(st_done, c + 1)
                pool.tensor_tensor(PM[:, :, :], tab[:, C_BLK:C_BLK + P].unsqueeze(1).to_broadcast([P, 4, PW]),
                                   PC[:, :, c:c + 1].to_broadcast([P, 4, PW]), ALU.mult).then_inc(pm_ready, 1)

        @block.tensor
        def _(pe):
            for c in range(NCH):
                t, q = divmod(c, 2)
                p0 = 64 * q
                ts = slice(c * CH, (c + 1) * CH)
                rows = slice(p0, p0 + 64)

                def unit(h, j):
                    return U[:, t * 8 + h, j * P + p0:j * P + p0 + 64]

                pe.wait_ge(st_done, c + 1)
                pe.wait_ge(v_ready, c + 1)
                if c:
                    pe.wait_ge(r_ev, c)
                for i in range(4):
                    pc = slice(i * PW, (i + 1) * PW)
                    pe.matmul(psR[rows, pc], KR[:, i, 0, ts], ST[:, i, :], start=True, stop=False)
                    for h in (2 * i, 2 * i + 1):
                        hc = slice(h * HD, (h + 1) * HD)
                        mm = pe.matmul(psR[rows, hc], unit(h, 2), Vc[q][:, hc], start=False, stop=(h % 2 == 1))
                mm.then_inc(r_mm, 1)
                pe.wait_ge(r_ev, c + 1)
                if c:
                    pe.wait_ge(u_ev, c)
                for h in range(8):
                    hc = slice(h * HD, (h + 1) * HD)
                    mm = pe.matmul(psU[rows, hc], unit(h, 0), R[:, hc], start=True, stop=True)
                mm.then_inc(u_mm, 1)
                pe.wait_ge(u_ev, c + 1)
                for i in range(4):
                    pc = slice(i * PW, (i + 1) * PW)
                    pe.matmul(psS[:, pc], KDt[:, t, pc], Vc[q][:, pc], start=True, stop=False)
                    mm = pe.matmul(psS[:, pc], Bt[:, t, pc], Uc[q][:, pc], start=False, stop=True)
                mm.then_inc(s_mm, 1)
                if c:
                    pe.wait_ge(y_ev, c)
                for i in range(4):
                    pc = slice(i * PW, (i + 1) * PW)
                    pe.matmul(psY[rows, pc], KR[:, i, 1, ts], ST[:, i, :], start=True, stop=False)
                    for h in (2 * i, 2 * i + 1):
                        hc = slice(h * HD, (h + 1) * HD)
                        pe.matmul(psY[rows, hc], unit(h, 3), Vc[q][:, hc], start=False, stop=False)
                        mm = pe.matmul(psY[rows, hc], unit(h, 1), Uc[q][:, hc], start=False, stop=(h % 2 == 1))
                mm.then_inc(y_mm, 1)

        @block.scalar
        def _(act):
            act.wait_ge(zeroed, 5)
            for c in range(NCH):
                t, q = divmod(c, 2)
                rows = slice(64 * q, 64 * q + 64)
                act.wait_ge(r_mm, c + 1)
                act.activation(R[rows, :], psR[rows, :], ACT.Copy).then_inc(r_ev, 1)
                act.wait_ge(y_mm, c + 1)
                act.activation(y[rows, t, :], psY[rows, :], ACT.Copy).then_inc(y_ev, 1)

        @block.vector
        def _(v):
            link = Chain(v, own)
            for z in (R, Uc[0], Uc[1], Vc[0], Vc[1]):
                v.memset(z[:, :], 0.0).then_inc(zeroed, 1)
            v.memset(ST[:, :, :], 0.0).then_inc(st_done, 1)
            v.wait_ge(st_done, 1)
            v.wait_ge(zeroed, 5)
            for c in range(NCH):
                q = c % 2
                rows = slice(64 * q, 64 * q + 64)
                v.wait_ge(u_mm, c + 1)
                v.tensor_copy(Uc[q][rows, :], psU[rows, :]).then_inc(u_ev, 1)
                v.wait_ge(s_mm, c + 1)
                link(v.tensor_tensor(tmp[:, :, :], psS[:, :].rearrange("p (i v) -> p i v", i=4), ST[:, :, :], ALU.add))
                v.wait_ge(y_mm, c + 1)
                v.wait_ge(pm_ready, c + 1)
                v.tensor_tensor(ST[:, :, :], tmp[:, :, :], PM[:, :, :], ALU.mult).then_inc(st_done, 1)
                v.wait_ge(st_done, c + 2)


def rwkv_finish(nc, tab, A, clear, y, Vt, bonus, gate):
    with Scope(nc, "rf") as s:
        lw = s.sb("lnw", [P, RW])
        lb = s.sb("lnb", [P, RW])
        sq = s.sb("sq", [P, NT, RW])
        st = s.sb("st", [P, 3, NT * 8])
        ld, ss, root, own = (s.sem(k) for k in ("ld", "ss", "root", "own"))
        block = s.block()

        @block.sync
        def _(sp):
            sp.dma_start(lw[:, :], bc_row(A["rwkv_ln_w"], RW)).then_inc(ld, 16)
            sp.dma_start(lb[:, :], bc_row(A["rwkv_ln_b"], RW)).then_inc(ld, 16)
            clear.end(sp)

        @block.scalar
        def _(act):
            act.wait_ge(ss, 1)
            act.activation(st[:, 2, :], st[:, 1, :], ACT.Sqrt).then_inc(root, 1)

        @block.vector
        def _(v):
            link = Chain(v, own)
            y3 = y[:, :, :].rearrange("p t (h d) -> p (t h) d", d=HD)
            q3 = sq[:, :, :].rearrange("p t (h d) -> p (t h) d", d=HD)
            wide = [P, NT * 8, HD]
            link(v.tensor_reduce(st[:, 0, :], y3, AX.X, ALU.add))
            link(v.tensor_scalar(st[:, 0, :], st[:, 0, :], 1.0 / HD, None, ALU.mult))
            link(v.tensor_tensor(y3, y3, st[:, 0, :].unsqueeze(2).to_broadcast(wide), ALU.subtract))
            link(v.tensor_tensor(q3, y3, y3, ALU.mult))
            link(v.tensor_reduce(st[:, 1, :], q3, AX.X, ALU.add))
            link(v.tensor_scalar(st[:, 1, :], st[:, 1, :], 1.0 / HD, GN_EPS, ALU.mult, ALU.add))
            v.tensor_copy(st[0:1, 0, 0:1], st[0:1, 1, 0:1]).then_inc(ss, 1)
            v.wait_ge(root, 1)
            link(v.reciprocal(st[:, 1, :], st[:, 2, :]))
            link(v.tensor_tensor(y3, y3, st[:, 1, :].unsqueeze(2).to_broadcast(wide), ALU.mult))
            v.wait_ge(ld, 32)
            link(v.tensor_tensor(y[:, :, :], y[:, :, :], lw[:, :].unsqueeze(1).to_broadcast([P, NT, RW]), ALU.mult))
            link(v.tensor_tensor(y[:, :, :], y[:, :, :], lb[:, :].unsqueeze(1).to_broadcast([P, NT, RW]), ALU.add))
            v3 = Vt[:, :, :].rearrange("p t (h d) -> p (t h) d", d=HD)
            link(v.tensor_tensor(q3, v3, bonus[:, :].unsqueeze(2).to_broadcast(wide), ALU.mult))
            link(v.tensor_tensor(y[:, :, :], y[:, :, :], sq[:, :, :], ALU.add))
            link(v.tensor_tensor(gate[:, :, :], y[:, :, :], gate[:, :, :], ALU.mult))


def route_phase(nc, name, tab, hT, nt, wg, bg, we, be, wts, slots, ovid, nov):
    NL = NG + NE
    with Scope(nc, name) as s:
        wr = s.sb("wr", [P, KD, NL])
        br = s.sb("br", [P, NL])
        L = s.sb("L", [P, nt, NL])
        G8 = s.sb("G8", [P, nt, 8])
        gm, em = s.sb("gm", [P, nt, 8]), s.sb("em", [P, nt, 8])
        gi, ei = s.sb("gi", [P, nt, 8], U32), s.sb("ei", [P, nt, 8], U32)
        gf, ef = s.sb("gf", [P, nt]), s.sb("ef", [P, nt, 2])
        goh = s.sb("goh", [P, nt, NG])
        ge = s.sb("ge", [P, nt, NG])
        gs = s.sb("gs", [P, nt])
        emk = s.sb("emk", [P, nt, NG, EPG])
        es = s.sb("es", [P, nt, EPG])
        e2 = s.sb("e2", [P, nt])
        oh = [s.sb(f"oh{k}", [P, nt, NE]) for k in range(2)]
        oh01 = s.sb("oh01", [P, nt, NE])
        cum = s.sb("cum", [P, nt, NE])
        z = s.sb("z", [P, nt, NE])
        cnt, nb, inc_, dlt = (s.sb(k, [P, NE]) for k in ("cnt", "nb", "inc", "dlt"))
        sf = s.sb("sf", [P, nt, 2])
        oc = s.sb("oc", [P, MAXOV, NE])
        of = s.sb("of", [P, MAXOV])
        nf = s.sb("nf", [P, 1])
        psL, psC = s.ps("L"), s.ps("C")
        ld, lg, ev, a_in, a_out, oh_done, c_mm, own = (s.sem(k) for k in ("ld", "lg", "ev", "ai", "ao", "oh", "cm", "own"))
        block = s.block()

        @block.sync
        def _(sp):
            sp.dma_start(wr[:, :, 0:NG], wg.rearrange("(k p) n -> p k n", p=P)).then_inc(ld, 16)
            sp.dma_start(wr[:, :, NG:NL], we.rearrange("(k p) n -> p k n", p=P)).then_inc(ld, 16)
            sp.dma_start(br[:, 0:NG], bc_row(bg, NG)).then_inc(ld, 16)
            sp.dma_start(br[:, NG:NL], bc_row(be, NE)).then_inc(ld, 16)

        @block.tensor
        def _(pe):
            pe.wait_ge(ld, 64)
            for t in range(nt):
                for k in range(KD):
                    mm = pe.matmul(psL[:, t * NL:(t + 1) * NL], hT[:, k, t * P:(t + 1) * P], wr[:, k, :],
                                   start=(k == 0), stop=(k == KD - 1))
            mm.then_inc(lg, 1)
            pe.wait_ge(oh_done, 1)
            for t in range(nt):
                for u in range(t + 1):
                    w = C_TRI if u == t else C_ONES
                    pe.matmul(psC[:, t * NE:(t + 1) * NE], tab[:, w:w + P], oh01[:, u, :], start=(u == 0), stop=(u == t))
            for u in range(nt):
                mm = pe.matmul(psC[:, nt * NE:(nt + 1) * NE], tab[:, C_ONES:C_ONES + P], oh01[:, u, :],
                               start=(u == 0), stop=(u == nt - 1))
            mm.then_inc(c_mm, 1)

        @block.scalar
        def _(act):
            act.wait_ge(a_in, 1)
            act.activation(ge[:, :, :], ge[:, :, :], ACT.Exp).then_inc(a_out, 1)
            act.wait_ge(a_in, 2)
            act.activation(e2[:, :], e2[:, :], ACT.Exp).then_inc(a_out, 1)

        @block.vector
        def _(v):
            link = Chain(v, own)
            io = tab[:, C_IO:C_IO + NE]
            link(v.memset(G8[:, :, :], NEG))
            v.wait_ge(lg, 1)
            v.wait_ge(ld, 64)
            link(v.tensor_tensor(L[:, :, :], psL[:, 0:nt * NL].rearrange("p (t n) -> p t n", n=NL),
                                 br[:, :].unsqueeze(1).to_broadcast([P, nt, NL]), ALU.add))
            link(v.tensor_copy(G8[:, :, 0:NG], L[:, :, 0:NG]))
            for t in range(nt):
                link(v.max(gm[:, t, :], G8[:, t, :]))
                link(v.max_index(gi[:, t, :], gm[:, t, :], G8[:, t, :]))
            link(v.tensor_copy(gf[:, :], gi[:, :, 0]))
            link(v.tensor_tensor(goh[:, :, :], io[:, 0:NG].unsqueeze(1).to_broadcast([P, nt, NG]),
                                 gf[:, :].unsqueeze(2).to_broadcast([P, nt, NG]), ALU.is_equal))
            v.tensor_tensor(ge[:, :, :], L[:, :, 0:NG], gm[:, :, 0:1].to_broadcast([P, nt, NG]),
                            ALU.subtract).then_inc(a_in, 1)
            for t in range(nt):
                link(v.tensor_tensor(emk[:, t, :, :], L[:, t, NG:NL].rearrange("p (g j) -> p g j", j=EPG),
                                     goh[:, t, :].unsqueeze(2).to_broadcast([P, NG, EPG]), ALU.mult))
                link(v.tensor_reduce(es[:, t, :], emk[:, t, :, :].rearrange("p g j -> p j g"), AX.X, ALU.add))
                link(v.max(em[:, t, :], es[:, t, :]))
                link(v.max_index(ei[:, t, :], em[:, t, :], es[:, t, :]))
            v.tensor_tensor(e2[:, :], em[:, :, 1], em[:, :, 0], ALU.subtract).then_inc(a_in, 1)
            link(v.tensor_copy(ef[:, :, :], ei[:, :, 0:2]))
            link(v.scalar_tensor_tensor(out=ef[:, :, :], in0=gf[:, :].unsqueeze(2).to_broadcast([P, nt, 2]), scalar=float(EPG),
                                        in1=ef[:, :, :], op0=ALU.mult, op1=ALU.add))
            for k in range(2):
                link(v.tensor_tensor(oh[k][:, :, :], io.unsqueeze(1).to_broadcast([P, nt, NE]),
                                     ef[:, :, k:k + 1].to_broadcast([P, nt, NE]), ALU.is_equal))
            v.tensor_tensor(oh01[:, :, :], oh[0][:, :, :], oh[1][:, :, :], ALU.add).then_inc(oh_done, 1)
            v.wait_ge(a_out, 2)
            link(v.tensor_reduce(gs[:, :], ge[:, :, :], AX.X, ALU.add))
            link(v.scalar_tensor_tensor(out=gs[:, :], in0=e2[:, :], scalar=1.0, in1=gs[:, :], op0=ALU.add, op1=ALU.mult))
            link(v.reciprocal(wts[:, :, 0], gs[:, :]))
            link(v.tensor_tensor(wts[:, :, 1], wts[:, :, 0], e2[:, :], ALU.mult))
            v.wait_ge(c_mm, 1)
            link(v.tensor_copy(cum[:, :, :], psC[:, 0:nt * NE].rearrange("p (t e) -> p t e", e=NE)))
            link(v.tensor_copy(cnt[:, :], psC[:, nt * NE:(nt + 1) * NE]))
            link(v.tensor_scalar(nb[:, :], cnt[:, :], float(P), None, ALU.is_gt))
            for m in range(2, nt):
                link(v.scalar_tensor_tensor(out=nb[:, :], in0=cnt[:, :], scalar=float(m * P), in1=nb[:, :],
                                            op0=ALU.is_gt, op1=ALU.add))
            link(v.tensor_tensor_scan(inc_[:, :], tab[:, C_ONES:C_ONES + NE], nb[:, :], 0.0, ALU.mult, ALU.add))
            link(v.tensor_tensor(dlt[:, :], inc_[:, :], nb[:, :], ALU.subtract))
            link(v.tensor_tensor(dlt[:, :], dlt[:, :], io, ALU.subtract))
            link(v.tensor_scalar(dlt[:, :], dlt[:, :], float(NE - 1), float(P), ALU.add, ALU.mult))
            link(v.tensor_scalar(z[:, :, :], cum[:, :, :], float(P), None, ALU.is_ge))
            link(v.tensor_tensor(z[:, :, :], z[:, :, :], dlt[:, :].unsqueeze(1).to_broadcast([P, nt, NE]), ALU.mult))
            link(v.tensor_tensor(z[:, :, :], z[:, :, :], cum[:, :, :], ALU.add))
            link(v.scalar_tensor_tensor(out=z[:, :, :], in0=io.unsqueeze(1).to_broadcast([P, nt, NE]), scalar=float(P),
                                        in1=z[:, :, :], op0=ALU.mult, op1=ALU.add))
            for k in range(2):
                link(v.tensor_tensor(oh[k][:, :, :], oh[k][:, :, :], z[:, :, :], ALU.mult))
                link(v.tensor_reduce(sf[:, :, k], oh[k][:, :, :], AX.X, ALU.add))
            link(v.tensor_copy(slots[:, :, :], sf[:, :, :]))
            jj = tab[:, C_IO:C_IO + MAXOV].unsqueeze(2).to_broadcast([P, MAXOV, NE])
            link(v.tensor_tensor(oc[:, :, :], inc_[:, :].unsqueeze(1).to_broadcast([P, MAXOV, NE]), jj, ALU.is_le))
            link(v.tensor_reduce(of[:, :], oc[:, :, :], AX.X, ALU.add))
            link(v.tensor_scalar(of[:, :], of[:, :], float(NE - 1), None, ALU.min))
            link(v.tensor_copy(ovid[:, :], of[:, :]))
            link(v.tensor_copy(nf[:, :], inc_[:, NE - 1:NE]))
            link(v.tensor_copy(nov[:, :], nf[:, :]))


def scatter_phase(nc, name, htok, nt, slots, xbuf):
    with Scope(nc, name) as s:
        sent = s.sem("sent")
        block = s.block()

        @block.gpsimd
        def _(pool):
            for t in range(nt):
                for k in range(2):
                    pool.indirect_dma_start(out=xbuf, out_offset=bass.IndirectOffsetOnAxis(ap=slots[:, t, k:k + 1], axis=0),
                                            in_=htok[:, t, :], in_offset=None).then_inc(sent, 16)
            pool.wait_ge(sent, 32 * nt)


class Stream:

    PIECES = 6
    COLS = KD * FF // 2

    def __init__(self, s, w1, w3, w2):
        self.raw = [s.sb(f"raw{i}", [P, self.COLS]) for i in range(self.PIECES)]
        self.raw_in = [s.sem(f"raw{i}") for i in range(self.PIECES)]
        self.src = [w.rearrange("e (p k) n -> e p (k n)", p=P)[:, :, i * self.COLS:(i + 1) * self.COLS]
                    for w in (w1, w3, w2) for i in range(2)]

    def first(self, sp):
        for i in range(self.PIECES):
            sp.dma_start(self.raw[i][:, :], self.src[i][0]).then_inc(self.raw_in[i], 16)


def experts_phase(nc, name, tab, stream, w1d, w3d, w2d, xbuf, ybuf, ovid, nov):
    R1 = w1d.rearrange("e (k p) n -> e p k n", p=P)
    R3 = w3d.rearrange("e (k p) n -> e p k n", p=P)
    R2 = w2d.rearrange("e (k p) n -> e p k n", p=P)
    xb = xbuf.rearrange("(b p) d -> b p d", p=P)
    yb = ybuf.rearrange("(b p) d -> b p d", p=P)
    ident = tab[:, C_IDENT:C_IDENT + P]
    NP, PAIRS = stream.PIECES, NE // 2
    raw, raw_in = stream.raw, stream.raw_in
    with Scope(nc, name) as s:
        w = [s.pair(f"w{i}", [P, stream.COLS]) for i in range(NP)]
        xin = s.sb("xin", [P, D])
        xT = [s.pair(f"xT{i}", [P, D]) for i in range(2)]
        hT = s.pair("hT", [P, FF])
        sg = s.sb("sig", [P, FF])
        h = s.sb("h", [P, FF])
        y = s.sb("y", [P, D])
        pg, pu, ph = s.ps("gate"), s.ps("up"), s.ps("hT")
        px, py = s.ps("xT", 2), s.ps("y", 2)
        hi, lo, used = ([s.sem(f"{k}{i}") for i in range(NP)] for k in ("hi", "lo", "used"))
        x_in, xt_done, xt_hi, xt_lo, sig_done, h_done = (s.sem(k) for k in ("xin", "xt", "xth", "xtl", "sig", "h"))
        ht_done, ht_hi, ht_lo, y_a, y_v, y_out = (s.sem(k) for k in ("ht", "hth", "htl", "ya", "yv", "yo"))
        block = s.block()

        @block.sync
        def _(sp):
            def hold(sem, value):
                sp.wait_ge(sem, value)
                sp.wait_ge(sem, 1)

            sp.dma_start(xin[:, :], xb[0]).then_inc(x_in, 16)
            sp.wait_ge(xt_done, 1)
            sp.dma_start(xin[:, :], xb[1]).then_inc(x_in, 16)
            with sp.Fori(1, NE) as i:
                for j in range(NP):
                    e = sp.snap(i + 0)
                    hold(lo[j], e)
                    src = stream.src[j][bass.ds(e, 1), :, :].rearrange("e p n -> p (e n)")
                    sp.dma_start(raw[j][:, :], src).then_inc(raw_in[j], 16)
                    if j == 0:
                        nxt = sp.snap(i + 1)
                        hold(xt_done, nxt)
                        sp.dma_start(xin[:, :], xb[bass.ds(nxt, 1), :, :].rearrange("b p d -> p (b d)")).then_inc(x_in, 16)
            sp.wait_ge(x_in, 16 * (NE + 1))

        @block.tensor
        def _(pe):
            def turn_x(n):
                pe.wait_ge(x_in, 16 * n)
                if not isinstance(n, int) or n > 1:
                    pe.wait_ge(xt_lo, n - 1)
                cols = xin[:, :].rearrange("t (p k) -> t k p", k=KD)
                for k in range(KD):
                    mm = pe.transpose(px[:, k * P:(k + 1) * P], cols[:, k, :], ident)
                mm.then_inc(xt_done, 1)

            def turn_h(n):
                pe.wait_ge(h_done, n)
                cols = h[:, :].rearrange("t (p k) -> t k p", k=KF)
                for k in range(KF):
                    mm = pe.transpose(ph[:, k * P:(k + 1) * P], cols[:, k, :], ident)
                mm.then_inc(ht_done, 1)

            def up(out, q, j, ks):
                for k in ks:
                    kk = 4 * (j % 2) + k
                    mm = products(pe, out[:, :], [t[:, kk * P:(kk + 1) * P] for t in xT[q]],
                                  [t[:, k * FF:(k + 1) * FF] for t in w[j]], kk == 0, kk == KD - 1)
                return mm

            def down(n, past):
                pe.wait_ge(ht_lo, n)
                if past > 1:
                    pe.wait_ge(y_a, n - 1)
                    pe.wait_ge(y_v, n - 1)
                for j in (4, 5):
                    pe.wait_ge(lo[j], n)
                    for half in range(2):
                        for k in range(2):
                            kk = 2 * (j - 4) + k
                            c = k * D + half * 512
                            mm = products(pe, py[:, half * 512:(half + 1) * 512], [t[:, kk * P:(kk + 1) * P] for t in hT],
                                          [t[:, c:c + 512] for t in w[j]], kk == 0, kk == KF - 1)
                    mm.then_inc(used[j], 1)

            def body(e, q, past, last=False):
                if not last:
                    turn_x(e + 2)
                pe.wait_ge(xt_lo, e + 1)
                pe.wait_ge(lo[0], e + 1)
                if past:
                    pe.wait_ge(sig_done, e)
                up(pg, q, 0, (0, 1))
                if past:
                    turn_h(e)
                up(pg, q, 0, (2, 3)).then_inc(used[0], 1)
                pe.wait_ge(lo[1], e + 1)
                up(pg, q, 1, range(4)).then_inc(used[1], 1)
                if past:
                    down(e, past)
                for j in (2, 3):
                    pe.wait_ge(lo[j], e + 1)
                    up(pu, q, j, range(4)).then_inc(used[j], 1)

            turn_x(1)
            body(0, 0, 0)
            body(1, 1, 1)
            with pe.Fori(1, PAIRS - 1) as i:
                body(2 * i, 0, 2)
                body(2 * i + 1, 1, 2)
            body(NE - 2, 0, 2)
            body(NE - 1, 1, 2, last=True)
            turn_h(NE)
            down(NE, 2)

        @block.scalar
        def _(act):
            def half(e, j, past):
                act.wait_ge(raw_in[j], 16 * e + 16)
                if past:
                    act.wait_ge(used[j], e)
                split_hi(act, w[j][0][:, :], raw[j][:, :]).then_inc(hi[j], 1)

            def take_x(n, q):
                act.wait_ge(xt_done, n)
                split_hi(act, xT[q][0][:, :], px[:, :]).then_inc(xt_hi, 1)

            def take_h(n):
                act.wait_ge(ht_done, n)
                split_hi(act, hT[0][:, :], ph[:, :]).then_inc(ht_hi, 1)

            def take_y(n, past):
                act.wait_ge(used[5], n)
                if past > 1:
                    act.wait_ge(y_out, 16 * n - 16)
                act.activation(y[:, 512:1024], py[:, 512:1024], ACT.Copy).then_inc(y_a, 1)

            def store(n):
                b = n - 1 if isinstance(n, int) else act.snap(n - 1)
                need = n if isinstance(n, int) else act.snap(n)
                act.wait_ge(y_a, need)
                act.wait_ge(y_v, need)
                dst = yb[b] if isinstance(n, int) else yb[bass.ds(b, 1), :, :].rearrange("b p d -> p (b d)")
                act.dma_start(dst, y[:, :]).then_inc(y_out, 16)

            def body(e, q, past, last=False):
                half(e, 0, past)
                if not last:
                    take_x(e + 2, 1 - q)
                half(e, 1, past)
                if past:
                    take_h(e)
                half(e, 2, past)
                act.wait_ge(used[1], e + 1)
                if past:
                    act.wait_ge(h_done, e)
                act.activation(sg[:, :], pg[:, :], ACT.Silu).then_inc(sig_done, 1)
                half(e, 3, past)
                half(e, 4, past)
                if past:
                    take_y(e, past)
                half(e, 5, past)
                if past:
                    store(e)

            take_x(1, 0)
            body(0, 0, 0)
            body(1, 1, 1)
            with act.Fori(1, PAIRS - 1) as i:
                body(2 * i, 0, 2)
                body(2 * i + 1, 1, 2)
            body(NE - 2, 0, 2)
            body(NE - 1, 1, 2, last=True)
            take_h(NE)
            take_y(NE, 2)
            store(NE)
            act.wait_ge(y_out, 16 * NE)

        @block.vector
        def _(v):
            def half(e, j):
                v.wait_ge(hi[j], e + 1)
                split_lo(v, w[j][1][:, :], raw[j][:, :], w[j][0][:, :]).then_inc(lo[j], 1)

            def take_x(n, q):
                v.wait_ge(xt_hi, n)
                split_lo(v, xT[q][1][:, :], px[:, :], xT[q][0][:, :]).then_inc(xt_lo, 1)

            def take_h(n):
                v.wait_ge(ht_hi, n)
                split_lo(v, hT[1][:, :], ph[:, :], hT[0][:, :]).then_inc(ht_lo, 1)

            def take_y(n, past):
                v.wait_ge(used[5], n)
                if past > 1:
                    v.wait_ge(y_out, 16 * n - 16)
                v.tensor_copy(y[:, 0:512], py[:, 0:512]).then_inc(y_v, 1)

            def body(e, q, past, last=False):
                half(e, 0)
                if not last:
                    take_x(e + 2, 1 - q)
                half(e, 1)
                if past:
                    take_h(e)
                half(e, 2)
                half(e, 3)
                half(e, 4)
                if past:
                    take_y(e, past)
                half(e, 5)
                v.wait_ge(sig_done, e + 1)
                v.wait_ge(used[3], e + 1)
                v.tensor_tensor(h[:, :], sg[:, :], pu[:, :], ALU.mult).then_inc(h_done, 1)

            take_x(1, 0)
            body(0, 0, 0)
            body(1, 1, 1)
            with v.Fori(1, PAIRS - 1) as i:
                body(2 * i, 0, 2)
                body(2 * i + 1, 1, 2)
            body(NE - 2, 0, 2)
            body(NE - 1, 1, 2, last=True)
            take_h(NE)
            take_y(NE, 2)

    with Scope(nc, name + "o") as s:
        W1, W3 = s.sb("w1", [P, KD, FF]), s.sb("w3", [P, KD, FF])
        W2 = s.sb("w2", [P, KF, D])
        xin, xT, y = (s.sb(k, [P, D]) for k in ("xin", "xT", "y"))
        sg, h, hT = (s.sb(k, [P, FF]) for k in ("sig", "h", "hT"))
        pg, pu, ph = s.ps("gate"), s.ps("up"), s.ps("hT")
        px, py = s.ps("xT", 2), s.ps("y", 2)
        w_in, xt, xta, gu, sig, hd, ht, hte, dn, ye, yo = (
            s.sem(k) for k in ("w", "xt", "xta", "gu", "sig", "hd", "ht", "hte", "dn", "ye", "yo"))
        block = s.block()

        @block.sync
        def _(sp):
            n = sp.value_load(nov[0:1, 0:1], min_val=0, max_val=MAXOV)
            with sp.If(n > 0):
                with sp.Fori(0, n) as j:
                    e = sp.value_load(ovid[0:1, bass.ds(j, 1)], min_val=0, max_val=NE - 1)
                    b = sp.snap(j + NE)
                    free = sp.snap(j + 1)
                    sp.wait_ge(dn, free)
                    sp.wait_ge(dn, 1)
                    sp.dma_start(xin[:, :], xb[bass.ds(b, 1), :, :].rearrange("b p d -> p (b d)")).then_inc(w_in, 16)
                    sp.dma_start(W1[:, :, :], R1[bass.ds(e, 1), :, :, :].rearrange("e p k n -> p (e k) n")).then_inc(w_in, 16)
                    sp.dma_start(W3[:, :, :], R3[bass.ds(e, 1), :, :, :].rearrange("e p k n -> p (e k) n")).then_inc(w_in, 16)
                    sp.dma_start(W2[:, :, :], R2[bass.ds(e, 1), :, :, :].rearrange("e p k n -> p (e k) n")).then_inc(w_in, 16)

        @block.tensor
        def _(pe):
            n = pe.value_load(nov[0:1, 0:1], min_val=0, max_val=MAXOV)
            with pe.If(n > 0):
                with pe.Fori(0, n) as j:
                    pe.wait_ge(w_in, 64 * j + 64)
                    for k in range(KD):
                        mm = pe.transpose(px[:, k * P:(k + 1) * P], xin[:, k * P:(k + 1) * P], ident)
                    mm.then_inc(xt, 1)
                    pe.wait_ge(xta, j + 1)
                    for ps, w in ((pg, W1), (pu, W3)):
                        for k in range(KD):
                            mm = pe.matmul(ps[:, :], xT[:, k * P:(k + 1) * P], w[:, k, :], start=(k == 0), stop=(k == KD - 1))
                    mm.then_inc(gu, 1)
                    pe.wait_ge(hd, j + 1)
                    for k in range(KF):
                        mm = pe.transpose(ph[:, k * P:(k + 1) * P], h[:, k * P:(k + 1) * P], ident)
                    mm.then_inc(ht, 1)
                    pe.wait_ge(hte, j + 1)
                    for half in range(2):
                        for k in range(KF):
                            mm = pe.matmul(py[:, half * 512:(half + 1) * 512], hT[:, k * P:(k + 1) * P],
                                           W2[:, k, half * 512:(half + 1) * 512], start=(k == 0), stop=(k == KF - 1))
                    mm.then_inc(dn, 1)

        @block.scalar
        def _(act):
            n = act.value_load(nov[0:1, 0:1], min_val=0, max_val=MAXOV)
            with act.If(n > 0):
                with act.Fori(0, n) as j:
                    b = act.snap(j + NE)
                    act.wait_ge(gu, j + 1)
                    act.activation(sg[:, :], pg[:, :], ACT.Silu).then_inc(sig, 1)
                    act.wait_ge(ye, j + 1)
                    act.dma_start(yb[bass.ds(b, 1), :, :].rearrange("b p d -> p (b d)"), y[:, :]).then_inc(yo, 16)

        @block.vector
        def _(v):
            v.memset(y[:, 0:1], 0.0).then_inc(dn, 1)
            n = v.value_load(nov[0:1, 0:1], min_val=0, max_val=MAXOV)
            with v.If(n > 0):
                with v.Fori(0, n) as j:
                    v.wait_ge(xt, j + 1)
                    v.tensor_copy(xT[:, :], px[:, :]).then_inc(xta, 1)
                    v.wait_ge(sig, j + 1)
                    v.tensor_tensor(h[:, :], sg[:, :], pu[:, :], ALU.mult).then_inc(hd, 1)
                    v.wait_ge(ht, j + 1)
                    v.tensor_copy(hT[:, :], ph[:, :]).then_inc(hte, 1)
                    v.wait_ge(dn, j + 2)
                    v.tensor_copy(y[:, :], py[:, :]).then_inc(ye, 1)
                    v.wait_ge(yo, 16 * j + 16)


def combine_phase(nc, name, xs, slots, wts, ybuf, gates=None):
    n = len(xs)
    with Scope(nc, name) as s:
        Y = [[s.sb(f"y{i}{k}", [P, D]) for k in range(2)] for i in range(2)]
        acc = s.sb("acc", [P, D])
        rows = []
        for g in gates or []:
            if not any(g is r for r in rows):
                rows.append(g)
        G = [s.sb(f"g{i}", [P, D]) for i in range(len(rows))]
        y_in = [[s.sem(f"y{i}{k}") for k in range(2)] for i in range(2)]
        g_in, used, own = s.sem("g"), s.sem("used"), s.sem("own")
        block = s.block()

        @block.sync
        def _(sp):
            for i, r in enumerate(rows):
                sp.dma_start(G[i][:, :], bc_row(r, D)).then_inc(g_in, 16)

        @block.gpsimd
        def _(pool):
            for t in range(n):
                if t >= 2:
                    pool.wait_ge(used, t - 1)
                for k in range(2):
                    pool.indirect_dma_start(out=Y[t % 2][k][:, :], out_offset=None, in_=ybuf,
                                            in_offset=bass.IndirectOffsetOnAxis(ap=slots[:, t, k:k + 1], axis=0)
                                            ).then_inc(y_in[t % 2][k], 16)

        @block.vector
        def _(v):
            link = Chain(v, own)
            if rows:
                v.wait_ge(g_in, 16 * len(rows))
            for t in range(n):
                for k in range(2):
                    v.wait_ge(y_in[t % 2][k], 16 * (t // 2 + 1))
                y0, y1 = Y[t % 2]
                if t:
                    v.wait_ge(used, t)
                link(v.tensor_scalar(acc[:, :], y0[:, :], wts[:, t, 0:1], None, ALU.mult))
                if rows:
                    link(v.scalar_tensor_tensor(out=acc[:, :], in0=y1[:, :], scalar=wts[:, t, 1:2], in1=acc[:, :],
                                                op0=ALU.mult, op1=ALU.add))
                    i = [k for k, r in enumerate(rows) if r is gates[t]][0]
                    link(v.tensor_tensor(acc[:, :], acc[:, :], G[i][:, :], ALU.mult))
                    v.tensor_tensor(xs[t], xs[t], acc[:, :], ALU.add).then_inc(used, 1)
                else:
                    link(v.scalar_tensor_tensor(out=acc[:, :], in0=y1[:, :], scalar=wts[:, t, 1:2], in1=acc[:, :],
                                                op0=ALU.mult, op1=ALU.add))
                    v.tensor_tensor(xs[t], xs[t], acc[:, :], ALU.add).then_inc(used, 1)


def moe(nc, name, tab, xs, gain, mods, gates, wg, bg, we, be, w1, w3, w2, xbuf, ybuf):
    n = len(xs)
    with Scope(nc, name) as o:
        wts, slots = o.sb("wts", [P, n, 2]), o.sb("slots", [P, n, 2], I32)
        ovid, nov = o.sb("ovid", [P, MAXOV], I32), o.sb("nov", [P, 1], I32)
        stream = Stream(o, w1, w3, w2)
        with Scope(nc, name + "h") as s:
            htok = s.sb("tok", [P, n, D])
            hT = s.sb("T", [P, KD, n * P])
            norm_phase(nc, name + "n", xs, tab, gain, hT=hT, htok=htok, mods=mods, ahead=stream.first)
            route_phase(nc, name + "r", tab, hT, n, wg, bg, we, be, wts, slots, ovid, nov)
            scatter_phase(nc, name + "s", htok, n, slots, xbuf)
        experts_phase(nc, name + "e", tab, stream, w1, w3, w2, xbuf, ybuf, ovid, nov)
        combine_phase(nc, name + "c", xs, slots, wts, ybuf, gates)


def modulation_phase(nc, tab, c, cc, w, b, modD):
    L, N = b.shape
    CHN = N // 512
    RING = 4
    with Scope(nc, "ada") as s:
        cT = s.sb("cT", [P, KD, 2])
        sT = s.sb("sT", [P, KD, 2])
        br = s.sb("b", [2, L, N])
        row = s.sb("row", [2, L, N])
        W = [s.sb(f"w{i}", [P, KD, 512]) for i in range(RING)]
        ps = [s.ps(f"acc{i}") for i in range(4)]
        c_in, b_in, sil, mm_done, ev, out = (s.sem(k) for k in ("c", "b", "sil", "mm", "ev", "out"))
        w_in = [s.sem(f"w{i}") for i in range(RING)]
        block = s.block()

        @block.sync
        def _(sp):
            with nc.allow_non_contiguous_dma("1024 numbers, once"):
                sp.dma_start(cT[:, :, 0], c.rearrange("(k p) -> p k", p=P)).then_inc(c_in, 16)
                sp.dma_start(cT[:, :, 1], cc.rearrange("(k p) -> p k", p=P)).then_inc(c_in, 16)
            for n in range(L * CHN):
                l, j = divmod(n, CHN)
                if n >= RING:
                    sp.wait_ge(mm_done, n - RING + 1)
                sp.dma_start(W[n % RING][:, :, :], w[l, :, j * 512:(j + 1) * 512].rearrange("(k p) n -> p k n", p=P)
                             ).then_inc(w_in[n % RING], 16)
                if n == 0:
                    for l2 in range(L):
                        sp.dma_start(br[:, l2, :], b[l2].rearrange("(a n) -> a n", a=1).to_broadcast([2, N])).then_inc(b_in, 16)
            for l in range(L):
                sp.wait_ge(ev, CHN * (l + 1))
                sp.dma_start(modD[l], row[:, l, :]).then_inc(out, 16)
            sp.wait_ge(out, 16 * L)

        @block.scalar
        def _(act):
            act.wait_ge(c_in, 32)
            act.activation(sT[:, :, :], cT[:, :, :], ACT.Silu).then_inc(sil, 1)

        @block.tensor
        def _(pe):
            pe.wait_ge(sil, 1)
            for n in range(L * CHN):
                pe.wait_ge(w_in[n % RING], 16 * (n // RING + 1))
                if n >= 4:
                    pe.wait_ge(ev, n - 3)
                for k in range(KD):
                    mm = pe.matmul(ps[n % 4][0:2, :], sT[:, k, :], W[n % RING][:, k, :], start=(k == 0), stop=(k == KD - 1))
                mm.then_inc(mm_done, 1)

        @block.vector
        def _(v):
            v.wait_ge(b_in, 16 * L)
            for n in range(L * CHN):
                l, j = divmod(n, CHN)
                v.wait_ge(mm_done, n + 1)
                v.tensor_tensor(row[:, l, j * 512:(j + 1) * 512], ps[n % 4][0:2, :], br[:, l, j * 512:(j + 1) * 512],
                                ALU.add).then_inc(ev, 1)


class Clear:

    def __init__(self, s, xbuf, ybuf, na, relpad):
        self.xbuf, self.ybuf, self.relpad = xbuf, ybuf, relpad
        self.rel = na.rearrange("h r c -> (h r) c")
        self.z = s.sb("zeros", [P, FF])
        self.rp = s.sb("relrows", [120, 2, P])
        self.zeroed, self.rel_in, self.out = s.sem("zeroed"), s.sem("relin"), s.sem("cleared")
        self.n = 0

    def zero(self, v):
        v.memset(self.rp[:, :, :], 0.0).then_inc(self.zeroed, 1)
        v.memset(self.z[:, :], 0.0).then_inc(self.zeroed, 1)

    def write(self, sp):
        sp.wait_ge(self.zeroed, 2)
        for i in range(2):
            sp.dma_start(self.rp[:, i, 48:79], self.rel[i * 120:(i + 1) * 120, :]).then_inc(self.rel_in, 16)
        for buf, r0, r1 in ((self.xbuf, 0, SLOTS), (self.ybuf, NE * P, SLOTS)):
            for r in range(r0, r1, 512):
                dst = buf[r:r + 512, :].rearrange("(p j) d -> p (j d)", j=4).rearrange("p (j d) -> p j d", d=FF)
                sp.dma_start(dst, self.z[:, :].unsqueeze(1).to_broadcast([P, 4 * D // FF, FF])).then_inc(self.out, 16)
                self.n += 1
        sp.wait_ge(self.rel_in, 32)
        for i in range(2):
            sp.dma_start(self.relpad[i * 120:(i + 1) * 120, :].rearrange("r (c n) -> r c n", n=P),
                         self.rp[:, i, :].unsqueeze(1).to_broadcast([120, HD, P])).then_inc(self.out, 16)
            self.n += 1

    def end(self, sp):
        sp.wait_ge(self.out, 16 * self.n)


def pool_phase(nc, name, band, pw, pscale, u, nt, dst):
    T = nt * P
    with Scope(nc, name) as s:
        bd = [s.sb(f"band{i}", [P, nt, T]) for i in range(2)]
        w = s.sb("w", [P, 4, P])
        sc = s.sb("sc", [P, 4])
        pl = [s.sb(f"pl{i}", [P, T]) for i in range(2)]
        ps1, ps2 = [s.ps(f"a{i}") for i in range(2)], [s.ps(f"b{i}") for i in range(2)]
        b_in, w_in = [s.sem(f"b{i}") for i in range(2)], s.sem("w")
        m1, ev1, m2, ev2, own = (s.sem(k) for k in ("m1", "e1", "m2", "e2", "own"))
        block = s.block()

        @block.sync
        def _(sp):
            sp.dma_start(w[:, :, :], pw.rearrange("g c d -> c g d")).then_inc(w_in, 16)
            with nc.allow_non_contiguous_dma("512 numbers, once"):
                sp.dma_start(sc[:, :], pscale.rearrange("(g p) -> p g", p=P)).then_inc(w_in, 16)
            for g in range(4):
                if g >= 2:
                    sp.wait_ge(m1, g - 1)
                sp.dma_start(bd[g % 2][:, :, :], band[g].rearrange("(t p) n -> p t n", p=P)).then_inc(b_in[g % 2], 16)

        @block.tensor
        def _(pe):
            def mix(g):
                pe.wait_ge(ev1, g + 1)
                if g >= 2:
                    pe.wait_ge(ev2, g - 1)
                pe.matmul(ps2[g % 2][:, 0:T], w[:, g, :], pl[g % 2][:, :], start=True, stop=True).then_inc(m2, 1)

            pe.wait_ge(w_in, 32)
            for g in range(4):
                pe.wait_ge(b_in[g % 2], 16 * (g // 2 + 1))
                if g >= 2:
                    pe.wait_ge(ev1, g - 1)
                for t in range(nt):
                    mm = pe.matmul(ps1[g % 2][:, 0:T], u(t)[:, g * P:(g + 1) * P], bd[g % 2][:, t, :], start=(t == 0), stop=(t == nt - 1))
                mm.then_inc(m1, 1)
                if g >= 1:
                    mix(g - 1)
            mix(3)

        @block.vector
        def _(v):
            link = Chain(v, own)

            def second(g):
                v.wait_ge(m2, g + 1)
                link(v.tensor_scalar(dst[0][:, g, :], ps2[g % 2][:, 0:T], sc[:, g:g + 1], None, ALU.mult))
                v.scalar_tensor_tensor(out=dst[1][:, g, :], in0=ps2[g % 2][:, 0:T], scalar=sc[:, g:g + 1],
                                       in1=dst[0][:, g, :].bitcast(F32), op0=ALU.mult, op1=ALU.subtract).then_inc(ev2, 1)

            v.wait_ge(w_in, 32)
            for g in range(4):
                v.wait_ge(m1, g + 1)
                if g >= 2:
                    v.wait_ge(m2, g - 1)
                v.tensor_copy(pl[g % 2][:, :], ps1[g % 2][:, 0:T]).then_inc(ev1, 1)
                if g >= 1:
                    second(g - 1)
            second(3)


def load_phase(nc, name, pairs):
    with Scope(nc, name) as s:
        done = s.sem("in")
        block = s.block()

        @block.sync
        def _(sp):
            with nc.allow_non_contiguous_dma("parameters"):
                for d, r in pairs:
                    sp.dma_start(d, r).then_inc(done, 16)
            sp.wait_ge(done, 16 * len(pairs))


def lambda_phase(nc, A, nlam, lam_init):
    with Scope(nc, "lam") as s:
        r = s.sb("r", [P, 4, HD])
        d = s.sb("d", [P, 2])
        pr = s.sb("p", [P, 2, HD])
        ld, dd, ee, own = (s.sem(k) for k in ("ld", "dd", "ee", "own"))
        block = s.block()

        @block.sync
        def _(sp):
            for i, n in enumerate(("lambda_q1", "lambda_k1", "lambda_q2", "lambda_k2")):
                sp.dma_start(r[:, i, :], bc_row(A[n], HD)).then_inc(ld, 16)

        @block.vector
        def _(v):
            link = Chain(v, own)
            v.wait_ge(ld, 64)
            link(v.tensor_tensor(pr[:, 0, :], r[:, 0, :], r[:, 1, :], ALU.mult))
            link(v.tensor_tensor(pr[:, 1, :], r[:, 2, :], r[:, 3, :], ALU.mult))
            v.tensor_reduce(d[:, :], pr[:, :, :], AX.X, ALU.add).then_inc(dd, 1)
            v.wait_ge(ee, 1)
            link(v.tensor_tensor(nlam[:, :], d[:, 1:2], d[:, 0:1], ALU.subtract))
            link(v.tensor_scalar(nlam[:, :], nlam[:, :], -lam_init, None, ALU.add))

        @block.scalar
        def _(act):
            act.wait_ge(dd, 1)
            act.activation(d[:, :], d[:, :], ACT.Exp).then_inc(ee, 1)


def subln_phase(nc, tab, o, w, factor):
    n = NT * 4
    with Scope(nc, "sub") as s:
        g = s.sb("g", [P, P])
        sq = s.sb("sq", [P, n, P])
        st = s.sb("st", [P, 2, n])
        ld, ms, rt, own = (s.sem(k) for k in ("ld", "ms", "rt", "own"))
        block = s.block()
        o3 = o[:, :, :].rearrange("p t (h d) -> p (t h) d", d=P)

        @block.sync
        def _(sp):
            sp.dma_start(g[:, :], bc_row(w, P)).then_inc(ld, 16)

        @block.scalar
        def _(act):
            act.wait_ge(ms, 1)
            act.activation(st[:, 1, :], st[:, 0, :], ACT.Sqrt).then_inc(rt, 1)

        @block.vector
        def _(v):
            link = Chain(v, own)
            link(v.tensor_tensor(sq[:, :, :], o3, o3, ALU.mult))
            link(v.tensor_reduce(st[:, 0, :], sq[:, :, :], AX.X, ALU.add))
            v.tensor_scalar(st[:, 0, :], st[:, 0, :], 1.0 / P, EPS, ALU.mult, ALU.add).then_inc(ms, 1)
            v.wait_ge(rt, 1)
            link(v.reciprocal(st[:, 0, :], st[:, 1, :]))
            link(v.tensor_tensor(o3, o3, st[:, 0, :].unsqueeze(2).to_broadcast([P, n, P]), ALU.mult))
            v.wait_ge(ld, 16)
            link(v.tensor_scalar(g[:, :], g[:, :], factor, None, ALU.mult))
            link(v.tensor_tensor(o3, o3, g[:, :].unsqueeze(1).to_broadcast([P, n, P]), ALU.mult))


def operand(pair):
    return lambda k, t: [h[:, k, t * P:(t + 1) * P] for h in pair]


def copy_evac(dst):
    def evac(eng, link, ps, t, c):
        return eng.tensor_copy(dst(t, c), ps)
    return evac


def add_evac(xs):
    def evac(v, link, ps, t, c):
        x = xs[t][:, c * 512:(c + 1) * 512]
        return v.tensor_tensor(x, x, ps, ALU.add)
    return evac


def first_mixer(nc, tab, A, xs, dram):
    with Scope(nc, "m1") as m:
        gate = m.sb("gate", [P, NT, RW])
        hT = m.pair("hT", [P, KD, SEQ])
        norm_phase(nc, "n1", xs, tab, A["norm_mix"], hT=hT)
        win = A["w_in"]
        with Scope(nc, "m2") as f:
            KR = f.sb("KR", [P, 4, 2, SEQ])
            BT, KDT = f.sb("BT", [P, 4, SEQ]), f.sb("KDT", [P, 4, SEQ])
            Vt, KDt, Bt = (f.sb(k, [P, NT, RW]) for k in ("Vt", "KDt", "Bt"))
            PC = f.sb("PC", [P, 4, NCH])
            rtab = f.sb("rtab", [P, R_END])
            clear = Clear(f, *dram)
            bonus = f.sb("bonus", [P, NT * 8])
            with Scope(nc, "m3") as q:
                pr = q.sb("pr", [P, 14, SEQ])
                feature_phase(nc, "rp", hT, win[:, 0:1792], [(m, 0, SEQ, pr[:, m, :], 1.0) for m in range(14)], RAW=1)
                rwkv_prepare(nc, tab, rtab, clear, pr, A, KR, BT, KDT, Vt, KDt, Bt, PC, bonus, gate)
            with Scope(nc, "m4") as q:
                U = q.sb("U", [P, 32, 512])
                rwkv_chunks(nc, tab, rtab, KR, BT, KDT, U)
                y = BT
                rwkv_scan(nc, tab, U, KR, Vt, KDt, Bt, PC, y)
                rwkv_finish(nc, tab, A, clear, y, Vt, bonus, gate)
        gates = m.sb("gates", [P, NT, 2 * D])
        o = m.sb("o", [P, NT, 512])
        with Scope(nc, "m5") as q:
            qkv = q.sb("qkv", [P, NT, 1536])
            nlam = q.sb("nlam", [P, 1])
            allt = lambda c: range(NT)
            lhs = operand(hT)
            linear_phase(nc, "l1", lhs, KD, allt, win[:, 1792:3328], 1536, copy_evac(lambda t, c: qkv[:, t, c * 512:(c + 1) * 512]))

            def gate_evac(act, link, ps, t, c):
                return act.activation(gates[:, t, c * 512:(c + 1) * 512], ps, ACT.Sigmoid)
            linear_phase(nc, "l2", lhs, KD, allt, win[:, 3328:5376], 2048, gate_evac, on="a")
            lam_init = 0.8 - 0.6 * math.exp(-0.3 * 0)
            lambda_phase(nc, A, nlam, lam_init)
            qT, kT = q.sb("qT", [P, 4, SEQ]), q.sb("kT", [P, 4, SEQ])
            part = lambda c0: (lambda t: qkv[:, t, c0:c0 + 512].rearrange("p (h d) -> p h d", d=64))
            turned = lambda d: (lambda t: d[:, :, t * P:(t + 1) * P])
            rope = A["rope"][0]
            heads_phase(nc, "h1", tab, [
                dict(src=part(0), heads=8, tiles=range(NT), gain=A["q_norm"], rope=lambda t: t, rope_src=rope, axes=1,
                     scale=0.125, dst=turned(qT)),
                dict(src=part(512), heads=8, tiles=range(NT), gain=A["k_norm"], rope=lambda t: t, rope_src=None, axes=1,
                     scale=1.0, dst=turned(kT))], SEQ)
            jobs = []
            for h in range(4):
                for t in range(NT):
                    for c in range(2):
                        def post(v, link, ps, r, h=h, t=t, c=c):
                            dst = o[:, t, h * P:(h + 1) * P]
                            if c == 0:
                                return v.tensor_scalar(dst, ps[:, 0:P], r, None, ALU.mult)
                            link(v.tensor_scalar(r, r, nlam[:, 0:1], None, ALU.mult))
                            return v.scalar_tensor_tensor(out=dst, in0=ps[:, 0:P], scalar=r, in1=dst, op0=ALU.mult, op1=ALU.add)
                        rows = slice(64 * c, 64 * c + 64)
                        jobs.append(dict(
                            q=qT[rows, h, t * P:(t + 1) * P], k=kT[rows, h, :], keys=(t + 1) * P, dv=P, post=post,
                            add=lambda b, t=t: [(t * P, P, tab[:, C_CAUS:C_CAUS + P])],
                            v=lambda k, h=h: qkv[:, k, 1024 + h * P:1024 + (h + 1) * P]))
            attention_phase(nc, "a1", tab, jobs)
            subln_phase(nc, tab, o, A["subln_w"], 1.0 - lam_init)
        with Scope(nc, "m6") as q:
            o1, o2 = q.pair("orT", [P, 4, SEQ]), q.pair("odT", [P, 4, SEQ])
            transpose_phase(nc, "ty", lambda t, k: gate[:, t, k * P:(k + 1) * P], NT, 4, o1, tab)
            transpose_phase(nc, "to", lambda t, k: o[:, t, k * P:(k + 1) * P], NT, 4, o2, tab)
            allt = lambda c: range(NT)

            def mix1(v, link, ps, t, c):
                g = gates[:, t, c * 512:(c + 1) * 512]
                return v.tensor_tensor(g, ps, g, ALU.mult)

            def mix2(v, link, ps, t, c):
                g = gates[:, t, D + c * 512:D + (c + 1) * 512]
                link(v.tensor_tensor(g, ps, g, ALU.mult))
                mx = gates[:, t, c * 512:(c + 1) * 512]
                return v.tensor_tensor(mx, mx, g, ALU.add)
            linear_phase(nc, "l3", operand(o1), 4, allt, A["w_branch_rwkv"], D, mix1)
            linear_phase(nc, "l4", operand(o2), 4, allt, A["w_branch_diff"], D, mix2)
            transpose_phase(nc, "tm", lambda t, k: gates[:, t, k * P:(k + 1) * P], NT, KD, hT, tab)
            linear_phase(nc, "l5", operand(hT), KD, allt, A["w_out"], D, add_evac(xs))


def ple(nc, tab, A, xs):
    allt = lambda c: range(NT)
    with Scope(nc, "pl") as m:
        hT = m.pair("hT", [P, KD, SEQ])
        g = m.sb("g", [P, NT, D])
        pt = m.sb("p", [P, NT, 256])
        pT = m.pair("pT", [P, 2, SEQ])
        norm_phase(nc, "np", xs, tab, A["norm_ple"], hT=hT)

        def gate_evac(act, link, ps, t, c):
            return act.activation(g[:, t, c * 512:(c + 1) * 512], ps, ACT.Sigmoid)
        linear_phase(nc, "lg", operand(hT), KD, allt, A["w_ple_gate"], D, gate_evac, on="a")
        load_phase(nc, "lp", [(pt[:, :, :], A["p"].rearrange("(t p) d -> p t d", p=P))])
        transpose_phase(nc, "pq", lambda t, k: pt[:, t, k * P:(k + 1) * P], NT, 2, pT, tab)

        def add(v, link, ps, t, c):
            gg = g[:, t, c * 512:(c + 1) * 512]
            link(v.tensor_tensor(gg, ps, gg, ALU.mult))
            x = xs[t][:, c * 512:(c + 1) * 512]
            return v.tensor_tensor(x, x, gg, ALU.add)
        linear_phase(nc, "lq", operand(pT), 2, allt, A["w_ple_proj"], D, add)


def gated_add(rows_of, xs, G):
    def evac(v, link, ps, t, c):
        cs = slice(c * 512, (c + 1) * 512)
        link(v.tensor_tensor(ps, ps, G[rows_of(t)][:, cs], ALU.mult))
        return v.tensor_tensor(xs[t][:, cs], xs[t][:, cs], ps, ALU.add)
    return evac


def even_mixer(nc, tab, A, xs, mod):
    is_x = lambda t: 0 if t >= XT0 else 1
    with Scope(nc, "e1") as m:
        pj = m.sb("pj", [P, NTA, 1280])
        with Scope(nc, "e3") as r:
            hT = r.pair("hT", [P, KD, NTA * P])
            mods = [(mod(j, 1), mod(j, 0)) for j in range(2)]
            norm_phase(nc, "ne", xs, tab, A["norm_mix_g_2"][0], hT=hT, mods=[mods[is_x(t)] for t in range(NTA)])

            def evac(v, link, ps, t, c):
                n = min(512, 1280 - 512 * c)
                return v.tensor_copy(pj[:, t, c * 512:c * 512 + n], ps)
            linear_phase(nc, "le", operand(hT), KD, lambda c: range(NTA),
                         A["even_w_in_2"], 1280, evac)
        oT = m.pair("oT", [P, 8, NTA * P])
        with Scope(nc, "e2") as q:
            dx, dc = [h[:, 4:8, XT0 * P:] for h in oT], [h[:, 4:8, 0:XT0 * P] for h in oT]
            pool_phase(nc, "px", A["band_x"], A["pool_w_2"], A["pool_scale_2"], lambda t: pj[:, XT0 + t, 768:1280], NT, dx)
            pool_phase(nc, "pc", A["band_c"], A["pool_w_2"], A["pool_scale_2"], lambda t: pj[:, t, 768:1280], XT0, dc)
            qT, kT = q.sb("qT", [P, 4, NTA * P]), q.sb("kT", [P, 2, NTA * P])
            kd = q.sb("kd", [P, NTA, 4, 64])
            o = q.sb("o", [P, NTA, 512])
            with Scope(nc, "e4") as s:
                dn = s.sem("dn")
                block = s.block()

                @block.vector
                def _(v):
                    for t in range(NTA):
                        src = pj[:, t, 512:640].rearrange("p (h d) -> p h d", d=64).unsqueeze(2).to_broadcast([P, 2, 2, 64])
                        v.tensor_copy(kd[:, t, :, :].rearrange("p (h e) d -> p h e d", e=2), src).then_inc(dn, 1)
            part = lambda t: pj[:, t, 0:512].rearrange("p (h d) -> p h d", d=64)
            turned = lambda d: (lambda t: d[:, :, t * P:(t + 1) * P])
            rope = A["rope"][1]
            rx, rc = range(XT0, NTA), range(XT0)
            common = dict(axes=2)
            heads_phase(nc, "he", tab, [
                dict(src=part, heads=8, tiles=rx, gain=A["a_q_gain_2"], rope=lambda t: t - XT0, rope_src=rope, scale=0.125,
                     dst=turned(qT), **common),
                dict(src=lambda t: kd[:, t, :, :], heads=4, tiles=rx, gain=A["a_k_gain_2"], rope=lambda t: t - XT0,
                     rope_src=None, scale=1.0, dst=turned(kT), **common),
                dict(src=part, heads=8, tiles=rc, gain=A["a_q_gain_2"], rope=None, rope_src=None, scale=0.125,
                     dst=turned(qT), **common),
                dict(src=lambda t: kd[:, t, :, :], heads=4, tiles=rc, gain=A["a_k_gain_2"], rope=None, rope_src=None,
                     scale=1.0, dst=turned(kT), **common)], NTA * P)
            jobs = []
            for h in range(8):
                rows = slice(64 * (h % 2), 64 * (h % 2) + 64)
                for t in range(NTA):
                    def post(v, link, ps, r, h=h, t=t):
                        return v.tensor_scalar(o[:, t, h * 64:(h + 1) * 64], ps[:, 0:64], r, None, ALU.mult)
                    jobs.append(dict(q=qT[rows, h // 2, t * P:(t + 1) * P], k=kT[rows, h // 4, :],
                                     keys=CTXL if t < XT0 else NTA * P, dv=64, post=post, add=lambda b: [],
                                     v=lambda k, h=h: pj[:, k, 640 + 64 * (h // 4):704 + 64 * (h // 4)]))
            attention_phase(nc, "ae", tab, jobs)
            transpose_phase(nc, "te", lambda t, k: o[:, t, k * P:(k + 1) * P], NTA, 4, oT, tab)
        G = [m.sb(f"G{j}", [P, D]) for j in range(2)]
        linear_phase(nc, "lf", operand(oT), 8, lambda c: range(NTA), A["even_w_out_2"], D,
                     gated_add(is_x, xs, G), loads=[(G[j][:, :], bc_row(mod(j, 2), D)) for j in range(2)])


def odd_mixer(nc, tab, A, xs, mod, relpad):
    is_x = lambda t: 0 if t >= XT0 else 1
    H = 16
    with Scope(nc, "o1") as m:
        with Scope(nc, "o2") as q:
            vv = q.sb("vv", [P, NTA, D])
            qT, kT = q.sb("qT", [P, 8, SEQ]), q.sb("kT", [P, 8, NTA * P])
            with Scope(nc, "o3") as r:
                hT = r.pair("hT", [P, KD, NTA * P])
                mods = [(mod(j, 1), mod(j, 0)) for j in range(2)]
                norm_phase(nc, "no", xs, tab, A["norm_mix_g_2"][1], hT=hT, mods=[mods[is_x(t)] for t in range(NTA)])
                C = XT0 * P
                feature_phase(nc, "lo", hT, A["odd_w_in_2"],
                              [(m, C, SEQ, qT[:, m, :], 0.125) for m in range(8)]
                              + [(8 + m, c0, n, kT[:, m, c0:c0 + n], 1.0) for m in range(8) for c0, n in ((0, C), (C, SEQ))])
                linear_phase(nc, "lv", operand(hT), KD, lambda c: range(NTA),
                             A["odd_w_in_2"][:, 2 * D:3 * D], D, copy_evac(lambda t, c: vv[:, t, c * 512:(c + 1) * 512]))
            o = q.sb("o", [P, NT, D])
            jobs = []
            for h in range(H):
                rows = slice(64 * (h % 2), 64 * (h % 2) + 64)
                for t in range(NT):
                    def post(v, link, ps, r, h=h, t=t):
                        return v.tensor_scalar(o[:, t, h * 64:(h + 1) * 64], ps[:, 0:64], r, None, ALU.mult)
                    jobs.append(dict(q=qT[rows, h // 2, t * P:(t + 1) * P], k=kT[rows, h // 2, :], keys=NTA * P, dv=64,
                                     post=post, v=lambda k, h=h: vv[:, k, 64 * h:64 * h + 64],
                                     add=lambda b, t=t: [(CTXL, SEQ, b[:, 7 - 2 * t:15 - 2 * t, :].rearrange("p r c -> p (r c)"))]))

            def load(h, bt):
                base = relpad[h * 15:(h + 1) * 15, :]

                def window(r):
                    return bass.AP(tensor=base.tensor, offset=base.offset + HD * P * r + HD - 1,
                                   ap=[[P - 1, HD], [HD * P, 14], [1, HD]])
                return [(bt[0:64, 1:15, :], window(1)), (bt[64:128, 1:15, :], window(0))]
            attention_phase(nc, "ao", tab, jobs, bias=dict(load=load, heads=H, per=NT))
            oT = q.pair("oT", [P, 8, SEQ])
            transpose_phase(nc, "tp", lambda t, k: o[:, t, k * P:(k + 1) * P], NT, 8, oT, tab)
            G = [q.sb("G0", [P, D])]
            xq = xs[XT0:]
            linear_phase(nc, "lr", operand(oT), 8, lambda c: range(NT), A["odd_w_out_2"], D,
                         gated_add(lambda t: 0, xq, G), loads=[(G[0][:, :], bc_row(mod(0, 2), D))])


def fused_blocks(nc, A, out, upto=None):
    Scope.used = []
    xbuf = nc.dram_tensor("xbuf", [SLOTS, D], F32, kind="Internal").ap()
    ybuf = nc.dram_tensor("ybuf", [SLOTS, D], F32, kind="Internal").ap()
    modD = nc.dram_tensor("modD", [2, 2, 6 * D], F32, kind="Internal").ap()
    relpad = nc.dram_tensor("relpad", [240, HD * P], F32, kind="Internal").ap()

    with nc.allow_non_contiguous_dma("parameter vectors, once"), Scope(nc, "g") as g:
        tab = g.sb("tab", [P, C_END])
        x = g.sb("x", [P, NT, D])
        xq = [x[:, t, :] for t in range(NT)]

        def stage(n):
            return upto is None or n in upto
        load_phase(nc, "ld", [(tab[:, :], A["table"]),
                              (x[:, :, :], A["x"].rearrange("(t p) d -> p t d", p=P))])
        if not stage("mix1"):
            with Scope(nc, "clr") as s:
                clear = Clear(s, xbuf, ybuf, A["na_rel_bias_2"], relpad)
                block = s.block()

                @block.vector
                def _(v):
                    clear.zero(v)

                @block.sync
                def _(sp):
                    clear.write(sp)
                    clear.end(sp)
        if stage("mix1"):
            first_mixer(nc, tab, A, xq, (xbuf, ybuf, A["na_rel_bias_2"], relpad))
        if stage("moe1"):
            moe(nc, "f1", tab, xq, A["norm_ffn"], None, None, A["w_group"], A["b_group"], A["w_expert_router"],
                A["b_expert_router"], A["w_gate"], A["w_up"], A["w_down"], xbuf, ybuf)
        if stage("ple"):
            ple(nc, tab, A, xq)
        if stage("ada"):
            modulation_phase(nc, tab, A["c_2"], A["c_ctx_2"], A["ada_w_2"], A["ada_b_2"], modD)
        ctx = g.sb("ctx", [P, XT0, D])
        xs = [ctx[:, t, :] for t in range(XT0)] + xq
        load_phase(nc, "lc", [(ctx[:, :, :], A["ctx_2"].rearrange("(t p) d -> p t d", p=P))])
        for l in range(2):
            rows = [[modD[l, j, i * D:(i + 1) * D] for i in range(6)] for j in range(2)]
            mod = lambda j, i, rows=rows: rows[j][i]
            moe_w = [A[k][l] for k in ("moe_w_group_2", "moe_b_group_2", "moe_w_expert_2", "moe_b_expert_2", "moe_w1_2",
                                       "moe_w3_2", "moe_w2_2")]
            pair = [(mod(j, 4), mod(j, 3)) for j in range(2)]
            if l == 0:
                if stage("mix2"):
                    even_mixer(nc, tab, A, xs, mod)
                if stage("moe2"):
                    moe(nc, "f2", tab, xs, A["norm_ffn_g_2"][0], [pair[1]] * XT0 + [pair[0]] * NT,
                        [mod(1, 5)] * XT0 + [mod(0, 5)] * NT, *moe_w, xbuf, ybuf)
            else:
                if stage("mix3"):
                    odd_mixer(nc, tab, A, xs, mod, relpad)
                if stage("moe3"):
                    moe(nc, "f3", tab, xq, A["norm_ffn_g_2"][1], [pair[0]] * NT, [mod(0, 5)] * NT, *moe_w, xbuf, ybuf)
        if stage("fin"):
            with Scope(nc, "fn") as s:
                h = s.sb("h", [P, NT, D])
                norm_phase(nc, "nf", xq, tab, A["final_g_2"], htok=h)
                store_phase(nc, h, out)
        else:
            store_phase(nc, x, out)


def store_phase(nc, h, out):
    with Scope(nc, "st") as s:
        done = s.sem("out")
        block = s.block()

        @block.sync
        def _(sp):
            sp.dma_start(out.rearrange("(t p) d -> p t d", p=P), h[:, :, :]).then_inc(done, 16)
            sp.wait_ge(done, 16)


_INS = """x p norm_mix w_in rwkv_mu rwkv_w0 rwkv_w2 rwkv_a0 rwkv_a2 rwkv_g2 rwkv_k_k rwkv_k_a rwkv_r_k rwkv_ln_w
rwkv_ln_b q_norm k_norm lambda_q1 lambda_k1 lambda_q2 lambda_k2 subln_w w_branch_rwkv w_branch_diff w_out norm_ffn
w_group b_group w_expert_router b_expert_router w_gate w_up w_down norm_ple w_ple_gate w_ple_proj c_2 ctx_2 c_ctx_2
ada_w_2 ada_b_2 norm_mix_g_2 norm_ffn_g_2 even_w_in_2 even_w_out_2 a_q_gain_2 a_k_gain_2 pool_w_2 pool_scale_2
odd_w_in_2 odd_w_out_2 na_rel_bias_2 moe_w_group_2 moe_b_group_2 moe_w_expert_2 moe_b_expert_2 moe_w1_2 moe_w3_2
moe_w2_2 final_g_2""".split()
_DROP = {"x": 1, "p": 2, "rwkv_r_k": 1, "c_2": 1, "ctx_2": 1}
_KEEP = {"c_ctx_2", "ada_w_2", "ada_b_2", "norm_mix_g_2", "norm_ffn_g_2", "final_g_2"}


def views(name, ap):
    if name in _KEEP or name.startswith("moe_"):
        return ap
    for _ in range(_DROP.get(name, 1)):
        ap = ap[0]
    if name == "rwkv_r_k":
        ap = ap.rearrange("h d -> (h d)")
    return ap


def kernel(**inputs):
    import numpy as _np
    import concourse.bacc as _bacc
    from concourse import mybir as _mybir
    from concourse.bass_utils import run_bass_kernel_spmd as _run

    nc = _bacc.Bacc("TRN2", target_bir_lowering=False, num_devices=1)
    arrays, aps = {}, {}
    for name in _INS:
        a = _np.ascontiguousarray(inputs[name])
        arrays[f"in_{name}_dram"] = a
        ap = nc.dram_tensor(f"in_{name}_dram", a.shape, _mybir.dt.from_np(a.dtype), kind="ExternalInput").ap()
        aps[name] = views(name, ap)
    for name, a in constants().items():
        arrays[f"const_{name}_dram"] = a
        aps[name] = nc.dram_tensor(f"const_{name}_dram", a.shape, _mybir.dt.float32, kind="ExternalInput").ap()
    out = nc.dram_tensor("out_0_dram", (1, SEQ, D), _mybir.dt.float32, kind="ExternalOutput").ap()
    fused_blocks(nc, aps, out[0])
    r = _run(nc, [arrays], core_ids=[0])
    return r.results[0]["out_0_dram"]
```
